# Optimizing a Trainium2 kernel written in Bass

```python
import jax, jax.numpy as jnp
from jax import lax
import numpy as np

D_MODEL = 1024
BATCH = 1
SEQ = 128
DEPTH = 1
DEC_BATCH = 1
DEC_SEQ = 128
PAST_LEN = 128

GRID_W = 64
N_HEADS_A = 8
HEAD_DIM_A = 64
D_A = N_HEADS_A * HEAD_DIM_A
WIN_ROWS = 8
WIN_COLS = 16
Q_COL_BLOCK = 16
K_COL_BLOCK = 2 * WIN_COLS
CTX_Q_BLOCK = 128
D_CONV = 512
CONV_WIDTH = 31
N_HEADS_M = 4
HEAD_DIM_M = 128
D_M = N_HEADS_M * HEAD_DIM_M
N_GATE_M = 4 * N_HEADS_M
CHUNK = 64
N_EXPERTS = 32
TOP_K = 4
D_EXPERT = 1024
SWIGLU_ALPHA = 1.702
SWIGLU_LIMIT = 7.0
MOE_BLOCK = 128
N_IN = 3 * D_A + 2 * D_CONV + 4 * D_M + N_GATE_M + 3 * D_MODEL
GATE_OFF = 3 * D_A + 2 * D_CONV + 4 * D_M
RMS_EPS = 1e-6
LN_EPS = 1e-5

kernel_name = 'hybrid_natten_conformer_mlstm_moe_step'

def _rmsnorm(x, g):
    xf = x.astype(jnp.float32)
    y = xf * lax.rsqrt(jnp.mean(xf * xf, axis=-1, keepdims=True) + RMS_EPS)
    return y.astype(x.dtype) * g

def _layernorm(x, g, b):
    xf = x.astype(jnp.float32)
    mu = jnp.mean(xf, axis=-1, keepdims=True)
    var = jnp.mean(jnp.square(xf - mu), axis=-1, keepdims=True)
    return ((xf - mu) * lax.rsqrt(var + LN_EPS)).astype(x.dtype) * g + b

def _split_in(z):
    sizes = [D_A, D_A, D_A, D_CONV, D_CONV, D_M, D_M, D_M, D_M, N_GATE_M, D_MODEL, D_MODEL, D_MODEL]
    return jnp.split(z, [int(s) for s in np.cumsum(sizes)[:-1]], axis=-1)

def _context_attention(q, k, v):
    B, L, H, Dh = q.shape
    nb = L // CTX_Q_BLOCK
    scale = Dh ** -0.5
    qb = q.reshape(B, nb, CTX_Q_BLOCK, H, Dh).transpose(1, 0, 2, 3, 4)

    def block(qi):
        s = jnp.einsum('bqhd,bkhd->bhqk', qi, k).astype(jnp.float32) * scale
        p = jax.nn.softmax(s, axis=-1).astype(q.dtype)
        return jnp.einsum('bhqk,bkhd->bqhd', p, v)

    o = lax.map(block, qb)
    return o.transpose(1, 0, 2, 3, 4).reshape(B, L, H * Dh)

def _neighbourhood_attention(q, k, v, k_ctx, v_ctx, rpb):
    B, L, H, Dh = q.shape
    rows = L // GRID_W
    kr = min(WIN_ROWS, rows)
    ncb = GRID_W // Q_COL_BLOCK
    scale = Dh ** -0.5
    qcol = np.arange(GRID_W).reshape(ncb, Q_COL_BLOCK)
    kcs = np.clip(np.arange(ncb) * Q_COL_BLOCK - WIN_COLS // 2, 0, GRID_W - K_COL_BLOCK)
    kcol = (kcs[:, None] + np.arange(K_COL_BLOCK)[None, :]).astype(np.int32)
    cs = np.clip(qcol - WIN_COLS // 2, 0, GRID_W - WIN_COLS)
    col_ok = (kcol[:, None, :] >= cs[:, :, None]) & (kcol[:, None, :] < cs[:, :, None] + WIN_COLS)
    dc_idx = np.clip(kcol[:, None, :] - qcol[:, :, None] + WIN_COLS - 1, 0, 2 * WIN_COLS - 2).astype(np.int32)
    mask = np.broadcast_to(col_ok[:, :, None, :], (ncb, Q_COL_BLOCK, kr, K_COL_BLOCK)).reshape(ncb, Q_COL_BLOCK, kr * K_COL_BLOCK)
    n_loc = kr * K_COL_BLOCK
    k_grid = k.reshape(B, rows, GRID_W, H, Dh)
    v_grid = v.reshape(B, rows, GRID_W, H, Dh)
    q_rows = q.reshape(B, rows, ncb, Q_COL_BLOCK, H, Dh).transpose(1, 0, 2, 3, 4, 5)

    def one_row(args):
        r, q_r = args
        rs = jnp.clip(r - kr // 2, 0, rows - kr)

        def band(t):
            t_r = lax.dynamic_slice_in_dim(t, rs, kr, axis=1)
            t_b = t_r[:, :, kcol]
            return t_b.transpose(0, 2, 1, 3, 4, 5).reshape(B, ncb, n_loc, H, Dh)

        k_b, v_b = band(k_grid), band(v_grid)
        dr_idx = rs + jnp.arange(kr) - r + WIN_ROWS - 1
        bias = rpb[:, dr_idx[:, None, None, None], dc_idx[None]]
        bias = bias.transpose(0, 2, 3, 1, 4).reshape(H, ncb, Q_COL_BLOCK, n_loc).astype(jnp.float32)
        s_loc = jnp.einsum('bnqhd,bnkhd->bhnqk', q_r, k_b).astype(jnp.float32) * scale + bias[None]
        s_loc = jnp.where(mask, s_loc, -jnp.inf)
        s_ctx = jnp.einsum('bnqhd,bchd->bhnqc', q_r, k_ctx).astype(jnp.float32) * scale
        p = jax.nn.softmax(jnp.concatenate([s_loc, s_ctx], axis=-1), axis=-1).astype(q.dtype)
        o = (jnp.einsum('bhnqk,bnkhd->bnqhd', p[..., :n_loc], v_b)
             + jnp.einsum('bhnqc,bchd->bnqhd', p[..., n_loc:], v_ctx))
        return o

    o = lax.map(one_row, (jnp.arange(rows), q_rows))
    return o.transpose(1, 0, 2, 3, 4, 5).reshape(B, L, H * Dh)

def _conformer_conv(u, g, w_dw, b_dw, ln_g, ln_b):
    a = u * jax.nn.sigmoid(g)
    a = lax.conv_general_dilated(a, w_dw[:, None, :], window_strides=(1,),
                                 padding=[(CONV_WIDTH // 2, CONV_WIDTH // 2)],
                                 dimension_numbers=('NWC', 'WIO', 'NWC'),
                                 feature_group_count=D_CONV) + b_dw
    return jax.nn.silu(_layernorm(a, ln_g, ln_b))

def _mlstm_scan(q, k, v, ig, lf, C0, n0, m0):
    B, L, H, _ = q.shape
    nc = L // CHUNK

    def seq_chunks(t):
        return t.reshape(B, nc, CHUNK, H, t.shape[-1]).transpose(1, 0, 3, 2, 4)

    def gate_chunks(t):
        return t.reshape(B, nc, CHUNK, H).transpose(1, 0, 3, 2)

    causal = jnp.tril(jnp.ones((CHUNK, CHUNK), dtype=bool))

    def step(carry, xs):
        C, n, m = carry
        qc, kc, vc, ic, fc = xs
        b = jnp.cumsum(fc, axis=-1)
        log_d = jnp.where(causal, b[..., :, None] - b[..., None, :] + ic[..., None, :], -jnp.inf)
        inter = b + m[..., None]
        m_t = jnp.maximum(inter, jnp.max(log_d, axis=-1))
        w_inter = jnp.exp(inter - m_t)
        s = jnp.einsum('bhtd,bhsd->bhts', qc, kc) * jnp.exp(log_d - m_t[..., None])
        num = w_inter[..., None] * jnp.einsum('bhvk,bhtk->bhtv', C, qc) + jnp.einsum('bhts,bhsv->bhtv', s, vc)
        den = w_inter * jnp.einsum('bhk,bhtk->bht', n, qc) + jnp.sum(s, axis=-1)
        h = num / jnp.maximum(jnp.abs(den), jnp.exp(-m_t))[..., None]
        m_new = m_t[..., -1]
        w_prev = jnp.exp(b[..., -1] + m - m_new)
        w_src = jnp.exp(b[..., -1:] - b + ic - m_new[..., None])
        C_new = w_prev[..., None, None] * C + jnp.einsum('bhs,bhsv,bhsk->bhvk', w_src, vc, kc)
        n_new = w_prev[..., None] * n + jnp.einsum('bhs,bhsk->bhk', w_src, kc)
        return (C_new, n_new, m_new), h

    (C, n, m), h = lax.scan(step, (C0, n0, m0),
                            (seq_chunks(q), seq_chunks(k), seq_chunks(v), gate_chunks(ig), gate_chunks(lf)))
    h = h.transpose(1, 0, 3, 2, 4).reshape(B, L, H, v.shape[-1])
    return h, (C, n, m)

def _mlstm_branch(qm, km, vm, om, gm, norm_g, C0, n0, m0):
    B, L, _ = qm.shape
    f32 = jnp.float32

    def heads(t):
        return t.reshape(B, L, N_HEADS_M, HEAD_DIM_M).astype(f32)

    q, k, v = heads(qm), heads(km) * HEAD_DIM_M ** -0.5, heads(vm)
    g = gm.reshape(B, L, 4, N_HEADS_M).astype(f32)
    C0, n0, m0 = C0.astype(f32), n0.astype(f32), m0.astype(f32)
    h_f, (C_f, n_f, m_f) = _mlstm_scan(q, k, v, g[:, :, 0], jax.nn.log_sigmoid(g[:, :, 1]),
                                       C0[:, 0], n0[:, 0], m0[:, 0])

    def rev(t):
        return jnp.flip(t, axis=1)

    h_b, (C_b, n_b, m_b) = _mlstm_scan(rev(q), rev(k), rev(v), rev(g[:, :, 2]),
                                       rev(jax.nn.log_sigmoid(g[:, :, 3])),
                                       C0[:, 1], n0[:, 1], m0[:, 1])
    h = h_f + rev(h_b)
    mu = jnp.mean(h, axis=-1, keepdims=True)
    var = jnp.mean(jnp.square(h - mu), axis=-1, keepdims=True)
    hn = ((h - mu) * lax.rsqrt(var + LN_EPS)).reshape(B, L, D_M) * norm_g.astype(f32)
    y = (jax.nn.sigmoid(om.astype(f32)) * hn).astype(qm.dtype)
    return y, (jnp.stack([C_f, C_b], axis=1), jnp.stack([n_f, n_b], axis=1), jnp.stack([m_f, m_b], axis=1))

def _merge(y_a, y_c, y_m, ga, gc, gm, lp):
    merged = (jax.nn.sigmoid(ga) * (y_a @ lp['w_pa'])
              + jax.nn.sigmoid(gc) * (y_c @ lp['w_pc'])
              + jax.nn.sigmoid(gm) * (y_m @ lp['w_pm']))
    return merged @ lp['w_out']

def _mixer_context(h, lp):
    B, L, _ = h.shape
    qa, ka, va, cu, cg, qm, km, vm, om, gm, ga, gc, gmx = _split_in(h @ lp['w_in'] + lp['b_in'])
    qa = qa.reshape(B, L, N_HEADS_A, HEAD_DIM_A)
    ka = ka.reshape(B, L, N_HEADS_A, HEAD_DIM_A)
    va = va.reshape(B, L, N_HEADS_A, HEAD_DIM_A)
    y_a = _context_attention(qa, ka, va)
    y_c = _conformer_conv(cu, cg, lp['w_dw'], lp['b_dw'], lp['cln_g'], lp['cln_b'])
    C0 = jnp.zeros((B, 2, N_HEADS_M, HEAD_DIM_M, HEAD_DIM_M), jnp.float32)
    n0 = jnp.zeros((B, 2, N_HEADS_M, HEAD_DIM_M), jnp.float32)
    m0 = jnp.full((B, 2, N_HEADS_M), -jnp.inf, jnp.float32)
    y_m, state = _mlstm_branch(qm, km, vm, om, gm, lp['mnorm_g'], C0, n0, m0)
    return _merge(y_a, y_c, y_m, ga, gc, gmx, lp), ka, va, state

def _mixer_latent(h, lp, k_ctx, v_ctx, C0, n0, m0):
    B, L, _ = h.shape
    qa, ka, va, cu, cg, qm, km, vm, om, gm, ga, gc, gmx = _split_in(h @ lp['w_in'] + lp['b_in'])
    qa = qa.reshape(B, L, N_HEADS_A, HEAD_DIM_A)
    ka = ka.reshape(B, L, N_HEADS_A, HEAD_DIM_A)
    va = va.reshape(B, L, N_HEADS_A, HEAD_DIM_A)
    y_a = _neighbourhood_attention(qa, ka, va, k_ctx.astype(qa.dtype), v_ctx.astype(qa.dtype), lp['rpb'])
    y_c = _conformer_conv(cu, cg, lp['w_dw'], lp['b_dw'], lp['cln_g'], lp['cln_b'])
    y_m, _ = _mlstm_branch(qm, km, vm, om, gm, lp['mnorm_g'], C0, n0, m0)
    return _merge(y_a, y_c, y_m, ga, gc, gmx, lp)

def _moe(x, lp):
    B, L, D = x.shape
    t = x.reshape(B * L, D)
    T = B * L
    logits = (t @ lp['w_router'] + lp['b_router']).astype(jnp.float32)
    top_val, top_idx = lax.top_k(logits, TOP_K)
    gate = jax.nn.softmax(top_val, axis=-1).astype(x.dtype)
    M = T * TOP_K
    flat_e = top_idx.reshape(M)
    flat_tok = jnp.repeat(jnp.arange(T, dtype=jnp.int32), TOP_K)
    flat_g = gate.reshape(M)
    order = jnp.argsort(flat_e)
    se = flat_e[order]
    counts = jnp.bincount(flat_e, length=N_EXPERTS)
    padded = (counts + MOE_BLOCK - 1) // MOE_BLOCK * MOE_BLOCK
    starts = jnp.cumsum(counts) - counts
    pend = jnp.cumsum(padded)
    pstarts = pend - padded
    pos = jnp.arange(M, dtype=jnp.int32) - starts[se] + pstarts[se]
    n_blocks = -(-M // MOE_BLOCK) + N_EXPERTS
    P = n_blocks * MOE_BLOCK
    slot_tok = jnp.full((P,), T, jnp.int32).at[pos].set(flat_tok[order])
    slot_g = jnp.zeros((P,), x.dtype).at[pos].set(flat_g[order])
    block_e = jnp.minimum(jnp.searchsorted(pend, jnp.arange(n_blocks, dtype=jnp.int32) * MOE_BLOCK, side='right'),
                          N_EXPERTS - 1)
    xs = jnp.concatenate([t, jnp.zeros((1, D), t.dtype)], axis=0)[slot_tok].reshape(n_blocks, MOE_BLOCK, D)
    w_gu, b_gu, w_down, b_down = lp['w_gu'], lp['b_gu'], lp['w_down'], lp['b_down']

    def expert_block(args):
        xb, e = args
        hgu = xb @ w_gu[e] + b_gu[e]
        h_glu, h_lin = jnp.split(hgu, 2, axis=-1)
        h_glu = jnp.minimum(h_glu, SWIGLU_LIMIT)
        h_lin = jnp.clip(h_lin, -SWIGLU_LIMIT, SWIGLU_LIMIT)
        act = (h_lin + 1) * (h_glu * jax.nn.sigmoid(SWIGLU_ALPHA * h_glu))
        return act @ w_down[e] + b_down[e]

    ys = lax.map(expert_block, (xs, block_e)).reshape(P, D) * slot_g[:, None]
    out = jnp.zeros((T + 1, D), x.dtype).at[slot_tok].add(ys)[:T]
    return out.reshape(B, L, D)

def setup_inputs(seed: int = 0) -> dict:
    key = jax.random.key(seed)
    ks = iter(jax.random.split(key, 40))

    def nrm(shape, scale):
        return jax.random.normal(next(ks), shape, jnp.float32) * scale

    D = D_MODEL
    x_prompt = nrm((BATCH, SEQ, D), 1.0)
    x_sample = nrm((DEC_BATCH, DEC_SEQ, D), 1.0)
    cache_k = nrm((DEC_BATCH, DEPTH, PAST_LEN, N_HEADS_A, HEAD_DIM_A), 1.0)
    cache_v = nrm((DEC_BATCH, DEPTH, PAST_LEN, N_HEADS_A, HEAD_DIM_A), 1.0)
    state_C = nrm((DEC_BATCH, DEPTH, 2, N_HEADS_M, HEAD_DIM_M, HEAD_DIM_M), 0.3)
    state_n = nrm((DEC_BATCH, DEPTH, 2, N_HEADS_M, HEAD_DIM_M), 0.3)
    state_m = nrm((DEC_BATCH, DEPTH, 2, N_HEADS_M), 0.5) + 1.0
    c = nrm((DEC_BATCH, D), 1.0)
    c_ctx = nrm((D,), 1.0)
    norm1_g = 1.0 + nrm((DEPTH, D), 0.02)
    w_mod = nrm((DEPTH, D, 6 * D), 0.5 * D ** -0.5)
    b_mod = nrm((DEPTH, 6 * D), 0.02)
    w_in = nrm((DEPTH, D, N_IN), D ** -0.5)
    forget_cols = np.concatenate([np.arange(GATE_OFF + N_HEADS_M, GATE_OFF + 2 * N_HEADS_M),
                                  np.arange(GATE_OFF + 3 * N_HEADS_M, GATE_OFF + 4 * N_HEADS_M)])
    forget_bias = jnp.tile(jnp.linspace(3.0, 6.0, N_HEADS_M), 2)
    b_in = nrm((DEPTH, N_IN), 0.02).at[:, forget_cols].add(forget_bias)
    rpb = nrm((DEPTH, N_HEADS_A, 2 * WIN_ROWS - 1, 2 * WIN_COLS - 1), 0.05)
    w_dw = nrm((DEPTH, CONV_WIDTH, D_CONV), CONV_WIDTH ** -0.5)
    b_dw = nrm((DEPTH, D_CONV), 0.02)
    cln_g = 1.0 + nrm((DEPTH, D_CONV), 0.02)
    cln_b = nrm((DEPTH, D_CONV), 0.02)
    mnorm_g = 1.0 + nrm((DEPTH, D_M), 0.02)
    w_pa = nrm((DEPTH, D_A, D), D_A ** -0.5)
    w_pc = nrm((DEPTH, D_CONV, D), D_CONV ** -0.5)
    w_pm = nrm((DEPTH, D_M, D), D_M ** -0.5)
    w_out = nrm((DEPTH, D, D), D ** -0.5)
    norm2_g = 1.0 + nrm((DEPTH, D), 0.02)
    w_router = nrm((DEPTH, D, N_EXPERTS), D ** -0.5)
    b_router = nrm((DEPTH, N_EXPERTS), 0.01)
    w_gu = nrm((DEPTH, N_EXPERTS, D, 2 * D_EXPERT), D ** -0.5)
    b_gu = nrm((DEPTH, N_EXPERTS, 2 * D_EXPERT), 0.02)
    w_down = nrm((DEPTH, N_EXPERTS, D_EXPERT, D), D_EXPERT ** -0.5)
    b_down = nrm((DEPTH, N_EXPERTS, D), 0.02)
    final_g = 1.0 + nrm((D,), 0.02)
    return {'x_prompt': x_prompt, 'x_sample': x_sample, 'cache_k': cache_k, 'cache_v': cache_v,
            'state_C': state_C, 'state_n': state_n, 'state_m': state_m, 'c': c, 'c_ctx': c_ctx,
            'norm1_g': norm1_g, 'w_mod': w_mod, 'b_mod': b_mod, 'w_in': w_in, 'b_in': b_in,
            'rpb': rpb, 'w_dw': w_dw, 'b_dw': b_dw, 'cln_g': cln_g, 'cln_b': cln_b,
            'mnorm_g': mnorm_g, 'w_pa': w_pa, 'w_pc': w_pc, 'w_pm': w_pm, 'w_out': w_out,
            'norm2_g': norm2_g, 'w_router': w_router, 'b_router': b_router, 'w_gu': w_gu,
            'b_gu': b_gu, 'w_down': w_down, 'b_down': b_down, 'final_g': final_g}

def reference(x_prompt, x_sample, cache_k, cache_v, state_C, state_n, state_m, c, c_ctx,
              norm1_g, w_mod, b_mod, w_in, b_in, rpb, w_dw, b_dw, cln_g, cln_b, mnorm_g,
              w_pa, w_pc, w_pm, w_out, norm2_g, w_router, b_router, w_gu, b_gu, w_down, b_down,
              final_g):
    ctx_cond = jax.nn.silu(c_ctx)
    lat_cond = jax.nn.silu(c)
    xp, xs = x_prompt, x_sample
    ks, vs, Cs, ns, ms = [], [], [], [], []
    for l in range(DEPTH):
        lp = {'w_in': w_in[l], 'b_in': b_in[l], 'rpb': rpb[l], 'w_dw': w_dw[l], 'b_dw': b_dw[l],
              'cln_g': cln_g[l], 'cln_b': cln_b[l], 'mnorm_g': mnorm_g[l], 'w_pa': w_pa[l],
              'w_pc': w_pc[l], 'w_pm': w_pm[l], 'w_out': w_out[l], 'w_router': w_router[l],
              'b_router': b_router[l], 'w_gu': w_gu[l], 'b_gu': b_gu[l], 'w_down': w_down[l],
              'b_down': b_down[l]}
        sh1, sc1, g1, sh2, sc2, g2 = jnp.split(ctx_cond @ w_mod[l] + b_mod[l], 6, axis=-1)
        h = _rmsnorm(xp, norm1_g[l]) * (1 + sc1) + sh1
        mix, k_l, v_l, (C_l, n_l, m_l) = _mixer_context(h, lp)
        xp = xp + g1 * mix
        h = _rmsnorm(xp, norm2_g[l]) * (1 + sc2) + sh2
        xp = xp + g2 * _moe(h, lp)
        ks.append(k_l)
        vs.append(v_l)
        Cs.append(C_l)
        ns.append(n_l)
        ms.append(m_l)
        sh1, sc1, g1, sh2, sc2, g2 = jnp.split((lat_cond @ w_mod[l] + b_mod[l])[:, None, :], 6, axis=-1)
        h = _rmsnorm(xs, norm1_g[l]) * (1 + sc1) + sh1
        mix = _mixer_latent(h, lp, cache_k[:, l], cache_v[:, l], state_C[:, l], state_n[:, l], state_m[:, l])
        xs = xs + g1 * mix
        h = _rmsnorm(xs, norm2_g[l]) * (1 + sc2) + sh2
        xs = xs + g2 * _moe(h, lp)
    y_prompt = _rmsnorm(xp, final_g)
    y_sample = _rmsnorm(xs, final_g)
    new_cache_k = jnp.stack(ks, axis=1)
    new_cache_v = jnp.stack(vs, axis=1)
    new_state_C = jnp.stack(Cs, axis=1)
    new_state_n = jnp.stack(ns, axis=1)
    new_state_m = jnp.stack(ms, axis=1)
    return (y_prompt, y_sample, new_cache_k, new_cache_v, new_state_C, new_state_n, new_state_m)


_drawn_inputs = setup_inputs


def setup_inputs(seed=0):
    import zlib

    import numpy as np

    out = dict(_drawn_inputs(seed))
    spreads = {}
    factors = {'cache_k': 2.817,
     'state_n': 2.667,
     'state_m': 3.058,
     'rpb': 64.0,
     'b_dw': 6.141,
     'cln_g': 7.612,
     'cln_b': 7.306,
     'mnorm_g': 8.0,
     'norm2_g': 3.517,
     'b_router': 4.631,
     'b_gu': 8.0,
     'b_down': 32.609,
     'final_g': 8.445}
    for name, (base, spread) in spreads.items():
        noise = np.random.default_rng([zlib.crc32(name.encode()), seed]).standard_normal(out[name].shape)
        drawn = base * np.exp(spread * noise) if base else spread * noise
        out[name] = __import__('jax').numpy.asarray(drawn.astype(out[name].dtype))
    for name, factor in factors.items():
        out[name] = (out[name] * factor).astype(out[name].dtype)
    return out
```

```python
from contextlib import ExitStack

import numpy as np

import concourse.bass as bass
from concourse import mybir

F32 = mybir.dt.float32
I32 = mybir.dt.int32
U32 = mybir.dt.uint32
ALU = mybir.AluOpType
ACT = mybir.ActivationFunctionType
AX = mybir.AxisListType.X

P = 128
D = 1024
KD = D // P
L = 128
TOK = 2 * L
GRID_W = 64
NH, HD = 8, 64
MH = 4
WIN_ROWS, WIN_COLS = 8, 16
RPB_ROWS, RPB_COLS = 2 * WIN_ROWS - 1, 2 * WIN_COLS - 1
CONV_W = 31
PAD = CONV_W // 2
NE, TOPK = 32, 4
SLOTS = 64
MAX_PASS = NE + TOK * TOPK // SLOTS
ALPHA, LIMIT = 1.702, 7.0
RMS_EPS, LN_EPS = 1e-6, 1e-5
ATT_SCALE = HD ** -0.5
M_SCALE = P ** -0.5
FAR = -1.0e30
LOWEST = -3.0e38

CHUNK = 4096
RING = 6
GU_CHUNKS, DN_CHUNKS = 4, 2
N_MOD = 12
PROJ = ["cu", "cg", "qa", "ka", "va", "qm", "km", "vm", "om"]
BRANCHES = ["c", "a", "m"]
C_MERGE = N_MOD + len(PROJ)
C_OUT = C_MERGE + 3 * len(BRANCHES)
N_TRUNK = C_OUT + 2
Z = {name: 4 * i for i, name in enumerate(PROJ)}
PAR_WIDTHS = [("norm1", KD), ("norm2", KD), ("final", KD), ("b_mod", 48), ("b_in", 60),
              ("w_dw", 4 * CONV_W), ("b_dw", 4), ("cln_g", 4), ("cln_b", 4), ("mnorm", MH), ("cond", 2 * KD)]
PC = {}
N_PAR = 0
for _name, _w in PAR_WIDTHS:
    PC[_name] = N_PAR
    N_PAR += _w
T_EXP, T_BASE = 0, MAX_PASS + 1
T_BEFORE = 2 * (MAX_PASS + 1)
T_ALL = T_BEFORE + NE
N_TAB = T_ALL + 1


def hybrid_layer(nc, trunk_w, expert_w, x_t, params, w_gate, b_gate, m_init, k_ctx_t, v_ctx,
                 c_init_t, rpb, w_router, b_router, b_gu, b_down,
                 y_t, k_new_t, v_new_t, c_new, n_new, m_new):
    with ExitStack() as ctx:
        def sb(name, shape, dt=F32):
            return ctx.enter_context(nc.sbuf_tensor(name, shape, dt))

        def sem(name):
            return ctx.enter_context(nc.semaphore(name))

        ring = sb("ring", [P, RING, CHUNK])
        x = sb("x", [P, KD, TOK])
        h = sb("h", [P, KD, TOK])
        par = sb("par", [P, N_PAR])
        bgu = sb("bgu", [P, NE, 16])
        mod = sb("mod", [P, 48, 2])
        cond = sb("cond", [P, 2 * KD])
        gain = sb("gain", [P, 2, KD, 2])
        rstd = sb("rstd", [P, TOK])
        ident = sb("ident", [P, P])
        ones = sb("ones", [P, P])
        strict = sb("strict", [P, P])
        iota = sb("iota", [P, TOK])
        tab = sb("tab", [1, N_TAB], I32)
        z = sb("z", [P, 36, TOK])
        merged = sb("merged", [P, KD, TOK])
        wgate = sb("wgate", [P, KD, 16])
        bgate = sb("bgate", [MH, 4])
        minit = sb("minit", [MH, 2])
        kctx = sb("kctx", [P, 4, L])
        vctx = sb("vctx", [P, NH * HD])
        cinit = sb("cinit", [P, 2, MH, P + 1])
        abias = sb("abias", [P, NH, L])
        amask = sb("amask", [P, L])
        dmask = sb("dmask", [P, 2, 2, L])
        apad = sb("apad", [P, 4, 2, L + 2 * PAD])
        vmt = sb("vmt", [P, 2, MH, P + 1])
        kmt = sb("kmt", [P, MH, P])
        gates = sb("gates", [MH, 4, TOK])
        selrow = sb("selrow", [MH, MH, P])
        work = sb("work", [P, 2840])
        small = sb("small", [P, 192])

        bank = [ctx.enter_context(nc.psum_tensor(f"bank{i}", [P, 512], F32)) for i in range(8)]

        def carve(base, at, shape, parts=P):
            n = int(np.prod(shape))
            v = base[0:parts, at:at + n]
            if len(shape) == 2:
                v = v.rearrange("p (a b) -> p a b", a=shape[0])
            if len(shape) == 3:
                v = v.rearrange("p (a b c) -> p a b c", a=shape[0], b=shape[1])
            return v, at + n

        def carve_all(base, what):
            out, at = {}, 0
            for name, shape, *parts in what:
                out[name], at = carve(base, at, shape, *parts)
            return out

        zf = z[:, :, :].rearrange("p a b -> p (a b)")
        mf = merged[:, :, :].rearrange("p a b -> p (a b)")
        af = apad[:, :, :, :].rearrange("p a b c -> p (a b c)")

        def zblocks(name, n=4):
            return z[:, Z[name]:Z[name] + n, :]

        va_tok = zf[:, Z["cg"] * TOK:(Z["cg"] + 4) * TOK].rearrange("p (s c) -> p s c", s=2)
        acc = zblocks("cu")
        branch_out = {"c": zblocks("cu"), "a": zblocks("qa"), "m": zblocks("om")}
        rows = carve_all(mf, [("b", [2, TOK], MH), ("g", [2, TOK], MH), ("negm", [2, TOK], MH),
                              ("w", [2, L], MH)])
        mirror = mf[:, 7 * TOK:7 * TOK + P]
        conv_sq = af[:, 0:4 * TOK].rearrange("p (a b) -> p a b", a=4)
        hm = af[:, 0:2 * MH * P].rearrange("p (s h d) -> p s h d", s=2, h=MH)
        att = carve_all(work, [("p", [2, 3 * L]), ("pt", [2, 3 * L])])
        ml = carve_all(work, [("decay", [4, L]), ("pt", [4, L]), ("inter", [2, 2, P + 1]),
                              ("ns", [2, 2 * (P + 1)]), ("hd", [4, P]), ("kw", [2, P])])
        c_out = abias[:, :, :].rearrange("p (h e) k -> p h e k", h=MH)
        sm = carve_all(small, [("amax", [NH, 2]), ("aneg", [NH, 2]), ("asum", [NH, 2]), ("arec", [NH, 2]),
                               ("cols", [10, MH]), ("em", [4, MH]), ("wsrc", [MH, 2]), ("den", [4]),
                               ("hsum", [8]), ("hvar", [8]), ("mlast", [2], MH)])
        sig_gate = work[:, 0:KD * TOK].rearrange("p (a b) -> p a b", a=KD)
        n_out = gates[0:2, 0:2, :].rearrange("p a b -> p (a b)")
        mo = carve_all(zf, [("h_tok", [2, D]), ("xg", [KD, SLOTS]), ("glu", [8, SLOTS]), ("lin", [8, SLOTS]),
                            ("sig", [8, SLOTS]), ("act", [8, SLOTS]), ("yt", [KD, SLOTS]),
                            ("y_tok", [D], SLOTS), ("selt", [TOK], SLOTS), ("bdn", [D], NE), ("gt", [TOK], NE),
                            ("sel", [2, SLOTS]), ("selg", [2, SLOTS])])
        rt = carve_all(work, [("lg", [2, NE]), ("top", [2, 8]), ("idxf", [2, 8]), ("ex", [2, TOPK]),
                              ("neg", [2]), ("sum", [2]), ("oh", [2 * TOPK, NE]),
                              ("ohg", [2 * TOPK, NE]), ("picked", [2, NE]), ("posm", [2, NE + 1]),
                              ("gm", [2, NE + 1]), ("cmp", [3], NE), ("np", [1], NE), ("pinc", [1], NE),
                              ("past", [MAX_PASS + 1], NE), ("tabf", [N_TAB], 1), ("brt", [NE], 1)])
        wrt = cinit[:, :, :, :].rearrange("p a b c -> p (a b c)")[:, 0:KD * NE].rearrange(
            "p (k e) -> p k e", k=KD)
        idx = sb("idx", [P, 2, 8], U32)

        def pcol(name, i=0, n=1):
            return par[:, PC[name] + i:PC[name] + i + n]

        def per_stream(v):
            return v.rearrange("p k (s t) -> p (k s) t", s=2)

        def over(v, n):
            return v.unsqueeze(2).to_broadcast([v.shape[0], v.shape[1], n])

        chunk_in = [sem(f"chunk_in{i}") for i in range(RING)]
        S = {}

        def S_(names):
            for n in names.split():
                S[n] = sem(n)

        S_("chunk_used x_in par_in gatew_in mrow_in kctx_in vctx_in cinit_in rpb_in bgu_in router_in bdn_in")
        S_("ones_made consts_made pads_made squared ssq var root cond_sig cond_ready h_ready")
        S_("proj_kept gates_summed gates_kept cg_sig glu_done f_abs f_exp f_log rows_ready w_ready km_scaled "
           "cols_turned cols_kept em_ready conv_step conv_done conv_sum conv_sq conv_sqsum conv_var conv_root "
           "conv_lin conv_sig yc_ready v_turned v_kept")
        S_("bias_turned bias_ready scored exp_in exp_done probs_ready probs_turned pt_kept attended att_kept")
        S_("spread decayed keyed weighed ptm_ready summed inter_made inter_kept kw_ready state_made state_kept ns_made "
           "hm_var hm_root hm_ready hm_turned om_sig ym_ready")
        S_("gate_sig merge_read merge_done mixed h2_turned h2_kept logits_made top_made "
           "top_exp picked_made gm_made ranked counted np_made before_made past_made tab_summed table_made gt_turned gt_kept acc_begun")
        S_("sel_ready selg_ready gathered xg_ready glu_ready sig_ready act_ready selt_turned selt_kept "
           "yt_kept y_turned y_kept scattered acc_kept acc_turned y_ready")
        S_("dve_step act_step pool_step dve_pass kv_stored state_stored y_stored")

        def linker(eng, name):
            n = [0]

            def link(ins):
                n[0] += 1
                ins.then_inc(S[name], 1)
                eng.wait_ge(S[name], n[0])
            return link

        def arrived(eng, c):
            eng.wait_ge(chunk_in[c % RING], 16 * (c // RING + 1))

        def expert_slot(j):
            return (N_TRUNK + j) % RING

        def expert_arrived(eng, j, e):
            before = len([c for c in range(N_TRUNK) if c % RING == expert_slot(j)])
            eng.wait_ge(chunk_in[expert_slot(j)], e * 16 + 16 * (before + 1))

        def table(eng, at, lo, hi):
            return eng.value_load(tab[0:1, bass.ds(at, 1)], min_val=lo, max_val=hi)

        block = ctx.enter_context(nc.Block())

        @block.sync
        def _(sp):
            for c in range(RING):
                sp.dma_start(ring[:, c, :], trunk_w[c]).then_inc(chunk_in[c], 16)
            rounds = N_TRUNK // RING
            with sp.Fori(1, rounds) as r:
                for s in range(RING):
                    sp.wait_ge(S["chunk_used"], r * RING + (s + 1 - RING))
                    sp.dma_start(ring[:, s, :], trunk_w[bass.ds(r * RING + s, 1)].rearrange(
                        "o p n -> (o p) n")).then_inc(chunk_in[s], 16)
            for c in range(rounds * RING, N_TRUNK):
                sp.wait_ge(S["chunk_used"], c - RING + 1)
                sp.dma_start(ring[:, c % RING, :], trunk_w[c]).then_inc(chunk_in[c % RING], 16)
            for j in range(RING):
                sp.wait_ge(S["chunk_used"], N_TRUNK - RING + j + 1)
                sp.dma_start(ring[:, expert_slot(j), :], expert_w[j]).then_inc(chunk_in[expert_slot(j)], 16)
            sp.wait_ge(S["table_made"], 1)
            with sp.Fori(1, NE) as e:
                before = table(sp, e + T_BEFORE, 1, MAX_PASS)
                for j in range(RING):
                    sp.wait_ge(S["chunk_used"], before * RING + (N_TRUNK - RING + j + 1))
                    sp.dma_start(ring[:, expert_slot(j), :], expert_w[bass.ds(e * RING + j, 1)].rearrange(
                        "o p n -> (o p) n")).then_inc(chunk_in[expert_slot(j)], 16)

        @block.gpsimd
        def _(pool):
            link = linker(pool, "pool_step")
            link(pool.memset(ident[:, :], 0.0))
            link(pool.affine_select(out=ident[:, :], in_=ident[:, :], compare_op=ALU.not_equal, fill=1.0,
                                    base=0, pattern=[[-1, P]], channel_multiplier=1))
            link(pool.memset(mirror[:, :], 0.0))
            for r in range(2):
                link(pool.affine_select(out=mirror[:, :], in_=mirror[:, :], compare_op=ALU.not_equal, fill=1.0,
                                        base=-(2 * r * GRID_W + GRID_W - 1), pattern=[[1, P]], channel_multiplier=1))
            link(pool.memset(strict[:, :], 1.0))
            link(pool.affine_select(out=strict[:, :], in_=strict[:, :], compare_op=ALU.is_gt, fill=0.0,
                                    base=0, pattern=[[1, P]], channel_multiplier=-1))
            link(pool.memset(selrow[:, :, :], 0.0))
            link(pool.affine_select(out=selrow[:, :, :], in_=selrow[:, :, :], compare_op=ALU.not_equal, fill=1.0,
                                    base=0, pattern=[[-1, MH], [0, P]], channel_multiplier=1))
            link(pool.memset(dmask[:, :, :, :], 0.0))
            for d, sign in ((0, 1), (1, -1)):
                link(pool.affine_select(out=dmask[:, d, :, :], in_=dmask[:, d, :, :], compare_op=ALU.is_ge,
                                        fill=FAR, base=0, pattern=[[0, 2], [sign, L]], channel_multiplier=-sign))
            link(pool.memset(amask[:, :], 0.0))
            half = WIN_COLS // 2
            for r in range(2):
                m = amask[r * GRID_W:(r + 1) * GRID_W, :].rearrange("p (r c) -> p r c", r=2)
                low, high = m[:, :, 0:GRID_W - WIN_COLS], m[:, :, WIN_COLS:GRID_W]
                link(pool.affine_select(out=low, in_=low, compare_op=ALU.is_ge, fill=FAR, base=half,
                                        pattern=[[0, 2], [1, GRID_W - WIN_COLS]], channel_multiplier=-1))
                link(pool.affine_select(out=high, in_=high, compare_op=ALU.is_ge, fill=FAR,
                                        base=half - 1 - WIN_COLS,
                                        pattern=[[0, 2], [-1, GRID_W - WIN_COLS]], channel_multiplier=1))
            pool.iota(iota[:, :], pattern=[[1, TOK]], base=0, channel_multiplier=0,
                      allow_small_or_imprecise_dtypes=True).then_inc(S["consts_made"], 1)

        @block.scalar
        def _(act):
            link = linker(act, "act_step")

            def func(out, in_, f, **kw):
                return act.activation(out, in_, f, **kw)

            act.dma_start(x[:, :, :], x_t).then_inc(S["x_in"], 16)
            act.dma_start(par[:, :], params).then_inc(S["par_in"], 16)
            act.dma_start(wgate[:, :, :], w_gate).then_inc(S["gatew_in"], 16)
            act.dma_start(bgate[:, :], b_gate).then_inc(S["mrow_in"], 16)
            act.dma_start(minit[:, :], m_init).then_inc(S["mrow_in"], 16)
            for r in range(2):
                for rk in range(2):
                    at = (rk - r + WIN_ROWS - 1) * RPB_COLS + WIN_COLS - 1 - (GRID_W - 1)
                    act.dma_start(abias[r * GRID_W:(r + 1) * GRID_W, :, rk * GRID_W:(rk + 1) * GRID_W],
                                  bass.AP(rpb.tensor, at, [[1, GRID_W], [RPB_ROWS * RPB_COLS, NH], [1, GRID_W]])
                                  ).then_inc(S["rpb_in"], 16)
            act.dma_start(kctx[:, :, :], k_ctx_t).then_inc(S["kctx_in"], 16)
            act.dma_start(vctx[:, :], v_ctx).then_inc(S["vctx_in"], 16)
            act.dma_start(cinit[:, :, :, :], c_init_t).then_inc(S["cinit_in"], 16)
            act.dma_start(bgu[:, :, :], b_gu).then_inc(S["bgu_in"], 16)

            def norm_root(n):
                act.wait_ge(S["var"], n)
                func(rstd[:, :], rstd[:, :], ACT.Sqrt).then_inc(S["root"], 1)

            act.wait_ge(S["x_in"], 16)
            func(h[:, :, :], x[:, :, :], ACT.Square).then_inc(S["squared"], 1)
            act.wait_ge(S["par_in"], 16)
            func(cond[:, :], pcol("cond", 0, 2 * KD), ACT.Sigmoid).then_inc(S["cond_sig"], 1)
            norm_root(1)

            def keep_proj(i):
                act.wait_ge(S["chunk_used"], N_MOD + i + 1)
                for b in range(4):
                    func(z[:, 4 * i + b, :], bank[2 * (i % 2) + b // 2][:, (b % 2) * TOK:(b % 2 + 1) * TOK],
                         ACT.Identity, bias=pcol("b_in", 4 * i + b)).then_inc(S["proj_kept"], 1)

            keep_proj(0)
            keep_proj(1)
            act.wait_ge(S["proj_kept"], 8)
            func(zblocks("cg"), zblocks("cg"), ACT.Sigmoid).then_inc(S["cg_sig"], 1)
            act.wait_ge(S["gates_summed"], 1)
            act.wait_ge(S["mrow_in"], 32)
            for q in range(4):
                func(gates[:, q, :], bank[6 + q // 2][0:MH, (q % 2) * TOK:(q % 2 + 1) * TOK], ACT.Identity,
                     bias=bgate[:, q:q + 1]).then_inc(S["gates_kept"], 1)
            act.wait_ge(S["f_abs"], 1)
            func(rows["g"], rows["g"], ACT.Exp, scale=-1.0).then_inc(S["f_exp"], 1)
            act.wait_ge(S["f_exp"], 1)
            func(rows["g"], rows["g"], ACT.Ln, bias=1.0).then_inc(S["f_log"], 1)
            act.wait_ge(S["rows_ready"], 1)
            for d in range(2):
                func(rows["w"][:, d, :], rows["negm"][:, d, L:TOK], ACT.Exp, bias=minit[:, d:d + 1]
                     ).then_inc(S["w_ready"], 1)
            for i in range(2, len(PROJ)):
                keep_proj(i)
            act.wait_ge(S["proj_kept"], 4 * len(PROJ))
            func(zblocks("km"), zblocks("km"), ACT.Copy, scale=M_SCALE).then_inc(S["km_scaled"], 1)

            act.wait_ge(S["proj_kept"], 4 * len(PROJ))
            act.dma_start(k_new_t, z[:, Z["ka"]:Z["ka"] + 4, 0:L]).then_inc(S["kv_stored"], 16)
            act.dma_start(v_new_t, z[:, Z["va"]:Z["va"] + 4, 0:L]).then_inc(S["kv_stored"], 16)

            act.wait_ge(S["cols_turned"], 1)
            func(sm["cols"], bank[6][:, 0:40].rearrange("p (a b) -> p a b", a=10), ACT.Copy
                 ).then_inc(S["cols_kept"], 1)
            act.wait_ge(S["cols_kept"], 1)
            func(sm["em"], sm["cols"][:, 4:8, :], ACT.Exp, scale=-1.0).then_inc(S["em_ready"], 1)
            act.wait_ge(S["v_turned"], 1)
            act.wait_ge(S["glu_done"], 1)
            for s in range(2):
                func(va_tok[:, s, :], bank[s][:, :], ACT.Copy).then_inc(S["v_kept"], 1)
            act.wait_ge(S["v_turned"], 2)
            for s in range(2):
                func(vmt[:, s, :, 0:P], bank[2 + s][:, :].rearrange("p (a b) -> p a b", a=MH), ACT.Copy
                     ).then_inc(S["v_kept"], 1)
            act.wait_ge(S["v_turned"], 3)
            func(kmt[:, :, :], bank[7][:, :].rearrange("p (a b) -> p a b", a=MH), ACT.Copy
                 ).then_inc(S["v_kept"], 1)

            act.wait_ge(S["conv_var"], 1)
            func(rstd[:, :], rstd[:, :], ACT.Sqrt).then_inc(S["conv_root"], 1)
            act.wait_ge(S["conv_lin"], 1)
            func(conv_sq, acc, ACT.Sigmoid).then_inc(S["conv_sig"], 1)
            func(zblocks("om"), zblocks("om"), ACT.Sigmoid).then_inc(S["om_sig"], 1)

            for i in range(NH):
                act.wait_ge(S["exp_in"], i + 1)
                if i >= 2:
                    act.wait_ge(S["probs_turned"], i - 1)
                b = bank[4 + i % 2]
                func(att["p"][:, i % 2, 0:L], b[:, 0:L], ACT.Exp, scale=ATT_SCALE, bias=sm["aneg"][:, i, 0:1],
                     accum_out=sm["asum"][:, i, 0:1]).then_inc(S["exp_done"], 1)
                func(att["p"][:, i % 2, L:3 * L], b[:, L:3 * L], ACT.Exp, scale=ATT_SCALE,
                     bias=sm["aneg"][:, i, 1:2], accum_out=sm["asum"][:, i, 1:2]).then_inc(S["exp_done"], 1)

            act.wait_ge(S["att_kept"], NH // 2)
            act.wait_ge(S["pads_made"], 3)
            for i in range(MH):
                act.wait_ge(S["spread"], i + 1)
                if i:
                    act.wait_ge(S["kw_ready"], i)
                for q in range(4):
                    func(ml["decay"][:, q, :], bank[4][:, q * L:(q + 1) * L], ACT.Exp,
                         bias=sm["cols"][:, q, i:i + 1]).then_inc(S["decayed"], 1)
                act.wait_ge(S["inter_made"], i + 1)
                if i:
                    act.wait_ge(S["ns_made"], 2 * i)
                for d in range(2):
                    func(ml["inter"][:, d, 1, :], bank[0][:, d * (P + 1):(d + 1) * (P + 1)], ACT.Copy,
                         scale=sm["cols"][:, 8 + d, i:i + 1]).then_inc(S["inter_kept"], 1)
                act.wait_ge(S["state_made"], i + 1)
                func(c_out[:, i, :, :], bank[1][:, 0:2 * P].rearrange("p (a b) -> p a b", a=2), ACT.Copy
                     ).then_inc(S["state_kept"], 1)
            func(n_out, bank[2][0:2, :], ACT.Copy).then_inc(S["state_kept"], 1)
            act.wait_ge(S["state_kept"], MH + 1)
            act.dma_start(c_new, c_out).then_inc(S["state_stored"], 16)
            act.dma_start(n_new, n_out).then_inc(S["state_stored"], 16)
            act.dma_start(m_new, sm["mlast"]).then_inc(S["state_stored"], 16)
            act.wait_ge(S["hm_var"], 1)
            func(sm["hvar"], sm["hvar"], ACT.Sqrt).then_inc(S["hm_root"], 1)

            act.wait_ge(S["ym_ready"], 1)
            for n, br in enumerate(BRANCHES):
                if n:
                    act.wait_ge(S["merge_read"], 4 * n)
                for g in range(2):
                    act.wait_ge(S["chunk_used"], C_MERGE + 3 * n + g + 1)
                    for b in range(4):
                        func(sig_gate[:, 4 * g + b, :],
                             bank[2 * g + b // 2][:, (b % 2) * TOK:(b % 2 + 1) * TOK], ACT.Sigmoid,
                             bias=pcol("b_in", 36 + 8 * n + 4 * g + b)).then_inc(S["gate_sig"], 1)

            act.wait_ge(S["mixed"], 1)
            act.dma_start(wrt, w_router).then_inc(S["router_in"], 16)
            act.dma_start(rt["brt"], b_router).then_inc(S["router_in"], 16)
            act.dma_start(mo["bdn"], b_down).then_inc(S["bdn_in"], 16)
            func(h[:, :, :], x[:, :, :], ACT.Square).then_inc(S["squared"], 1)
            norm_root(2)
            act.wait_ge(S["h2_turned"], 1)
            for q in range(4):
                func(mo["h_tok"][:, q // 2, (q % 2) * 512:(q % 2 + 1) * 512], bank[q][:, :], ACT.Copy
                     ).then_inc(S["h2_kept"], 1)
            act.wait_ge(S["top_made"], 1)
            for s in range(2):
                func(rt["ex"][:, s, :], rt["top"][:, s, 0:TOPK], ACT.Exp, bias=rt["neg"][:, s:s + 1],
                     accum_out=rt["sum"][:, s:s + 1]).then_inc(S["top_exp"], 1)

            act.wait_ge(S["gathered"], 1)
            func(mo["xg"], bank[4][:, :].rearrange("p (a b) -> p a b", a=KD), ACT.Copy).then_inc(S["xg_ready"], 1)
            act.wait_ge(S["table_made"], 1)
            n_pass = table(act, T_ALL, NE, MAX_PASS)
            with act.Fori(0, n_pass) as n:
                for f in range(2):
                    act.wait_ge(S["glu_ready"], n * 2 + (f + 1))
                    func(mo["sig"][:, 4 * f:4 * f + 4, :], mo["glu"][:, 4 * f:4 * f + 4, :], ACT.Sigmoid,
                         scale=ALPHA).then_inc(S["sig_ready"], 1)
                act.wait_ge(S["selt_turned"], n + 1)
                func(mo["selt"], bank[7][0:SLOTS, 0:TOK], ACT.Copy).then_inc(S["selt_kept"], 1)
                act.wait_ge(S["gathered"], n + 2)
                func(mo["xg"], bank[4][:, :].rearrange("p (a b) -> p a b", a=KD), ACT.Copy
                     ).then_inc(S["xg_ready"], 1)
                act.wait_ge(S["chunk_used"], n * RING + (N_TRUNK + RING))
                func(mo["yt"], bank[7][:, :].rearrange("p (a b) -> p a b", a=KD), ACT.Copy
                     ).then_inc(S["yt_kept"], 1)
                act.wait_ge(S["y_turned"], n + 1)
                func(mo["y_tok"][:, 0:512], bank[5][0:SLOTS, :], ACT.Copy).then_inc(S["y_kept"], 1)

            act.wait_ge(S["scattered"], n_pass)
            for q in range(4):
                func(mo["h_tok"][:, q // 2, (q % 2) * 512:(q % 2 + 1) * 512], bank[q][:, :], ACT.Copy
                     ).then_inc(S["acc_kept"], 1)
            act.wait_ge(S["mixed"], 2)
            func(h[:, :, :], x[:, :, :], ACT.Square).then_inc(S["squared"], 1)
            norm_root(3)
            act.wait_ge(S["y_ready"], 1)
            act.dma_start(y_t, x[:, :, :]).then_inc(S["y_stored"], 16)
            act.wait_ge(S["y_stored"], 16)
            act.wait_ge(S["kv_stored"], 32)
            act.wait_ge(S["state_stored"], 48)

        @block.vector
        def _(dve):
            link = linker(dve, "dve_step")

            def rstd_from(src, count, eps, ready, root, n):
                dve.tensor_scalar(rstd[:, :], src, 1.0 / count, eps, ALU.mult, ALU.add).then_inc(S[ready], 1)
                dve.wait_ge(S[root], n)
                link(dve.reciprocal(rstd[:, :], rstd[:, :]))

            def modulated(which, n):
                dve.wait_ge(S["ssq"], n)
                rstd_from(bank[4][:, 0:TOK], D, RMS_EPS, "var", "root", n)
                link(dve.tensor_tensor(h[:, :, :], x[:, :, :],
                                       rstd[:, :].unsqueeze(1).to_broadcast([P, KD, TOK]), ALU.mult))
                if which == 0:
                    dve.wait_ge(S["chunk_used"], N_MOD)
                    link(dve.tensor_tensor(mod[:, :, :], bank[5][:, 0:96].rearrange("p (a b) -> p a b", a=48),
                                           over(pcol("b_mod", 0, 48), 2), ALU.add))
                    for i, name in enumerate(("norm1", "norm2")):
                        link(dve.scalar_tensor_tensor(gain[:, i, :, :], mod[:, 24 * i + 8:24 * i + 16, :], 1.0,
                                                      over(pcol(name, 0, KD), 2), ALU.add, ALU.mult))
                g = gain[:, which, :, :].rearrange("p k s -> p (k s)")
                sh = mod[:, 24 * which:24 * which + KD, :].rearrange("p k s -> p (k s)")
                hs = per_stream(h[:, :, :])
                link(dve.tensor_tensor(hs, hs, over(g, L), ALU.mult))
                dve.tensor_tensor(hs, hs, over(sh, L), ALU.add).then_inc(S["h_ready"], 1)

            dve.memset(ones[:, :], 1.0).then_inc(S["ones_made"], 1)
            dve.memset(apad[:, :, :, :], 0.0).then_inc(S["pads_made"], 1)
            dve.memset(vmt[:, :, :, P:P + 1], 1.0).then_inc(S["pads_made"], 1)
            dve.wait_ge(S["cond_sig"], 1)
            dve.tensor_tensor(cond[:, :], cond[:, :], pcol("cond", 0, 2 * KD), ALU.mult).then_inc(S["cond_ready"], 1)
            dve.wait_ge(S["bias_turned"], 1)
            for q in range(2):
                dve.scalar_tensor_tensor(abias[:, 4 * q:4 * q + 4, :],
                                         bank[6 + q][:, :].rearrange("p (a b) -> p a b", a=4), 1.0 / ATT_SCALE,
                                         amask[:, :].unsqueeze(1).to_broadcast([P, 4, L]), ALU.mult, ALU.add
                                         ).then_inc(S["bias_ready"], 1)
            modulated(0, 1)

            dve.wait_ge(S["cg_sig"], 1)
            dve.wait_ge(S["pads_made"], 1)
            dve.tensor_tensor(apad[:, :, :, PAD:PAD + L], zblocks("cu").rearrange("p k (s t) -> p k s t", s=2),
                              zblocks("cg").rearrange("p k (s t) -> p k s t", s=2), ALU.mult
                              ).then_inc(S["glu_done"], 1)

            dve.wait_ge(S["gates_kept"], 4)
            dve.scalar_tensor_tensor(rows["g"], gates[:, 1:4:2, :], -1.0, gates[:, 1:4:2, :], ALU.mult, ALU.max
                                     ).then_inc(S["f_abs"], 1)
            dve.wait_ge(S["f_log"], 1)
            link(dve.scalar_tensor_tensor(rows["g"], gates[:, 1:4:2, :], 0.0, rows["g"], ALU.min, ALU.subtract))

            def along(v, d, s):
                v = v[:, d, s * L:(s + 1) * L]
                return v if d == 0 else v[:, ::-1]

            dve.wait_ge(S["ones_made"], 1)
            for d in range(2):
                for s in range(2):
                    link(dve.tensor_tensor_scan(along(rows["b"], d, s), ones[0:MH, :], along(rows["g"], d, s), 0.0,
                                                ALU.mult, ALU.add))
            link(dve.tensor_tensor(rows["g"], gates[:, 0:4:2, :], rows["b"], ALU.subtract))
            for d in range(2):
                for s in range(2):
                    g = along(rows["g"], d, s)
                    link(dve.tensor_tensor_scan(along(rows["negm"], d, s), g, g,
                                                minit[:, d:d + 1] if s else LOWEST, ALU.max, ALU.max))
            link(dve.tensor_tensor(rows["b"], rows["b"], rows["negm"], ALU.add))
            dve.tensor_scalar(rows["negm"], rows["negm"], -1.0, None, ALU.mult).then_inc(S["rows_ready"], 1)
            link(dve.tensor_copy(sm["mlast"][:, 0:1], rows["b"][:, 0, L - 1:L]))
            link(dve.tensor_copy(sm["mlast"][:, 1:2], rows["b"][:, 1, 0:1]))

            dve.wait_ge(S["glu_done"], 1)

            def conv_in(b, w):
                return apad[:, b, :, bass.ds(w, L)]

            accs = [acc[:, b, :].rearrange("p (s t) -> p s t", s=2) for b in range(4)]
            for b in range(4):
                dve.tensor_scalar(accs[b], conv_in(b, 0), pcol("w_dw", b * CONV_W), pcol("b_dw", b),
                                  ALU.mult, ALU.add).then_inc(S["conv_step"], 1)
            with dve.Fori(1, CONV_W) as w:
                for b in range(4):
                    dve.wait_ge(S["conv_step"], w * 4 + (b + 1 - 4))
                    tap = par[:, bass.ds(w + (PC["w_dw"] + b * CONV_W), 1)]
                    dve.scalar_tensor_tensor(accs[b], conv_in(b, w), tap, accs[b], ALU.mult, ALU.add
                                             ).then_inc(S["conv_step"], 1)
            dve.wait_ge(S["conv_sum"], 1)
            link(dve.tensor_scalar(rstd[:, :], bank[4][:, 0:TOK], -1.0 / (4 * P), None, ALU.mult))
            link(dve.tensor_tensor(acc, acc, rstd[:, :].unsqueeze(1).to_broadcast([P, 4, TOK]), ALU.add))
            dve.tensor_tensor(conv_sq, acc, acc, ALU.mult).then_inc(S["conv_sq"], 1)
            dve.wait_ge(S["conv_sqsum"], 1)
            rstd_from(bank[4][:, TOK:2 * TOK], 4 * P, LN_EPS, "conv_var", "conv_root", 1)
            link(dve.tensor_tensor(acc, acc, rstd[:, :].unsqueeze(1).to_broadcast([P, 4, TOK]), ALU.mult))
            for b in range(4):
                dve.tensor_scalar(acc[:, b, :], acc[:, b, :], pcol("cln_g", b), pcol("cln_b", b),
                                  ALU.mult, ALU.add).then_inc(S["conv_lin"] if b == 3 else S["conv_step"], 1)
            dve.wait_ge(S["conv_sig"], 1)
            dve.tensor_tensor(acc, acc, conv_sq, ALU.mult).then_inc(S["yc_ready"], 1)

            def att_front(i):
                dve.wait_ge(S["scored"], i + 1)
                b = bank[4 + i % 2]
                link(dve.tensor_tensor(b[:, L:2 * L], b[:, L:2 * L], abias[:, i, :], ALU.add))
                dve.tensor_reduce(sm["amax"][:, i, 0:1], b[:, 0:L], AX, ALU.max)
                link(dve.tensor_reduce(sm["amax"][:, i, 1:2], b[:, L:3 * L], AX, ALU.max))
                dve.tensor_scalar(sm["aneg"][:, i, :], sm["amax"][:, i, :], -ATT_SCALE, None, ALU.mult
                                  ).then_inc(S["exp_in"], 1)

            def att_back(i):
                dve.wait_ge(S["exp_done"], 2 * i + 2)
                link(dve.reciprocal(sm["arec"][:, i, :], sm["asum"][:, i, :]))
                p = att["p"][:, i % 2, :]
                link(dve.tensor_scalar(p[:, 0:L], p[:, 0:L], sm["arec"][:, i, 0:1], None, ALU.mult))
                dve.tensor_scalar(p[:, L:3 * L], p[:, L:3 * L], sm["arec"][:, i, 1:2], None, ALU.mult
                                  ).then_inc(S["probs_ready"], 1)
                dve.wait_ge(S["probs_turned"], i + 1)
                if i >= 2:
                    dve.wait_ge(S["attended"], i - 1)
                dve.tensor_copy(att["pt"][:, i % 2, :], bank[6 + i % 2][:, 0:3 * L]).then_inc(S["pt_kept"], 1)
                if i % 2:
                    dve.wait_ge(S["attended"], i + 1)
                    dve.tensor_copy(branch_out["a"][:, i // 2, :], bank[(i // 2) % 2][:, 0:TOK]
                                    ).then_inc(S["att_kept"], 1)

            dve.wait_ge(S["bias_ready"], 2)
            for i in range(NH + 1):
                if i < NH:
                    att_front(i)
                if i:
                    att_back(i - 1)

            km_tok = kmt[:, :, :]
            dve.memset(ml["inter"][:, :, 0, :], 0.0).then_inc(S["pads_made"], 1)
            dve.wait_ge(S["em_ready"], 1)
            dve.wait_ge(S["v_kept"], 5)
            for i in range(MH):
                dve.wait_ge(S["decayed"], 4 * i + 4)
                dve.wait_ge(S["keyed"], i + 1)
                if i:
                    dve.wait_ge(S["summed"], i)
                keys = bank[5][:, 0:TOK].unsqueeze(1).to_broadcast([P, 2, TOK])
                dve.tensor_tensor(ml["pt"].rearrange("p (d s) t -> p d (s t)", d=2), keys,
                                  ml["decay"].rearrange("p (d s) t -> p d (s t)", d=2), ALU.mult
                                  ).then_inc(S["ptm_ready"], 1)
                link(dve.tensor_copy(sm["wsrc"][:, i, 0:1], ml["decay"][:, 0, L - 1:L]))
                link(dve.tensor_copy(sm["wsrc"][:, i, 1:2], ml["decay"][:, 2, 0:1]))
                if i:
                    dve.wait_ge(S["state_made"], i)
                link(dve.tensor_scalar(ml["kw"][:, 0, :], km_tok[:, i, :], sm["wsrc"][:, i, 0:1], None, ALU.mult))
                dve.tensor_scalar(ml["kw"][:, 1, :], km_tok[:, i, :], sm["wsrc"][:, i, 1:2], None, ALU.mult
                                  ).then_inc(S["kw_ready"], 1)
                dve.wait_ge(S["summed"], i + 1)
                dve.wait_ge(S["inter_kept"], 2 * i + 2)
                for d in range(2):
                    dve.tensor_tensor(ml["ns"][:, d, :], bank[6 + d][:, 0:2 * (P + 1)],
                                      ml["inter"][:, d, :, :].rearrange("p s c -> p (s c)"), ALU.add
                                      ).then_inc(S["ns_made"], 1)
                dve.wait_ge(S["ns_made"], 2 * i + 2)
                ns = ml["ns"].rearrange("p d (s c) -> p (d s) c", s=2)
                den = ns[:, :, P:P + 1].rearrange("p a b -> p (a b)")
                link(dve.scalar_tensor_tensor(sm["den"], den, -1.0, den, ALU.mult, ALU.max))
                link(dve.tensor_tensor(sm["den"], sm["den"], sm["em"][:, :, i:i + 1].rearrange("p a b -> p (a b)"),
                                       ALU.max))
                link(dve.reciprocal(sm["den"], sm["den"]))
                link(dve.tensor_tensor(ml["hd"], ns[:, :, 0:P], over(sm["den"], P), ALU.mult))
                link(dve.tensor_tensor(hm[:, :, i, :], ml["hd"][:, 0:2, :], ml["hd"][:, 2:4, :], ALU.add))
            hv = hm.rearrange("p s h d -> p (s h) d")
            sq = work[:, 0:2 * MH * P].rearrange("p (a d) -> p a d", a=2 * MH)
            link(dve.tensor_reduce(sm["hsum"], hv, AX, ALU.add))
            link(dve.tensor_scalar(sm["hsum"], sm["hsum"], -1.0 / P, None, ALU.mult))
            link(dve.tensor_tensor(hv, hv, over(sm["hsum"], P), ALU.add))
            link(dve.tensor_tensor(sq, hv, hv, ALU.mult))
            link(dve.tensor_reduce(sm["hvar"], sq, AX, ALU.add))
            dve.tensor_scalar(sm["hvar"], sm["hvar"], 1.0 / P, LN_EPS, ALU.mult, ALU.add).then_inc(S["hm_var"], 1)
            dve.wait_ge(S["hm_root"], 1)
            link(dve.reciprocal(sm["hvar"], sm["hvar"]))
            dve.tensor_tensor(hv, hv, over(sm["hvar"], P), ALU.mult).then_inc(S["hm_ready"], 1)
            dve.wait_ge(S["hm_turned"], 1)
            dve.wait_ge(S["om_sig"], 1)
            for i in range(MH):
                om = branch_out["m"][:, i, :]
                ins = dve.scalar_tensor_tensor(om, bank[4 + i // 2][:, (i % 2) * TOK:(i % 2 + 1) * TOK],
                                               pcol("mnorm", i), om, ALU.mult, ALU.mult)
            ins.then_inc(S["ym_ready"], 1)

            for n in range(len(BRANCHES)):
                dve.wait_ge(S["chunk_used"], C_MERGE + 3 * n + 3)
                dve.wait_ge(S["gate_sig"], 8 * n + 8)
                for q in range(4):
                    s2 = sig_gate[:, 2 * q:2 * q + 2, :]
                    m2 = merged[:, 2 * q:2 * q + 2, :]
                    pr = bank[4 + q][:, :].rearrange("p (a b) -> p a b", a=2)
                    if n == 0:
                        dve.tensor_tensor(m2, s2, pr, ALU.mult).then_inc(S["merge_read"], 1)
                    else:
                        link(dve.tensor_tensor(s2, s2, pr, ALU.mult))
                        dve.tensor_tensor(m2, m2, s2, ALU.add).then_inc(S["merge_read"], 1)

            def add_gated(src, part, n):
                for k in range(KD):
                    for s in range(2):
                        ins = dve.scalar_tensor_tensor(x[:, k, s * L:(s + 1) * L], src(k, s), mod[:, part + k, s:s + 1],
                                                       x[:, k, s * L:(s + 1) * L], ALU.mult, ALU.add)
                ins.then_inc(S["mixed"], 1)

            dve.wait_ge(S["chunk_used"], N_TRUNK)
            add_gated(lambda k, s: bank[k // 2][:, (k % 2) * TOK + s * L:(k % 2) * TOK + (s + 1) * L], 16, 1)
            modulated(1, 2)

            dve.wait_ge(S["logits_made"], 1)
            link(dve.tensor_copy(rt["lg"], bank[5][:, 0:2 * NE].rearrange("p (a b) -> p a b", a=2)))
            for s in range(2):
                link(dve.max(rt["top"][:, s, :], rt["lg"][:, s, :]))
                link(dve.max_index(idx[:, s, :], rt["top"][:, s, :], rt["lg"][:, s, :]))
            dve.tensor_scalar(rt["neg"], rt["top"][:, :, 0:1].rearrange("p a b -> p (a b)"), -1.0, None, ALU.mult
                              ).then_inc(S["top_made"], 1)
            link(dve.tensor_copy(rt["idxf"], idx[:, :, :]))
            for s in range(2):
                oh = rt["oh"][:, TOPK * s:TOPK * s + TOPK, :]
                link(dve.tensor_tensor(oh, iota[:, 0:NE].unsqueeze(1).to_broadcast([P, TOPK, NE]),
                                       over(rt["idxf"][:, s, 0:TOPK], NE), ALU.is_equal))
                dve.tensor_reduce(rt["picked"][:, s, :], oh.rearrange("p k e -> p e k"), AX, ALU.add
                                  ).then_inc(S["picked_made"], 1)
            dve.memset(rt["gm"], 0.0)
            link(dve.memset(rt["posm"], -1.0))
            dve.wait_ge(S["top_exp"], 2)
            link(dve.reciprocal(rt["sum"], rt["sum"]))
            for s in range(2):
                oh = rt["oh"][:, TOPK * s:TOPK * s + TOPK, :]
                ohg = rt["ohg"][:, TOPK * s:TOPK * s + TOPK, :]
                link(dve.tensor_scalar(rt["ex"][:, s, :], rt["ex"][:, s, :], rt["sum"][:, s:s + 1], None, ALU.mult))
                link(dve.tensor_tensor(ohg, oh, over(rt["ex"][:, s, :], NE), ALU.mult))
                dve.tensor_reduce(rt["gm"][:, s, 0:NE], ohg.rearrange("p k e -> p e k"), AX, ALU.add
                                  ).then_inc(S["gm_made"], 1)
            dve.wait_ge(S["ranked"], 1)
            dve.wait_ge(S["picked_made"], 2)
            link(dve.scalar_tensor_tensor(rt["posm"][:, :, 0:NE],
                                          bank[5][:, 64:64 + 2 * NE].rearrange("p (a b) -> p a b", a=2), 1.0,
                                          rt["picked"], ALU.add, ALU.mult))
            link(dve.tensor_scalar(rt["posm"][:, :, 0:NE], rt["posm"][:, :, 0:NE], -1.0, None, ALU.add))
            dve.wait_ge(S["counted"], 1)
            link(dve.tensor_scalar(rt["cmp"], iota[0:NE, SLOTS:TOK:SLOTS], bank[6][0:NE, 0:1], None, ALU.is_lt))
            link(dve.tensor_reduce(rt["np"], rt["cmp"], AX, ALU.add))
            dve.tensor_scalar(rt["np"], rt["np"], 1.0, None, ALU.add).then_inc(S["np_made"], 1)
            dve.wait_ge(S["before_made"], 1)
            link(dve.tensor_tensor(rt["pinc"], bank[6][0:NE, 1:2], rt["np"], ALU.add))
            dve.tensor_scalar(rt["past"], iota[0:NE, 0:MAX_PASS + 1], rt["pinc"], None, ALU.is_ge
                              ).then_inc(S["past_made"], 1)
            dve.wait_ge(S["tab_summed"], 1)
            M1 = MAX_PASS + 1
            link(dve.tensor_copy(rt["tabf"], bank[6][0:1, 64:64 + N_TAB]))
            base = rt["tabf"][:, T_BASE:T_BASE + M1]
            link(dve.tensor_tensor(base, iota[0:1, 0:M1], base, ALU.subtract))
            link(dve.tensor_scalar(base, base, float(SLOTS), float(TOK - SLOTS), ALU.mult, ALU.min))
            dve.tensor_copy(tab[:, :], rt["tabf"]).then_inc(S["table_made"], 1)
            dve.wait_ge(S["gt_turned"], 1)
            dve.tensor_copy(mo["gt"], bank[7][0:NE, 0:TOK]).then_inc(S["gt_kept"], 1)

            def select(n):
                e = table(dve, n + T_EXP, 0, NE)
                base = table(dve, n + T_BASE, 0, TOK - SLOTS)
                for s in range(2):
                    dve.tensor_scalar(mo["sel"][:, s, :], iota[:, bass.ds(base, SLOTS)],
                                      rt["posm"][:, s, bass.ds(e, 1)], None, ALU.is_equal
                                      ).then_inc(S["sel_ready"], 1)

            dve.wait_ge(S["table_made"], 1)
            select(0)
            dve.wait_ge(S["bgu_in"], 16)
            n_pass = table(dve, T_ALL, NE, MAX_PASS)
            STEPS = 8
            with dve.Fori(0, n_pass) as n:
                e = table(dve, n + T_EXP, 0, NE - 1)
                step = [0]

                def link_pass(ins):
                    step[0] += 1
                    ins.then_inc(S["dve_pass"], 1)
                    dve.wait_ge(S["dve_pass"], n * STEPS + step[0])

                dve.wait_ge(S["sel_ready"], n * 2 + 2)
                for s in range(2):
                    dve.tensor_scalar(mo["selg"][:, s, :], mo["sel"][:, s, :], rt["gm"][:, s, bass.ds(e, 1)], None,
                                      ALU.mult).then_inc(S["selg_ready"], 1)
                dve.wait_ge(S["gathered"], n + 1)
                dve.wait_ge(S["selg_ready"], n * 2 + 2)
                select(n + 1)
                for f in range(2):
                    dve.wait_ge(S["chunk_used"], n * RING + (N_TRUNK + 2 * (f + 1)))
                    gu = bank[5 + f][:, :].rearrange("p (a b) -> p a b", a=8)
                    glu, lin, sig = (mo[k][:, 4 * f:4 * f + 4, :] for k in ("glu", "lin", "sig"))
                    bias = bgu[:, :, :].rearrange("p e b -> p (e b)")
                    link_pass(dve.tensor_tensor(glu, gu[:, 0:4, :], over(bias[:, bass.ds(e * 16 + 4 * f, 4)], SLOTS),
                                                ALU.add))
                    dve.tensor_scalar(glu, glu, LIMIT, None, ALU.min).then_inc(S["glu_ready"], 1)
                    link_pass(dve.tensor_tensor(lin, gu[:, 4:8, :],
                                                over(bias[:, bass.ds(e * 16 + (8 + 4 * f), 4)], SLOTS), ALU.add))
                    link_pass(dve.tensor_scalar(lin, lin, LIMIT, -LIMIT, ALU.min, ALU.max))
                    dve.wait_ge(S["sig_ready"], n * 2 + (f + 1))
                    link_pass(dve.tensor_tensor(sig, sig, glu, ALU.mult))
                    dve.scalar_tensor_tensor(mo["act"][:, 4 * f:4 * f + 4, :], lin, 1.0, sig, ALU.add, ALU.mult
                                             ).then_inc(S["act_ready"], 1)
                assert step[0] == STEPS
                dve.wait_ge(S["y_turned"], n + 1)
                dve.tensor_copy(mo["y_tok"][:, 512:1024], bank[6][0:SLOTS, :]).then_inc(S["y_kept"], 1)

            dve.wait_ge(S["acc_turned"], 1)
            add_gated(lambda k, s: bank[4 + k // 2][:, (k % 2) * TOK + s * L:(k % 2) * TOK + (s + 1) * L], 40, 2)
            dve.wait_ge(S["mixed"], 2)
            dve.wait_ge(S["ssq"], 3)
            rstd_from(bank[0][:, 0:TOK], D, RMS_EPS, "var", "root", 3)
            link(dve.tensor_tensor(x[:, :, :], x[:, :, :], rstd[:, :].unsqueeze(1).to_broadcast([P, KD, TOK]),
                                   ALU.mult))
            dve.tensor_tensor(x[:, :, :], x[:, :, :], over(pcol("final", 0, KD), TOK), ALU.mult
                              ).then_inc(S["y_ready"], 1)

        @block.tensor
        def _(pe):
            def norm_sum(n, to):
                pe.wait_ge(S["squared"], n)
                for k in range(KD):
                    ins = pe.matmul(to, ones[:, :], h[:, k, :], start=k == 0, stop=k == KD - 1)
                ins.then_inc(S["ssq"], 1)

            def product4(c, src, to):
                arrived(pe, c)
                w = ring[:, c % RING, :].rearrange("p (k n) -> p k n", k=KD)
                for b in range(4):
                    for k in range(KD):
                        ins = pe.matmul(to(b), w[:, k, b * P:(b + 1) * P], src[:, k, :], start=k == 0, stop=k == KD - 1)
                ins.then_inc(S["chunk_used"], 1)

            pe.wait_ge(S["ones_made"], 1)
            norm_sum(1, bank[4][:, 0:TOK])

            pe.wait_ge(S["consts_made"], 1)
            pe.wait_ge(S["rpb_in"], 64)
            for q in range(2):
                ins = pe.matmul(bank[6 + q][:, :], mirror[:, :],
                                abias[:, 4 * q:4 * q + 4, :].rearrange("p a b -> p (a b)"), start=True, stop=True)
            ins.then_inc(S["bias_turned"], 1)

            pe.wait_ge(S["cond_ready"], 1)
            with pe.Fori(0, N_MOD // RING) as r:
                for s in range(RING):
                    pe.wait_ge(chunk_in[s], r * 16 + 16)
                    w = ring[:, s, :].rearrange("p (k n) -> p k n", k=KD)
                    for b in range(4):
                        for k in range(KD):
                            ins = pe.matmul(bank[5][:, bass.ds(r * (8 * RING) + (8 * s + 2 * b), 2)],
                                            w[:, k, b * P:(b + 1) * P], cond[:, 2 * k:2 * k + 2],
                                            start=k == 0, stop=k == KD - 1)
                    ins.then_inc(S["chunk_used"], 1)

            def project(i):
                if i >= 2:
                    pe.wait_ge(S["proj_kept"], 4 * (i - 1))
                product4(N_MOD + i, h, lambda b: bank[2 * (i % 2) + b // 2][:, (b % 2) * TOK:(b % 2 + 1) * TOK])

            pe.wait_ge(S["h_ready"], 1)
            project(0)
            project(1)
            pe.wait_ge(S["gatew_in"], 16)
            pe.wait_ge(S["bias_ready"], 2)
            for q in range(4):
                for k in range(KD):
                    ins = pe.matmul(bank[6 + q // 2][0:MH, (q % 2) * TOK:(q % 2 + 1) * TOK],
                                    wgate[:, k, 4 * q:4 * q + 4], h[:, k, :], start=k == 0, stop=k == KD - 1)
            ins.then_inc(S["gates_summed"], 1)
            for i in range(2, len(PROJ)):
                project(i)

            pe.wait_ge(S["consts_made"], 1)
            pe.wait_ge(S["rows_ready"], 1)
            pe.wait_ge(S["w_ready"], 2)
            pe.wait_ge(S["gates_kept"], 4)
            turns = [rows["g"][:, d, s * L:(s + 1) * L] for d in range(2) for s in range(2)]
            turns += [rows["b"][:, d, s * L:(s + 1) * L] for d in range(2) for s in range(2)]
            turns += [rows["w"][:, d, :] for d in range(2)]
            for i, v in enumerate(turns):
                ins = pe.transpose(bank[6][:, MH * i:MH * i + MH], v, ident[0:MH, 0:MH])
            ins.then_inc(S["cols_turned"], 1)
            pe.wait_ge(S["proj_kept"], 4 * len(PROJ))
            for at, name in ((0, "va"), (2, "vm")):
                for s in range(2):
                    for b in range(4):
                        ins = pe.transpose(bank[at + s][:, b * P:(b + 1) * P], z[:, Z[name] + b, s * L:(s + 1) * L],
                                           ident[:, :])
                ins.then_inc(S["v_turned"], 1)
            pe.wait_ge(S["km_scaled"], 1)
            for b in range(4):
                ins = pe.transpose(bank[7][:, b * P:(b + 1) * P], z[:, Z["km"] + b, 0:L], ident[:, :])
            ins.then_inc(S["v_turned"], 1)

            pe.wait_ge(S["conv_step"], 4 * CONV_W)
            for b in range(4):
                ins = pe.matmul(bank[4][:, 0:TOK], ones[:, :], acc[:, b, :], start=b == 0, stop=b == 3)
            ins.then_inc(S["conv_sum"], 1)
            pe.wait_ge(S["conv_sq"], 1)
            for b in range(4):
                ins = pe.matmul(bank[4][:, TOK:2 * TOK], ones[:, :], conv_sq[:, b, :], start=b == 0, stop=b == 3)
            ins.then_inc(S["conv_sqsum"], 1)

            def scores(i):
                if i >= 2:
                    pe.wait_ge(S["exp_done"], 2 * (i - 1))
                o = HD * (i % 2)
                b = bank[4 + i % 2]
                q = z[o:o + HD, Z["qa"] + i // 2, :]
                k = z[o:o + HD, Z["ka"] + i // 2, :]
                pe.matmul(b[:, 0:L], q[:, 0:L], k[:, 0:L], start=True, stop=True)
                pe.matmul(b[:, L:2 * L], q[:, L:TOK], k[:, L:TOK], start=True, stop=True)
                pe.matmul(b[:, 2 * L:3 * L], q[:, L:TOK], kctx[o:o + HD, i // 2, :], start=True, stop=True
                          ).then_inc(S["scored"], 1)

            def attend(i):
                pe.wait_ge(S["probs_ready"], i + 1)
                if i >= 2:
                    pe.wait_ge(S["pt_kept"], i - 1)
                for q in range(3):
                    ins = pe.transpose(bank[6 + i % 2][:, q * L:(q + 1) * L], att["p"][:, i % 2, q * L:(q + 1) * L],
                                       ident[:, :])
                ins.then_inc(S["probs_turned"], 1)
                pe.wait_ge(S["pt_kept"], i + 1)
                if i >= 4 and i % 2 == 0:
                    pe.wait_ge(S["att_kept"], i // 2 - 1)
                o = HD * (i % 2)
                to = bank[(i // 2) % 2][o:o + HD, :]
                pt = att["pt"][:, i % 2, :]
                cols = slice(i * HD, (i + 1) * HD)
                pe.matmul(to[:, 0:L], va_tok[:, 0, cols], pt[:, 0:L], start=True, stop=True)
                pe.matmul(to[:, L:TOK], va_tok[:, 1, cols], pt[:, L:2 * L], start=True, stop=False)
                pe.matmul(to[:, L:TOK], vctx[:, cols], pt[:, 2 * L:3 * L], start=False, stop=True
                          ).then_inc(S["attended"], 1)

            pe.wait_ge(S["kctx_in"], 16)
            pe.wait_ge(S["vctx_in"], 16)
            pe.wait_ge(S["v_kept"], 5)
            pe.wait_ge(S["cols_kept"], 1)
            pe.wait_ge(S["conv_var"], 1)
            for i in range(NH + 1):
                if i < NH:
                    scores(i)
                if i:
                    attend(i - 1)

            def ml_front(i):
                if i:
                    pe.wait_ge(S["decayed"], 4 * i)
                pe.matmul(bank[4][:, :], selrow[:, i, :], rows["negm"].rearrange("p d t -> p (d t)"),
                          start=True, stop=False)
                pe.matmul(bank[4][:, :], ident[:, :], dmask[:, :, :, :].rearrange("p d s t -> p (d s t)"),
                          start=False, stop=True).then_inc(S["spread"], 1)
                if i:
                    pe.wait_ge(S["ptm_ready"], i)
                q, k = z[:, Z["qm"] + i, :], z[:, Z["km"] + i, :]
                for s in range(2):
                    ins = pe.matmul(bank[5][:, s * L:(s + 1) * L], k[:, s * L:(s + 1) * L], q[:, s * L:(s + 1) * L],
                                    start=True, stop=True)
                ins.then_inc(S["keyed"], 1)
                if i:
                    pe.wait_ge(S["inter_kept"], 2 * i)
                for d in range(2):
                    ins = pe.matmul(bank[0][:, d * (P + 1):(d + 1) * (P + 1)], q[:, L:TOK], cinit[:, d, i, :],
                                    start=True, stop=True)
                ins.then_inc(S["inter_made"], 1)

            def ml_back(i):
                pe.wait_ge(S["ptm_ready"], i + 1)
                if i:
                    pe.wait_ge(S["ns_made"], 2 * i)
                for d in range(2):
                    for s in range(2):
                        ins = pe.matmul(bank[6 + d][:, s * (P + 1):(s + 1) * (P + 1)], ml["pt"][:, 2 * d + s, :],
                                        vmt[:, s, i, :], start=True, stop=True)
                ins.then_inc(S["summed"], 1)
                pe.wait_ge(S["kw_ready"], i + 1)
                if i:
                    pe.wait_ge(S["state_kept"], i)
                pe.matmul(bank[1][:, 0:2 * P], vmt[:, 0, i, 0:P], ml["kw"].rearrange("p d k -> p (d k)"),
                          start=True, stop=True)
                pe.matmul(bank[2][0:2, i * P:(i + 1) * P], sm["wsrc"][:, i, :], kmt[:, i, :], start=True, stop=True
                          ).then_inc(S["state_made"], 1)

            pe.wait_ge(S["cinit_in"], 16)
            pe.wait_ge(S["pads_made"], 2)
            pe.wait_ge(S["exp_done"], 2 * NH)
            pe.wait_ge(S["pt_kept"], NH)
            pe.wait_ge(S["att_kept"], NH // 2)
            ml_front(0)
            for i in range(MH):
                if i < MH - 1:
                    ml_front(i + 1)
                ml_back(i)
            pe.wait_ge(S["hm_ready"], 1)
            pe.wait_ge(S["decayed"], 4 * MH)
            for i in range(MH):
                for s in range(2):
                    at = (i % 2) * TOK + s * L
                    ins = pe.transpose(bank[4 + i // 2][:, at:at + L], hm[:, s, i, :], ident[:, :])
            ins.then_inc(S["hm_turned"], 1)

            pe.wait_ge(S["state_kept"], MH + 1)
            pe.wait_ge(S["ym_ready"], 1)
            pe.wait_ge(S["yc_ready"], 1)
            for n, br in enumerate(BRANCHES):
                for g in range(2):
                    if n:
                        pe.wait_ge(S["gate_sig"], 8 * (n - 1) + 4 * (g + 1))
                    product4(C_MERGE + 3 * n + g, h,
                             lambda b: bank[2 * g + b // 2][:, (b % 2) * TOK:(b % 2 + 1) * TOK])
                c = C_MERGE + 3 * n + 2
                arrived(pe, c)
                w = ring[:, c % RING, :].rearrange("p (k n) -> p k n", k=4)
                for b in range(KD):
                    if n and b % 2 == 0:
                        pe.wait_ge(S["merge_read"], 4 * (n - 1) + b // 2 + 1)
                    for k in range(4):
                        ins = pe.matmul(bank[4 + b // 2][:, (b % 2) * TOK:(b % 2 + 1) * TOK], w[:, k, b * P:(b + 1) * P],
                                        branch_out[br][:, k, :], start=k == 0, stop=k == 3)
                ins.then_inc(S["chunk_used"], 1)
            pe.wait_ge(S["merge_read"], 4 * len(BRANCHES))
            pe.wait_ge(S["gate_sig"], 8 * len(BRANCHES))
            for c in range(2):
                product4(C_OUT + c, merged, lambda b: bank[2 * c + b // 2][:, (b % 2) * TOK:(b % 2 + 1) * TOK])

            norm_sum(2, bank[4][:, 0:TOK])
            pe.wait_ge(S["h_ready"], 2)
            pe.wait_ge(S["router_in"], 32)
            for s in range(2):
                for k in range(KD):
                    pe.matmul(bank[5][:, s * NE:(s + 1) * NE], h[:, k, s * L:(s + 1) * L], wrt[:, k, :],
                              start=k == 0, stop=False)
                ins = pe.matmul(bank[5][:, s * NE:(s + 1) * NE], ones[0:1, :], rt["brt"], start=False, stop=True)
            ins.then_inc(S["logits_made"], 1)
            pe.wait_ge(S["mixed"], 1)
            for s in range(2):
                for k in range(KD):
                    ins = pe.transpose(bank[2 * s + k // 4][:, (k % 4) * P:(k % 4 + 1) * P], h[:, k, s * L:(s + 1) * L],
                                       ident[:, :])
            ins.then_inc(S["h2_turned"], 1)
            pe.wait_ge(S["picked_made"], 2)
            pe.matmul(bank[5][:, 64:64 + NE], strict[:, :], rt["picked"][:, 0, :], start=True, stop=True)
            pe.matmul(bank[5][:, 64 + NE:64 + 2 * NE], ones[:, :], rt["picked"][:, 0, :], start=True, stop=False)
            pe.matmul(bank[5][:, 64 + NE:64 + 2 * NE], strict[:, :], rt["picked"][:, 1, :], start=False, stop=True
                      ).then_inc(S["ranked"], 1)
            for s in range(2):
                ins = pe.matmul(bank[6][0:NE, 0:1], rt["picked"][:, s, :], ones[:, 0:1], start=s == 0, stop=s == 1)
            ins.then_inc(S["counted"], 1)
            pe.wait_ge(S["np_made"], 1)
            pe.matmul(bank[6][0:NE, 1:2], strict[0:NE, 0:NE], rt["np"], start=True, stop=True
                      ).then_inc(S["before_made"], 1)
            pe.wait_ge(S["past_made"], 1)
            M1 = MAX_PASS + 1
            row = bank[6][0:1, 64:64 + N_TAB]
            pe.matmul(row[:, T_EXP:T_EXP + M1], ones[0:NE, 0:1], rt["past"], start=True, stop=True)
            pe.matmul(row[:, T_BASE:T_BASE + M1], rt["np"], rt["past"], start=True, stop=True)
            pe.matmul(row[:, T_BEFORE:T_BEFORE + NE], rt["np"], strict[0:NE, 0:NE], start=True, stop=True)
            pe.matmul(row[:, T_ALL:T_ALL + 1], rt["np"], ones[0:NE, 0:1], start=True, stop=True
                      ).then_inc(S["tab_summed"], 1)
            pe.wait_ge(S["gm_made"], 2)
            for s in range(2):
                ins = pe.transpose(bank[7][0:NE, s * L:(s + 1) * L], rt["gm"][:, s, 0:NE], ident[:, :])
            ins.then_inc(S["gt_turned"], 1)
            pe.wait_ge(S["gt_kept"], 1)
            pe.wait_ge(S["bdn_in"], 16)
            pe.wait_ge(S["h2_kept"], 4)
            for q in range(4):
                pe.matmul(bank[q][:, :], mo["gt"][:, (q // 2) * L:(q // 2 + 1) * L],
                          mo["bdn"][:, (q % 2) * 512:(q % 2 + 1) * 512], start=True, stop=False,
                          skip_group_check=True)

            def gather(n):
                pe.wait_ge(S["sel_ready"], n * 2 + 2)
                for k in range(KD):
                    for s in range(2):
                        ins = pe.matmul(bank[4][:, k * SLOTS:(k + 1) * SLOTS],
                                        mo["h_tok"][:, s, k * P:(k + 1) * P], mo["sel"][:, s, :],
                                        start=s == 0, stop=s == 1)
                ins.then_inc(S["gathered"], 1)

            gather(0)
            pe.wait_ge(S["table_made"], 1)
            n_pass = table(pe, T_ALL, NE, MAX_PASS)
            with pe.Fori(0, n_pass) as n:
                e = table(pe, n + T_EXP, 0, NE - 1)
                pe.wait_ge(S["xg_ready"], n + 1)
                for j in range(GU_CHUNKS):
                    expert_arrived(pe, j, e)
                    w = ring[:, expert_slot(j), :].rearrange("p (k n) -> p k n", k=KD)
                    for b in range(4):
                        at = ((b // 2) * 4 + (j % 2) * 2 + b % 2) * SLOTS
                        for k in range(KD):
                            ins = pe.matmul(bank[5 + j // 2][:, at:at + SLOTS], w[:, k, b * P:(b + 1) * P],
                                            mo["xg"][:, k, :], start=k == 0, stop=k == KD - 1)
                    ins.then_inc(S["chunk_used"], 1)
                pe.wait_ge(S["selg_ready"], n * 2 + 2)
                gather(n + 1)
                for s in range(2):
                    ins = pe.transpose(bank[7][0:SLOTS, s * L:(s + 1) * L], mo["selg"][:, s, :], ident[:, :])
                ins.then_inc(S["selt_turned"], 1)
                pe.wait_ge(S["act_ready"], n * 2 + 2)
                pe.wait_ge(S["selt_kept"], n + 1)
                for j in range(DN_CHUNKS):
                    expert_arrived(pe, GU_CHUNKS + j, e)
                    w = ring[:, expert_slot(GU_CHUNKS + j), :].rearrange("p (k n) -> p k n", k=KD)
                    for b in range(4):
                        at = (4 * j + b) * SLOTS
                        for k in range(KD):
                            ins = pe.matmul(bank[7][:, at:at + SLOTS], w[:, k, b * P:(b + 1) * P],
                                            mo["act"][:, k, :], start=k == 0, stop=k == KD - 1)
                    ins.then_inc(S["chunk_used"], 1)
                pe.wait_ge(S["yt_kept"], n + 1)
                pe.matmul(bank[5][0:SLOTS, 0:P], mo["yt"][:, 0, :], ident[:, :], start=True, stop=True)
                for k in range(1, KD):
                    ins = pe.transpose(bank[5 + k // 4][0:SLOTS, (k % 4) * P:(k % 4 + 1) * P], mo["yt"][:, k, :],
                                       ident[:, :])
                ins.then_inc(S["y_turned"], 1)
                pe.wait_ge(S["y_kept"], n * 2 + 2)
                for q in range(4):
                    ins = pe.matmul(bank[q][:, :], mo["selt"][:, (q // 2) * L:(q // 2 + 1) * L],
                                    mo["y_tok"][:, (q % 2) * 512:(q % 2 + 1) * 512], start=False, stop=False,
                                    skip_group_check=True)
                ins.then_inc(S["scattered"], 1)

            pe.wait_ge(S["acc_kept"], 4)
            for k in range(KD):
                for s in range(2):
                    at = (k % 2) * TOK + s * L
                    ins = pe.transpose(bank[4 + k // 2][:, at:at + L], mo["h_tok"][:, s, k * P:(k + 1) * P], ident[:, :])
            ins.then_inc(S["acc_turned"], 1)
            norm_sum(3, bank[0][:, 0:TOK])


def _blocks(v):
    return v.reshape(-1, P).T


def _chunks(w, width=512):
    k, n = w.shape
    return w.reshape(k // P, P, n // width, width).transpose(2, 1, 0, 3).reshape(n // width, P, -1)


def pack(a):
    dA, dC, dM = NH * HD, 4 * P, MH * P
    sizes = [("qa", dA), ("ka", dA), ("va", dA), ("cu", dC), ("cg", dC), ("qm", dM), ("km", dM), ("vm", dM),
             ("om", dM), ("gate", 16), ("ga", D), ("gc", D), ("gm", D)]
    w_in, b_in = a["w_in"][0], a["b_in"][0]
    w, b, at = {}, {}, 0
    for name, n in sizes:
        w[name], b[name] = w_in[:, at:at + n], b_in[at:at + n]
        at += n
    trunk = [_chunks(a["w_mod"][0])] + [_chunks(w[name]) for name in PROJ]
    for br in BRANCHES:
        trunk += [_chunks(w["g" + br]), _chunks(a["w_p" + br][0], D)]
    trunk.append(_chunks(a["w_out"][0]))
    gu = a["w_gu"][0].reshape(NE, KD, P, 2, GU_CHUNKS, 2 * P).transpose(0, 4, 2, 1, 3, 5)
    gu = gu.reshape(NE, GU_CHUNKS, P, CHUNK)
    dn = a["w_down"][0].reshape(NE, KD, P, DN_CHUNKS, 512).transpose(0, 3, 2, 1, 4).reshape(NE, DN_CHUNKS, P, CHUNK)
    params = {
        "norm1": _blocks(a["norm1_g"][0]), "norm2": _blocks(a["norm2_g"][0]), "final": _blocks(a["final_g"]),
        "b_mod": _blocks(a["b_mod"][0]),
        "b_in": np.concatenate([_blocks(b[n]) for n in PROJ + ["g" + br for br in BRANCHES]], axis=1),
        "w_dw": a["w_dw"][0].T.reshape(4, P, CONV_W).transpose(1, 0, 2).reshape(P, -1),
        "b_dw": _blocks(a["b_dw"][0]), "cln_g": _blocks(a["cln_g"][0]), "cln_b": _blocks(a["cln_b"][0]),
        "mnorm": _blocks(a["mnorm_g"][0]),
        "cond": np.stack([_blocks(a["c_ctx"]), _blocks(a["c"][0])], axis=2).reshape(P, -1),
    }
    x_all = np.concatenate([a["x_prompt"][0], a["x_sample"][0]], axis=0)
    c_init = np.concatenate([a["state_C"][0, 0].transpose(3, 0, 1, 2), a["state_n"][0, 0].transpose(2, 0, 1)[..., None]],
                            axis=3)
    packed = {
        "trunk_w": np.concatenate(trunk, axis=0),
        "expert_w": np.concatenate([gu, dn], axis=1).reshape(NE * RING, P, CHUNK),
        "x_t": x_all.T.reshape(KD, P, TOK).transpose(1, 0, 2),
        "params": np.concatenate([params[n] for n, _ in PAR_WIDTHS], axis=1),
        "w_gate": w["gate"].reshape(KD, P, 16).transpose(1, 0, 2),
        "b_gate": b["gate"].reshape(4, MH).T,
        "m_init": a["state_m"][0, 0].T,
        "k_ctx_t": a["cache_k"][0, 0].reshape(L, 4, P).transpose(2, 1, 0),
        "v_ctx": a["cache_v"][0, 0].reshape(L, NH * HD),
        "c_init_t": c_init,
        "rpb": a["rpb"][0],
        "w_router": a["w_router"][0].reshape(KD, P, NE).transpose(1, 0, 2),
        "b_router": a["b_router"],
        "b_gu": a["b_gu"][0].reshape(NE, 16, P).transpose(2, 0, 1),
        "b_down": a["b_down"][0],
    }
    return {n: np.ascontiguousarray(v) for n, v in packed.items()}


_OUTS = {"y_t": (P, KD, TOK), "k_new_t": (P, 4, L), "v_new_t": (P, 4, L), "c_new": (P, MH, 2, P),
         "n_new": (2, MH * P), "m_new": (MH, 2)}


def kernel(**inputs):
    import concourse.bacc as _bacc
    from concourse.bass_utils import run_bass_kernel_spmd as _run

    arrays = pack({n: np.asarray(v) for n, v in inputs.items()})
    nc = _bacc.Bacc("TRN2", target_bir_lowering=False, num_devices=1)
    feeds, args = {}, []
    for name, v in arrays.items():
        feeds[f"in_{name}"] = v
        args.append(nc.dram_tensor(f"in_{name}", v.shape, F32, kind="ExternalInput").ap())
    for name, shape in _OUTS.items():
        args.append(nc.dram_tensor(f"out_{name}", shape, F32, kind="ExternalOutput").ap())
    hybrid_layer(nc, *args)
    r = _run(nc, [feeds], core_ids=[0]).results[0]
    got = {n: r[f"out_{n}"] for n in _OUTS}
    y = got["y_t"].transpose(1, 0, 2).reshape(D, TOK).T
    kv = [got[n].transpose(2, 1, 0).reshape(1, 1, L, NH, HD) for n in ("k_new_t", "v_new_t")]
    return (y[None, 0:L], y[None, L:TOK], kv[0], kv[1],
            got["c_new"].transpose(2, 1, 0, 3)[None, None],
            got["n_new"].reshape(1, 1, 2, MH, P), got["m_new"].T[None, None])
```

```python
from contextlib import ExitStack

import numpy as np

import concourse.bass as bass
from concourse import mybir

F32 = mybir.dt.float32
I32 = mybir.dt.int32
U32 = mybir.dt.uint32
ALU = mybir.AluOpType
ACT = mybir.ActivationFunctionType
AX = mybir.AxisListType.X

P = 128
D = 1024
KD = D // P
L = 128
TOK = 2 * L
GRID_W = 64
NH, HD = 8, 64
MH = 4
WIN_ROWS, WIN_COLS = 8, 16
RPB_ROWS, RPB_COLS = 2 * WIN_ROWS - 1, 2 * WIN_COLS - 1
CONV_W = 31
PAD = CONV_W // 2
NE, TOPK = 32, 4
SLOTS = 64
MAX_PASS = NE + TOK * TOPK // SLOTS
ALPHA, LIMIT = 1.702, 7.0
RMS_EPS, LN_EPS = 1e-6, 1e-5
ATT_SCALE = HD ** -0.5
M_SCALE = P ** -0.5
FAR = -1.0e30
LOWEST = -3.0e38

CHUNK = 4096
RING = 6
GU_CHUNKS, DN_CHUNKS = 4, 2
MOD_GROUPS, MOD_CHUNKS = 3, 4
PROJ = ["cu", "cg", "qa", "ka", "va", "qm", "km", "vm", "om"]
EARLY = 5
BRANCHES = ["c", "a", "m"]
C_PROJ = MOD_CHUNKS
C_MOD = [0, C_PROJ + len(PROJ), C_PROJ + len(PROJ) + MOD_CHUNKS]
C_MERGE = C_MOD[2] + MOD_CHUNKS
C_OUT = C_MERGE + 3 * len(BRANCHES)
N_TRUNK = C_OUT + 2
Z = {name: 4 * i for i, name in enumerate(PROJ)}
PAR_WIDTHS = [("norm1", KD), ("norm2", KD), ("final", KD), ("b_mod", 48), ("b_in", 60),
              ("w_dw", 4 * CONV_W), ("b_dw", 4), ("cln_g", 4), ("cln_b", 4), ("mnorm", MH), ("cond", 2 * KD)]
PC = {}
N_PAR = 0
for _name, _w in PAR_WIDTHS:
    PC[_name] = N_PAR
    N_PAR += _w
T_EXP, T_BASE = 0, MAX_PASS + 1
T_BEFORE = 2 * (MAX_PASS + 1)
T_ALL = T_BEFORE + NE
N_TAB = T_ALL + 1


def hybrid_layer(nc, trunk_w, w_gu, w_down, x_t, params, w_gate, b_gate, m_init, k_ctx_t, v_ctx,
                 c_init_t, rpb, w_router, b_router, b_gu, b_down,
                 y_t, k_new_t, v_new_t, c_new, n_new, m_new):
    with ExitStack() as ctx:
        def sb(name, shape, dt=F32):
            return ctx.enter_context(nc.sbuf_tensor(name, shape, dt))

        def sem(name):
            return ctx.enter_context(nc.semaphore(name))

        ring = sb("ring", [P, RING, CHUNK])
        x = sb("x", [P, KD, TOK])
        h = sb("h", [P, KD, TOK])
        par = sb("par", [P, N_PAR])
        mod = sb("mod", [P, 48, 2])
        gain = sb("gain", [P, 2, KD, 2])
        rstd = sb("rstd", [P, TOK])
        ident = sb("ident", [P, P])
        ones = sb("ones", [P, P])
        strict = sb("strict", [P, P])
        iota = sb("iota", [P, TOK])
        tab = sb("tab", [1, N_TAB], I32)
        z = sb("z", [P, 36, TOK])
        merged = sb("merged", [P, KD, TOK])
        wgate = sb("wgate", [P, KD, 16])
        bgate = sb("bgate", [MH, 4])
        minit = sb("minit", [MH, 2])
        kctx = sb("kctx", [P, 4, L])
        vctx = sb("vctx", [P, NH * HD])
        cinit = sb("cinit", [P, 2, MH, P + 1])
        abias = sb("abias", [P, NH, L])
        amask = sb("amask", [P, L])
        dmask = sb("dmask", [P, 2, 2, L])
        apad = sb("apad", [P, 4, 2, L + 2 * PAD])
        vmt = sb("vmt", [P, 2, MH, P + 1])
        kmt = sb("kmt", [P, MH, P])
        gates = sb("gates", [MH, 4, TOK])
        selrow = sb("selrow", [MH, MH, P])
        work = sb("work", [P, 2840])
        small = sb("small", [P, 192])

        bank = [ctx.enter_context(nc.psum_tensor(f"bank{i}", [P, 512], F32)) for i in range(8)]

        def carve(base, at, shape, parts=P):
            n = int(np.prod(shape))
            v = base[0:parts, at:at + n]
            if len(shape) == 2:
                v = v.rearrange("p (a b) -> p a b", a=shape[0])
            if len(shape) == 3:
                v = v.rearrange("p (a b c) -> p a b c", a=shape[0], b=shape[1])
            return v, at + n

        def carve_all(base, what):
            out, at = {}, 0
            for name, shape, *parts in what:
                out[name], at = carve(base, at, shape, *parts)
            return out

        zf = z[:, :, :].rearrange("p a b -> p (a b)")
        mf = merged[:, :, :].rearrange("p a b -> p (a b)")
        af = apad[:, :, :, :].rearrange("p a b c -> p (a b c)")

        def zblocks(name, n=4):
            return z[:, Z[name]:Z[name] + n, :]

        va_tok = zf[:, Z["cg"] * TOK:(Z["cg"] + 4) * TOK].rearrange("p (s c) -> p s c", s=2)
        acc = zblocks("cu")
        branch_out = {"c": zblocks("cu"), "a": zblocks("qa"), "m": zblocks("om")}
        rows = carve_all(mf, [("b", [2, TOK], MH), ("g", [2, TOK], MH), ("w", [2, L], MH)])
        negm = gates[:, 0:2, :]
        n_out = gates[0:2, 2:4, :].rearrange("p a b -> p (a b)")
        mirror = mf[:, 5 * TOK:5 * TOK + P]
        cond = mf[:, 6 * TOK:7 * TOK].rearrange("p (k c) -> p k c", k=KD)
        conv_sq = af[:, 0:4 * TOK].rearrange("p (a b) -> p a b", a=4)
        hm = af[:, 0:2 * MH * P].rearrange("p (s h d) -> p s h d", s=2, h=MH)
        att = carve_all(work, [("p", [2, 3 * L]), ("pt", [2, 3 * L])])
        mod_rows = work[:, 2048:2048 + 512]
        ml = carve_all(work, [("decay", [4, L]), ("pt", [4, L]), ("inter", [2, 2, P + 1]),
                              ("ns", [2, 2 * (P + 1)]), ("hd", [4, P]), ("kw", [2, P])])
        c_out = abias[:, :, :].rearrange("p (h e) k -> p h e k", h=MH)
        sm = carve_all(small, [("amax", [NH, 2]), ("aneg", [NH, 2]), ("asum", [NH, 2]), ("arec", [NH, 2]),
                               ("cols", [10, MH]), ("em", [4, MH]), ("wsrc", [MH, 2]), ("den", [4]),
                               ("hsum", [8]), ("hvar", [8]), ("mlast", [2], MH)])
        N_SIG = 2
        sig_gate = zblocks("ka", N_SIG)
        mo = carve_all(zf, [("h_tok", [2, D]), ("gath", [512]), ("xg", [4, 2, SLOTS]), ("glu", [512]), ("lin", [512]),
                            ("sig", [512]), ("act", [512]), ("actt", [4, 2, SLOTS]), ("y", [512]),
                            ("selt", [2, 2, L]), ("gt", [TOK], NE), ("sel", [2, SLOTS]),
                            ("selz", [2, 3 * SLOTS]), ("esel", [SLOTS], NE)])
        bgu = mf[0:NE, :]
        bdn = abias[0:NE, :, :].rearrange("p a b -> p (a b)")
        rt = carve_all(work, [("lg", [2, NE]), ("top", [2, 8]), ("idxf", [2, 8]), ("ex", [2, TOPK]),
                              ("neg", [2]), ("sum", [2]), ("oh", [2 * TOPK, NE]),
                              ("ohg", [2 * TOPK, NE]), ("picked", [2, NE]), ("posm", [2, NE + 1]),
                              ("gm", [2, NE + 1]), ("cmp", [3], NE), ("np", [1], NE), ("pinc", [1], NE),
                              ("past", [MAX_PASS + 1], NE), ("tabf", [N_TAB], 1), ("brt", [NE], 1)])
        wrt = cinit[:, :, :, :].rearrange("p a b c -> p (a b c)")[:, 0:KD * NE].rearrange(
            "p (k e) -> p k e", k=KD)
        idx = sb("idx", [P, 2, 8], U32)

        def pcol(name, i=0, n=1):
            return par[:, PC[name] + i:PC[name] + i + n]

        def per_stream(v):
            return v.rearrange("p k (s t) -> p (k s) t", s=2)

        def over(v, n):
            return v.unsqueeze(2).to_broadcast([v.shape[0], v.shape[1], n])

        chunk_in = [sem(f"chunk_in{i}") for i in range(RING)]
        S = {}

        def S_(names):
            for n in names.split():
                S[n] = sem(n)

        S_("chunk_used x_in par_in gatew_in mrow_in kctx_in vctx_in cinit_in rpb_in bgu_in router_in bdn_in")
        S_("ones_made consts_made pads_made squared ssq var root cond_sig cond_ready mod_summed mod_kept mod_turned "
           "mod_made h_ready bias_turned bias_ready")
        S_("block_made proj_kept gates_summed gates_kept cg_sig glu_done f_abs f_exp f_log rows_ready w_ready "
           "km_scaled cols_turned cols_kept em_ready conv_step conv_sum conv_sq conv_sqsum conv_var conv_root "
           "conv_lin conv_sig yc_ready va_turned va_kept v_turned v_kept")
        S_("scored exp_in exp_done probs_ready probs_turned pt_kept attended att_kept")
        S_("spread decayed keyed ptm_ready summed inter_made inter_kept kw_ready state_made state_kept ns_made "
           "hm_var hm_root hm_ready hm_turned om_sig ym_ready")
        S_("merge_made gate_sig merge_read mixed h2_turned h2_kept logits_made top_made top_exp picked_made gm_made "
           "ranked counted np_made before_made past_made tab_summed table_made gt_turned gt_kept")
        S_("sel_ready esel_ready selg_ready biased gathered gath_kept xg_turned xg_ready glu_ready sig_ready act_ready "
           "act_turned actt_kept selt_turned selt_kept y_kept scattered acc_kept acc_turned y_ready")
        S_("dve_step act_step pool_step dve_pass kv_stored state_stored y_stored")

        def linker(eng, name):
            n = [0]

            def link(ins):
                n[0] += 1
                ins.then_inc(S[name], 1)
                eng.wait_ge(S[name], n[0])
            return link

        def arrived(eng, c):
            eng.wait_ge(chunk_in[c % RING], 16 * (c // RING + 1))

        def expert_slot(j):
            return (N_TRUNK + j) % RING

        def expert_arrived(eng, j, e):
            before = len([c for c in range(N_TRUNK) if c % RING == expert_slot(j)])
            eng.wait_ge(chunk_in[expert_slot(j)], e * 16 + 16 * (before + 1))

        def late_bank(t):
            return bank[2 + t % 2][:, 0:TOK]

        def merge_bank(u):
            return bank[1 + u % N_SIG]

        def table(eng, at, lo, hi):
            return eng.value_load(tab[0:1, bass.ds(at, 1)], min_val=lo, max_val=hi)

        block = ctx.enter_context(nc.Block())

        @block.sync
        def _(sp):
            for c in range(RING):
                sp.dma_start(ring[:, c, :], trunk_w[c]).then_inc(chunk_in[c], 16)
            rounds = N_TRUNK // RING
            with sp.Fori(1, rounds) as r:
                for s in range(RING):
                    sp.wait_ge(S["chunk_used"], r * RING + (s + 1 - RING))
                    sp.dma_start(ring[:, s, :], trunk_w[bass.ds(r * RING + s, 1)].rearrange(
                        "o p n -> (o p) n")).then_inc(chunk_in[s], 16)
            for c in range(rounds * RING, N_TRUNK):
                sp.wait_ge(S["chunk_used"], c - RING + 1)
                sp.dma_start(ring[:, c % RING, :], trunk_w[c]).then_inc(chunk_in[c % RING], 16)
            def expert_chunk(e, j):
                if j < GU_CHUNKS:
                    w, n = w_gu, KD // GU_CHUNKS
                else:
                    w, n, j = w_down, KD // DN_CHUNKS, j - GU_CHUNKS
                return w[bass.ds(e, 1), bass.ds(j * n * P, n * P), :].rearrange("o (k p) n -> p (o k) n", p=P)

            def slot(j):
                n = KD // GU_CHUNKS if j < GU_CHUNKS else KD // DN_CHUNKS
                return ring[:, expert_slot(j), :].rearrange("p (k n) -> p k n", k=n)

            for j in range(RING):
                sp.wait_ge(S["chunk_used"], N_TRUNK - RING + j + 1)
                sp.dma_start(slot(j), expert_chunk(0, j)).then_inc(chunk_in[expert_slot(j)], 16)
            sp.wait_ge(S["table_made"], 1)
            with sp.Fori(1, NE) as e:
                before = table(sp, e + T_BEFORE, 1, MAX_PASS)
                for j in range(RING):
                    sp.wait_ge(S["chunk_used"], before * RING + (N_TRUNK - RING + j + 1))
                    sp.dma_start(slot(j), expert_chunk(e, j)).then_inc(chunk_in[expert_slot(j)], 16)

        @block.gpsimd
        def _(pool):
            link = linker(pool, "pool_step")
            link(pool.memset(ident[:, :], 0.0))
            link(pool.affine_select(out=ident[:, :], in_=ident[:, :], compare_op=ALU.not_equal, fill=1.0,
                                    base=0, pattern=[[-1, P]], channel_multiplier=1))
            link(pool.memset(mirror[:, :], 0.0))
            for r in range(2):
                link(pool.affine_select(out=mirror[:, :], in_=mirror[:, :], compare_op=ALU.not_equal, fill=1.0,
                                        base=-(2 * r * GRID_W + GRID_W - 1), pattern=[[1, P]], channel_multiplier=1))
            link(pool.memset(strict[:, :], 1.0))
            link(pool.affine_select(out=strict[:, :], in_=strict[:, :], compare_op=ALU.is_gt, fill=0.0,
                                    base=0, pattern=[[1, P]], channel_multiplier=-1))
            link(pool.memset(selrow[:, :, :], 0.0))
            link(pool.affine_select(out=selrow[:, :, :], in_=selrow[:, :, :], compare_op=ALU.not_equal, fill=1.0,
                                    base=0, pattern=[[-1, MH], [0, P]], channel_multiplier=1))
            link(pool.memset(dmask[:, :, :, :], 0.0))
            for d, sign in ((0, 1), (1, -1)):
                link(pool.affine_select(out=dmask[:, d, :, :], in_=dmask[:, d, :, :], compare_op=ALU.is_ge,
                                        fill=FAR, base=0, pattern=[[0, 2], [sign, L]], channel_multiplier=-sign))
            link(pool.memset(amask[:, :], 0.0))
            half = WIN_COLS // 2
            for r in range(2):
                m = amask[r * GRID_W:(r + 1) * GRID_W, :].rearrange("p (r c) -> p r c", r=2)
                low, high = m[:, :, 0:GRID_W - WIN_COLS], m[:, :, WIN_COLS:GRID_W]
                link(pool.affine_select(out=low, in_=low, compare_op=ALU.is_ge, fill=FAR, base=half,
                                        pattern=[[0, 2], [1, GRID_W - WIN_COLS]], channel_multiplier=-1))
                link(pool.affine_select(out=high, in_=high, compare_op=ALU.is_ge, fill=FAR,
                                        base=half - 1 - WIN_COLS,
                                        pattern=[[0, 2], [-1, GRID_W - WIN_COLS]], channel_multiplier=1))
            pool.iota(iota[:, :], pattern=[[1, TOK]], base=0, channel_multiplier=0,
                      allow_small_or_imprecise_dtypes=True).then_inc(S["consts_made"], 1)

        @block.scalar
        def _(act):
            link = linker(act, "act_step")

            def func(out, in_, f, **kw):
                return act.activation(out, in_, f, **kw)

            act.dma_start(x[:, :, :], x_t).then_inc(S["x_in"], 16)
            act.dma_start(par[:, :], params).then_inc(S["par_in"], 16)
            act.dma_start(wgate[:, :, :], w_gate).then_inc(S["gatew_in"], 16)
            act.dma_start(bgate[:, :], b_gate).then_inc(S["mrow_in"], 16)
            act.dma_start(minit[:, :], m_init).then_inc(S["mrow_in"], 16)
            for r in range(2):
                for rk in range(2):
                    at = (rk - r + WIN_ROWS - 1) * RPB_COLS + WIN_COLS - 1 - (GRID_W - 1)
                    act.dma_start(abias[r * GRID_W:(r + 1) * GRID_W, :, rk * GRID_W:(rk + 1) * GRID_W],
                                  bass.AP(rpb.tensor, at, [[1, GRID_W], [RPB_ROWS * RPB_COLS, NH], [1, GRID_W]])
                                  ).then_inc(S["rpb_in"], 16)
            act.dma_start(kctx[:, :, :], k_ctx_t).then_inc(S["kctx_in"], 16)
            act.dma_start(vctx[:, :], v_ctx).then_inc(S["vctx_in"], 16)
            act.dma_start(cinit[:, :, :, :], c_init_t).then_inc(S["cinit_in"], 16)

            def norm_root(n):
                act.wait_ge(S["var"], n)
                func(rstd[:, :], rstd[:, :], ACT.Sqrt).then_inc(S["root"], 1)

            act.wait_ge(S["x_in"], 16)
            func(h[:, :, :], x[:, :, :], ACT.Square).then_inc(S["squared"], 1)
            act.wait_ge(S["par_in"], 16)
            act.wait_ge(S["pads_made"], 3)
            cond_in = pcol("cond", 0, 2 * KD).rearrange("p (k s) -> p k s", k=KD)
            func(cond[:, :, 0:2], cond_in, ACT.Sigmoid).then_inc(S["cond_sig"], 1)
            norm_root(1)

            def keep_mod(g):
                act.wait_ge(S["chunk_used"], C_MOD[g] + MOD_CHUNKS)
                func(mod_rows, bank[5][:, :], ACT.Copy).then_inc(S["mod_kept"], 1)

            keep_mod(0)

            def keep_proj(i):
                act.wait_ge(S["chunk_used"], C_PROJ + i + 1)
                for b in range(4):
                    func(z[:, 4 * i + b, :], bank[2 * (i % 2) + b // 2][:, (b % 2) * TOK:(b % 2 + 1) * TOK],
                         ACT.Identity, bias=pcol("b_in", 4 * i + b)).then_inc(S["proj_kept"], 1)

            keep_proj(0)
            keep_proj(1)
            act.wait_ge(S["proj_kept"], 8)
            func(zblocks("cg"), zblocks("cg"), ACT.Sigmoid).then_inc(S["cg_sig"], 1)
            act.wait_ge(S["gates_summed"], 1)
            act.wait_ge(S["mrow_in"], 32)
            for q in range(4):
                func(gates[:, q, :], bank[6 + q // 2][0:MH, (q % 2) * TOK:(q % 2 + 1) * TOK], ACT.Identity,
                     bias=bgate[:, q:q + 1]).then_inc(S["gates_kept"], 1)
            act.wait_ge(S["f_abs"], 1)
            func(rows["g"], rows["g"], ACT.Exp, scale=-1.0).then_inc(S["f_exp"], 1)
            act.wait_ge(S["f_exp"], 1)
            func(rows["g"], rows["g"], ACT.Ln, bias=1.0).then_inc(S["f_log"], 1)
            act.wait_ge(S["rows_ready"], 1)
            for d in range(2):
                func(rows["w"][:, d, :], negm[:, d, L:TOK], ACT.Exp, bias=minit[:, d:d + 1]
                     ).then_inc(S["w_ready"], 1)
            for i in range(2, EARLY):
                keep_proj(i)
            act.wait_ge(S["proj_kept"], 4 * EARLY)
            act.dma_start(k_new_t, z[:, Z["ka"]:Z["ka"] + 4, 0:L]).then_inc(S["kv_stored"], 16)
            act.dma_start(v_new_t, z[:, Z["va"]:Z["va"] + 4, 0:L]).then_inc(S["kv_stored"], 16)
            act.wait_ge(S["va_turned"], 1)
            act.wait_ge(S["glu_done"], 1)
            for s in range(2):
                func(va_tok[:, s, :], bank[6 + s][:, :], ACT.Copy).then_inc(S["va_kept"], 1)

            def late_block(t):
                if t % 4 == 3:
                    act.wait_ge(S["chunk_used"], C_PROJ + EARLY + t // 4 + 1)
                else:
                    act.wait_ge(S["block_made"], 3 * (t // 4) + t % 4 + 1)
                func(z[:, 4 * EARLY + t, :], late_bank(t), ACT.Identity, bias=pcol("b_in", 4 * EARLY + t)
                     ).then_inc(S["proj_kept"], 1)

            for i in range(NH):
                act.wait_ge(S["exp_in"], i + 1)
                if i >= 2:
                    act.wait_ge(S["probs_turned"], i - 1)
                b = bank[4 + i % 2]
                func(att["p"][:, i % 2, 0:L], b[:, 0:L], ACT.Exp, scale=ATT_SCALE, bias=sm["aneg"][:, i, 0:1],
                     accum_out=sm["asum"][:, i, 0:1]).then_inc(S["exp_done"], 1)
                func(att["p"][:, i % 2, L:3 * L], b[:, L:3 * L], ACT.Exp, scale=ATT_SCALE,
                     bias=sm["aneg"][:, i, 1:2], accum_out=sm["asum"][:, i, 1:2]).then_inc(S["exp_done"], 1)
                late_block(2 * i)
                late_block(2 * i + 1)
            act.wait_ge(S["proj_kept"], 4 * len(PROJ))
            func(zblocks("km"), zblocks("km"), ACT.Copy, scale=M_SCALE).then_inc(S["km_scaled"], 1)
            func(zblocks("om"), zblocks("om"), ACT.Sigmoid).then_inc(S["om_sig"], 1)

            act.wait_ge(S["v_turned"], 1)
            for s in range(2):
                func(vmt[:, s, :, 0:P], bank[2 + s][:, :].rearrange("p (a b) -> p a b", a=MH), ACT.Copy
                     ).then_inc(S["v_kept"], 1)
            keep_mod(1)
            act.wait_ge(S["v_turned"], 2)
            func(kmt[:, :, :], bank[7][:, :].rearrange("p (a b) -> p a b", a=MH), ACT.Copy
                 ).then_inc(S["v_kept"], 1)
            act.wait_ge(S["conv_var"], 1)
            func(rstd[:, :], rstd[:, :], ACT.Sqrt).then_inc(S["conv_root"], 1)
            act.wait_ge(S["mod_turned"], 2)
            keep_mod(2)
            act.wait_ge(S["cols_turned"], 1)
            func(sm["cols"], bank[6][:, 0:40].rearrange("p (a b) -> p a b", a=10), ACT.Copy
                 ).then_inc(S["cols_kept"], 1)
            act.wait_ge(S["conv_lin"], 1)
            func(conv_sq, acc, ACT.Sigmoid).then_inc(S["conv_sig"], 1)
            act.wait_ge(S["cols_kept"], 1)
            func(sm["em"], sm["cols"][:, 4:8, :], ACT.Exp, scale=-1.0).then_inc(S["em_ready"], 1)

            def merge_gate(u):
                if u % 8 == 7:
                    act.wait_ge(S["chunk_used"], C_MERGE + 3 * (u // 8 + 1))
                else:
                    act.wait_ge(S["merge_made"], 7 * (u // 8) + u % 8 + 1)
                if u >= N_SIG:
                    act.wait_ge(S["merge_read"], u - N_SIG + 1)
                func(sig_gate[:, u % N_SIG, :], merge_bank(u)[:, 0:TOK], ACT.Sigmoid, bias=pcol("b_in", 36 + u)
                     ).then_inc(S["gate_sig"], 1)

            act.wait_ge(S["kv_stored"], 32)
            act.wait_ge(S["att_kept"], NH // 2)
            act.wait_ge(S["mod_turned"], 3)
            for i in range(MH):
                act.wait_ge(S["spread"], i + 1)
                if i:
                    act.wait_ge(S["kw_ready"], i)
                for q in range(4):
                    func(ml["decay"][:, q, :], bank[4][:, q * L:(q + 1) * L], ACT.Exp,
                         bias=sm["cols"][:, q, i:i + 1]).then_inc(S["decayed"], 1)
                act.wait_ge(S["inter_made"], i + 1)
                if i:
                    act.wait_ge(S["ns_made"], 2 * i)
                for d in range(2):
                    func(ml["inter"][:, d, 1, :], bank[0][:, d * (P + 1):(d + 1) * (P + 1)], ACT.Copy,
                         scale=sm["cols"][:, 8 + d, i:i + 1]).then_inc(S["inter_kept"], 1)
                merge_gate(2 * i)
                act.wait_ge(S["state_made"], i + 1)
                func(c_out[:, i, :, :], bank[3][:, 0:2 * P].rearrange("p (a b) -> p a b", a=2), ACT.Copy
                     ).then_inc(S["state_kept"], 1)
                func(n_out[:, i * P:(i + 1) * P], bank[3][0:2, TOK:TOK + P], ACT.Copy).then_inc(S["state_kept"], 1)
                merge_gate(2 * i + 1)
            act.wait_ge(S["state_kept"], 2 * MH)
            act.dma_start(c_new, c_out).then_inc(S["state_stored"], 16)
            act.dma_start(n_new, n_out).then_inc(S["state_stored"], 16)
            act.dma_start(m_new, sm["mlast"]).then_inc(S["state_stored"], 16)
            act.wait_ge(S["hm_var"], 1)
            func(sm["hvar"], sm["hvar"], ACT.Sqrt).then_inc(S["hm_root"], 1)

            for u in range(8, 24):
                merge_gate(u)

            act.wait_ge(S["mixed"], 1)
            act.dma_start(wrt, w_router).then_inc(S["router_in"], 16)
            act.dma_start(rt["brt"], b_router).then_inc(S["router_in"], 16)
            act.wait_ge(S["state_stored"], 48)
            act.dma_start(bdn, b_down).then_inc(S["bdn_in"], 16)
            act.dma_start(bgu, b_gu).then_inc(S["bgu_in"], 16)
            func(h[:, :, :], x[:, :, :], ACT.Square).then_inc(S["squared"], 1)
            norm_root(2)
            act.wait_ge(S["h2_turned"], 1)
            for q in range(4):
                func(mo["h_tok"][:, q // 2, (q % 2) * 512:(q % 2 + 1) * 512], bank[q][:, :], ACT.Copy
                     ).then_inc(S["h2_kept"], 1)
            act.wait_ge(S["top_made"], 1)
            for s in range(2):
                func(rt["ex"][:, s, :], rt["top"][:, s, 0:TOPK], ACT.Exp, bias=rt["neg"][:, s:s + 1],
                     accum_out=rt["sum"][:, s:s + 1]).then_inc(S["top_exp"], 1)

            def keep(out, in_, name):
                func(out, in_, ACT.Copy).then_inc(S[name], 1)

            def by_half(b):
                return bank[b][:, :].rearrange("p (j h c) -> p j h c", j=4, h=2)

            act.wait_ge(S["gathered"], 1)
            keep(mo["gath"], bank[4][:, :], "gath_kept")
            act.wait_ge(S["xg_turned"], 1)
            keep(mo["xg"], by_half(6), "xg_ready")
            act.wait_ge(S["table_made"], 1)
            n_pass = table(act, T_ALL, NE, MAX_PASS)
            with act.Fori(0, n_pass) as n:
                act.wait_ge(S["glu_ready"], n + 1)
                func(mo["sig"], mo["glu"], ACT.Sigmoid, scale=ALPHA).then_inc(S["sig_ready"], 1)
                act.wait_ge(S["gathered"], n + 2)
                keep(mo["gath"], bank[4][:, :], "gath_kept")
                act.wait_ge(S["selt_turned"], n + 1)
                keep(mo["selt"], bank[7][:, :].rearrange("p (s h t) -> p s h t", s=2, h=2), "selt_kept")
                act.wait_ge(S["act_turned"], n + 1)
                keep(mo["actt"], by_half(5), "actt_kept")
                act.wait_ge(S["xg_turned"], n + 2)
                keep(mo["xg"], by_half(6), "xg_ready")
                act.wait_ge(S["chunk_used"], n * RING + (N_TRUNK + RING))
                keep(mo["y"], bank[7][:, :], "y_kept")

            act.wait_ge(S["scattered"], n_pass + 1)
            for q in range(4):
                func(mo["h_tok"][:, q // 2, (q % 2) * 512:(q % 2 + 1) * 512], bank[q][:, :], ACT.Copy
                     ).then_inc(S["acc_kept"], 1)
            act.wait_ge(S["mixed"], 2)
            func(h[:, :, :], x[:, :, :], ACT.Square).then_inc(S["squared"], 1)
            norm_root(3)
            act.wait_ge(S["y_ready"], 1)
            act.dma_start(y_t, x[:, :, :]).then_inc(S["y_stored"], 16)
            act.wait_ge(S["y_stored"], 16)
            act.wait_ge(S["kv_stored"], 32)
            act.wait_ge(S["state_stored"], 48)

        @block.vector
        def _(dve):
            link = linker(dve, "dve_step")

            def rstd_from(src, count, eps, ready, root, n):
                dve.tensor_scalar(rstd[:, :], src, 1.0 / count, eps, ALU.mult, ALU.add).then_inc(S[ready], 1)
                dve.wait_ge(S[root], n)
                link(dve.reciprocal(rstd[:, :], rstd[:, :]))

            def mod_group(g):
                dve.wait_ge(S["mod_turned"], g + 1)
                made = bank[0][:, :].rearrange("p (j q c) -> p j q c", j=4, q=4)[:, :, :, 0:2]
                to = mod[:, 16 * g:16 * g + 16, :].rearrange("p (q j) s -> p j q s", q=4)
                bias = pcol("b_mod", 16 * g, 16).rearrange("p (q j) -> p j q", q=4)
                for j in range(4):
                    ins = dve.tensor_tensor(to[:, j, :, :], made[:, j, :, :], over(bias[:, j, :], 2), ALU.add)
                    ins.then_inc(S["mod_made"], 1)
                dve.wait_ge(S["mod_made"], 4 * g + 4)
                if g != 1:
                    i = g // 2
                    link(dve.scalar_tensor_tensor(gain[:, i, :, :], mod[:, 24 * i + 8:24 * i + 16, :], 1.0,
                                                  over(pcol(("norm1", "norm2")[i], 0, KD), 2), ALU.add, ALU.mult))

            def modulated(which, n):
                dve.wait_ge(S["ssq"], n)
                rstd_from(bank[4][:, 0:TOK], D, RMS_EPS, "var", "root", n)
                link(dve.tensor_tensor(h[:, :, :], x[:, :, :],
                                       rstd[:, :].unsqueeze(1).to_broadcast([P, KD, TOK]), ALU.mult))
                if which == 0:
                    mod_group(0)
                g = gain[:, which, :, :].rearrange("p k s -> p (k s)")
                sh = mod[:, 24 * which:24 * which + KD, :].rearrange("p k s -> p (k s)")
                hs = per_stream(h[:, :, :])
                link(dve.tensor_tensor(hs, hs, over(g, L), ALU.mult))
                dve.tensor_tensor(hs, hs, over(sh, L), ALU.add).then_inc(S["h_ready"], 1)

            dve.memset(ones[:, :], 1.0).then_inc(S["ones_made"], 1)
            dve.memset(apad[:, :, :, :], 0.0).then_inc(S["pads_made"], 1)
            dve.memset(vmt[:, :, :, P:P + 1], 1.0).then_inc(S["pads_made"], 1)
            dve.memset(cond, 0.0).then_inc(S["pads_made"], 1)
            dve.wait_ge(S["cond_sig"], 1)
            dve.tensor_tensor(cond[:, :, 0:2], cond[:, :, 0:2],
                              pcol("cond", 0, 2 * KD).rearrange("p (k s) -> p k s", k=KD), ALU.mult
                              ).then_inc(S["cond_ready"], 1)
            dve.wait_ge(S["bias_turned"], 1)
            for q in range(2):
                dve.scalar_tensor_tensor(abias[:, 4 * q:4 * q + 4, :],
                                         bank[6 + q][:, :].rearrange("p (a b) -> p a b", a=4), 1.0 / ATT_SCALE,
                                         amask[:, :].unsqueeze(1).to_broadcast([P, 4, L]), ALU.mult, ALU.add
                                         ).then_inc(S["bias_ready"], 1)
            modulated(0, 1)

            dve.wait_ge(S["cg_sig"], 1)
            dve.wait_ge(S["pads_made"], 1)
            dve.tensor_tensor(apad[:, :, :, PAD:PAD + L], zblocks("cu").rearrange("p k (s t) -> p k s t", s=2),
                              zblocks("cg").rearrange("p k (s t) -> p k s t", s=2), ALU.mult
                              ).then_inc(S["glu_done"], 1)

            dve.wait_ge(S["gates_kept"], 4)
            dve.scalar_tensor_tensor(rows["g"], gates[:, 1:4:2, :], -1.0, gates[:, 1:4:2, :], ALU.mult, ALU.max
                                     ).then_inc(S["f_abs"], 1)
            dve.wait_ge(S["f_log"], 1)
            link(dve.scalar_tensor_tensor(rows["g"], gates[:, 1:4:2, :], 0.0, rows["g"], ALU.min, ALU.subtract))

            def along(v, d, s):
                v = v[:, d, s * L:(s + 1) * L]
                return v if d == 0 else v[:, ::-1]

            dve.wait_ge(S["ones_made"], 1)
            for d in range(2):
                for s in range(2):
                    link(dve.tensor_tensor_scan(along(rows["b"], d, s), ones[0:MH, :], along(rows["g"], d, s), 0.0,
                                                ALU.mult, ALU.add))
            link(dve.tensor_tensor(rows["g"], gates[:, 0:4:2, :], rows["b"], ALU.subtract))
            for d in range(2):
                for s in range(2):
                    g = along(rows["g"], d, s)
                    link(dve.tensor_tensor_scan(along(negm, d, s), g, g,
                                                minit[:, d:d + 1] if s else LOWEST, ALU.max, ALU.max))
            link(dve.tensor_tensor(rows["b"], rows["b"], negm, ALU.add))
            dve.tensor_scalar(negm, negm, -1.0, None, ALU.mult).then_inc(S["rows_ready"], 1)
            link(dve.tensor_copy(sm["mlast"][:, 0:1], rows["b"][:, 0, L - 1:L]))
            link(dve.tensor_copy(sm["mlast"][:, 1:2], rows["b"][:, 1, 0:1]))

            dve.wait_ge(S["glu_done"], 1)

            def conv_in(b, w):
                return apad[:, b, :, bass.ds(w, L)]

            accs = [acc[:, b, :].rearrange("p (s t) -> p s t", s=2) for b in range(4)]
            for b in range(4):
                dve.tensor_scalar(accs[b], conv_in(b, 0), pcol("w_dw", b * CONV_W), pcol("b_dw", b),
                                  ALU.mult, ALU.add).then_inc(S["conv_step"], 1)
            with dve.Fori(1, CONV_W) as w:
                for b in range(4):
                    dve.wait_ge(S["conv_step"], w * 4 + (b + 1 - 4))
                    tap = par[:, bass.ds(w + (PC["w_dw"] + b * CONV_W), 1)]
                    dve.scalar_tensor_tensor(accs[b], conv_in(b, w), tap, accs[b], ALU.mult, ALU.add
                                             ).then_inc(S["conv_step"], 1)
            def att_front(i):
                dve.wait_ge(S["scored"], i + 1)
                b = bank[4 + i % 2]
                link(dve.tensor_tensor(b[:, L:2 * L], b[:, L:2 * L], abias[:, i, :], ALU.add))
                dve.tensor_reduce(sm["amax"][:, i, 0:1], b[:, 0:L], AX, ALU.max)
                link(dve.tensor_reduce(sm["amax"][:, i, 1:2], b[:, L:3 * L], AX, ALU.max))
                dve.tensor_scalar(sm["aneg"][:, i, :], sm["amax"][:, i, :], -ATT_SCALE, None, ALU.mult
                                  ).then_inc(S["exp_in"], 1)

            def att_back(i):
                dve.wait_ge(S["exp_done"], 2 * i + 2)
                link(dve.reciprocal(sm["arec"][:, i, :], sm["asum"][:, i, :]))
                p = att["p"][:, i % 2, :]
                link(dve.tensor_scalar(p[:, 0:L], p[:, 0:L], sm["arec"][:, i, 0:1], None, ALU.mult))
                dve.tensor_scalar(p[:, L:3 * L], p[:, L:3 * L], sm["arec"][:, i, 1:2], None, ALU.mult
                                  ).then_inc(S["probs_ready"], 1)
                dve.wait_ge(S["probs_turned"], i + 1)
                if i >= 2:
                    dve.wait_ge(S["attended"], i - 1)
                dve.tensor_copy(att["pt"][:, i % 2, :], bank[6 + i % 2][:, 0:3 * L]).then_inc(S["pt_kept"], 1)
                if i % 2:
                    dve.wait_ge(S["attended"], i + 1)
                    dve.tensor_copy(branch_out["a"][:, i // 2, :], bank[(i // 2) % 2][:, 0:TOK]
                                    ).then_inc(S["att_kept"], 1)

            dve.wait_ge(S["bias_ready"], 2)
            for i in range(NH + 1):
                if i < NH:
                    att_front(i)
                if i:
                    att_back(i - 1)

            dve.wait_ge(S["conv_sum"], 1)
            link(dve.tensor_scalar(rstd[:, :], bank[4][:, 0:TOK], -1.0 / (4 * P), None, ALU.mult))
            link(dve.tensor_tensor(acc, acc, rstd[:, :].unsqueeze(1).to_broadcast([P, 4, TOK]), ALU.add))
            dve.tensor_tensor(conv_sq, acc, acc, ALU.mult).then_inc(S["conv_sq"], 1)
            dve.wait_ge(S["conv_sqsum"], 1)
            rstd_from(bank[4][:, TOK:2 * TOK], 4 * P, LN_EPS, "conv_var", "conv_root", 1)
            link(dve.tensor_tensor(acc, acc, rstd[:, :].unsqueeze(1).to_broadcast([P, 4, TOK]), ALU.mult))
            for b in range(4):
                dve.tensor_scalar(acc[:, b, :], acc[:, b, :], pcol("cln_g", b), pcol("cln_b", b),
                                  ALU.mult, ALU.add).then_inc(S["conv_lin"] if b == 3 else S["conv_step"], 1)
            dve.wait_ge(S["conv_sig"], 1)
            dve.tensor_tensor(acc, acc, conv_sq, ALU.mult).then_inc(S["yc_ready"], 1)
            mod_group(1)
            mod_group(2)

            def merge(u):
                b = u % 8
                dve.wait_ge(S["gate_sig"], u + 1)
                sg, pr = sig_gate[:, u % N_SIG, :], merge_bank(u)[:, TOK:2 * TOK]
                if u < 8:
                    dve.tensor_tensor(merged[:, b, :], sg, pr, ALU.mult).then_inc(S["merge_read"], 1)
                else:
                    link(dve.tensor_tensor(sg, sg, pr, ALU.mult))
                    dve.tensor_tensor(merged[:, b, :], merged[:, b, :], sg, ALU.add).then_inc(S["merge_read"], 1)

            km_tok = kmt[:, :, :]
            dve.wait_ge(S["mod_turned"], 3)
            dve.memset(ml["inter"][:, :, 0, :], 0.0).then_inc(S["pads_made"], 1)
            dve.wait_ge(S["em_ready"], 1)
            dve.wait_ge(S["v_kept"], 3)
            for i in range(MH):
                dve.wait_ge(S["decayed"], 4 * i + 4)
                dve.wait_ge(S["keyed"], i + 1)
                if i:
                    dve.wait_ge(S["summed"], i)
                keys = bank[5][:, 0:TOK].unsqueeze(1).to_broadcast([P, 2, TOK])
                dve.tensor_tensor(ml["pt"].rearrange("p (d s) t -> p d (s t)", d=2), keys,
                                  ml["decay"].rearrange("p (d s) t -> p d (s t)", d=2), ALU.mult
                                  ).then_inc(S["ptm_ready"], 1)
                link(dve.tensor_copy(sm["wsrc"][:, i, 0:1], ml["decay"][:, 0, L - 1:L]))
                link(dve.tensor_copy(sm["wsrc"][:, i, 1:2], ml["decay"][:, 2, 0:1]))
                if i:
                    dve.wait_ge(S["state_made"], i)
                link(dve.tensor_scalar(ml["kw"][:, 0, :], km_tok[:, i, :], sm["wsrc"][:, i, 0:1], None, ALU.mult))
                dve.tensor_scalar(ml["kw"][:, 1, :], km_tok[:, i, :], sm["wsrc"][:, i, 1:2], None, ALU.mult
                                  ).then_inc(S["kw_ready"], 1)
                merge(2 * i)
                dve.wait_ge(S["summed"], i + 1)
                dve.wait_ge(S["inter_kept"], 2 * i + 2)
                for d in range(2):
                    dve.tensor_tensor(ml["ns"][:, d, :], bank[6 + d][:, 0:2 * (P + 1)],
                                      ml["inter"][:, d, :, :].rearrange("p s c -> p (s c)"), ALU.add
                                      ).then_inc(S["ns_made"], 1)
                dve.wait_ge(S["ns_made"], 2 * i + 2)
                ns = ml["ns"].rearrange("p d (s c) -> p (d s) c", s=2)
                den = ns[:, :, P:P + 1].rearrange("p a b -> p (a b)")
                link(dve.scalar_tensor_tensor(sm["den"], den, -1.0, den, ALU.mult, ALU.max))
                link(dve.tensor_tensor(sm["den"], sm["den"], sm["em"][:, :, i:i + 1].rearrange("p a b -> p (a b)"),
                                       ALU.max))
                link(dve.reciprocal(sm["den"], sm["den"]))
                link(dve.tensor_tensor(ml["hd"], ns[:, :, 0:P], over(sm["den"], P), ALU.mult))
                link(dve.tensor_tensor(hm[:, :, i, :], ml["hd"][:, 0:2, :], ml["hd"][:, 2:4, :], ALU.add))
                merge(2 * i + 1)
            hv = hm.rearrange("p s h d -> p (s h) d")
            sq = work[:, 0:2 * MH * P].rearrange("p (a d) -> p a d", a=2 * MH)
            link(dve.tensor_reduce(sm["hsum"], hv, AX, ALU.add))
            link(dve.tensor_scalar(sm["hsum"], sm["hsum"], -1.0 / P, None, ALU.mult))
            link(dve.tensor_tensor(hv, hv, over(sm["hsum"], P), ALU.add))
            link(dve.tensor_tensor(sq, hv, hv, ALU.mult))
            link(dve.tensor_reduce(sm["hvar"], sq, AX, ALU.add))
            dve.tensor_scalar(sm["hvar"], sm["hvar"], 1.0 / P, LN_EPS, ALU.mult, ALU.add).then_inc(S["hm_var"], 1)
            dve.wait_ge(S["hm_root"], 1)
            link(dve.reciprocal(sm["hvar"], sm["hvar"]))
            dve.tensor_tensor(hv, hv, over(sm["hvar"], P), ALU.mult).then_inc(S["hm_ready"], 1)
            for u in range(8, 12):
                merge(u)
            dve.wait_ge(S["hm_turned"], 1)
            dve.wait_ge(S["om_sig"], 1)
            for i in range(MH):
                om = branch_out["m"][:, i, :]
                ins = dve.scalar_tensor_tensor(om, bank[4 + i // 2][:, (i % 2) * TOK:(i % 2 + 1) * TOK],
                                               pcol("mnorm", i), om, ALU.mult, ALU.mult)
            ins.then_inc(S["ym_ready"], 1)

            for u in range(12, 24):
                merge(u)

            def add_gated(src, part, n):
                for k in range(KD):
                    for s in range(2):
                        ins = dve.scalar_tensor_tensor(x[:, k, s * L:(s + 1) * L], src(k, s), mod[:, part + k, s:s + 1],
                                                       x[:, k, s * L:(s + 1) * L], ALU.mult, ALU.add)
                ins.then_inc(S["mixed"], 1)

            dve.wait_ge(S["chunk_used"], N_TRUNK)
            add_gated(lambda k, s: bank[4 + k // 2][:, (k % 2) * TOK + s * L:(k % 2) * TOK + (s + 1) * L], 16, 1)
            modulated(1, 2)

            dve.wait_ge(S["logits_made"], 1)
            link(dve.tensor_copy(rt["lg"], bank[5][:, 0:2 * NE].rearrange("p (a b) -> p a b", a=2)))
            for s in range(2):
                link(dve.max(rt["top"][:, s, :], rt["lg"][:, s, :]))
                link(dve.max_index(idx[:, s, :], rt["top"][:, s, :], rt["lg"][:, s, :]))
            dve.tensor_scalar(rt["neg"], rt["top"][:, :, 0:1].rearrange("p a b -> p (a b)"), -1.0, None, ALU.mult
                              ).then_inc(S["top_made"], 1)
            link(dve.tensor_copy(rt["idxf"], idx[:, :, :]))
            for s in range(2):
                oh = rt["oh"][:, TOPK * s:TOPK * s + TOPK, :]
                link(dve.tensor_tensor(oh, iota[:, 0:NE].unsqueeze(1).to_broadcast([P, TOPK, NE]),
                                       over(rt["idxf"][:, s, 0:TOPK], NE), ALU.is_equal))
                dve.tensor_reduce(rt["picked"][:, s, :], oh.rearrange("p k e -> p e k"), AX, ALU.add
                                  ).then_inc(S["picked_made"], 1)
            dve.memset(rt["gm"], 0.0)
            link(dve.memset(rt["posm"], -1.0))
            dve.wait_ge(S["top_exp"], 2)
            link(dve.reciprocal(rt["sum"], rt["sum"]))
            for s in range(2):
                oh = rt["oh"][:, TOPK * s:TOPK * s + TOPK, :]
                ohg = rt["ohg"][:, TOPK * s:TOPK * s + TOPK, :]
                link(dve.tensor_scalar(rt["ex"][:, s, :], rt["ex"][:, s, :], rt["sum"][:, s:s + 1], None, ALU.mult))
                link(dve.tensor_tensor(ohg, oh, over(rt["ex"][:, s, :], NE), ALU.mult))
                dve.tensor_reduce(rt["gm"][:, s, 0:NE], ohg.rearrange("p k e -> p e k"), AX, ALU.add
                                  ).then_inc(S["gm_made"], 1)
            dve.wait_ge(S["ranked"], 1)
            dve.wait_ge(S["picked_made"], 2)
            link(dve.scalar_tensor_tensor(rt["posm"][:, :, 0:NE],
                                          bank[5][:, 64:64 + 2 * NE].rearrange("p (a b) -> p a b", a=2), 1.0,
                                          rt["picked"], ALU.add, ALU.mult))
            link(dve.tensor_scalar(rt["posm"][:, :, 0:NE], rt["posm"][:, :, 0:NE], -1.0, None, ALU.add))
            dve.wait_ge(S["counted"], 1)
            link(dve.tensor_scalar(rt["cmp"], iota[0:NE, SLOTS:TOK:SLOTS], bank[6][0:NE, 0:1], None, ALU.is_lt))
            link(dve.tensor_reduce(rt["np"], rt["cmp"], AX, ALU.add))
            dve.tensor_scalar(rt["np"], rt["np"], 1.0, None, ALU.add).then_inc(S["np_made"], 1)
            dve.wait_ge(S["before_made"], 1)
            link(dve.tensor_tensor(rt["pinc"], bank[6][0:NE, 1:2], rt["np"], ALU.add))
            dve.tensor_scalar(rt["past"], iota[0:NE, 0:MAX_PASS + 1], rt["pinc"], None, ALU.is_ge
                              ).then_inc(S["past_made"], 1)
            dve.wait_ge(S["tab_summed"], 1)
            M1 = MAX_PASS + 1
            link(dve.tensor_copy(rt["tabf"], bank[6][0:1, 64:64 + N_TAB]))
            base = rt["tabf"][:, T_BASE:T_BASE + M1]
            link(dve.tensor_tensor(base, iota[0:1, 0:M1], base, ALU.subtract))
            link(dve.tensor_scalar(base, base, float(SLOTS), float(TOK - SLOTS), ALU.mult, ALU.min))
            dve.tensor_copy(tab[:, :], rt["tabf"]).then_inc(S["table_made"], 1)
            dve.wait_ge(S["gt_turned"], 1)
            dve.tensor_copy(mo["gt"], bank[7][0:NE, 0:TOK]).then_inc(S["gt_kept"], 1)

            def select(n):
                e = table(dve, n + T_EXP, 0, NE)
                base = table(dve, n + T_BASE, 0, TOK - SLOTS)
                for s in range(2):
                    dve.tensor_scalar(mo["sel"][:, s, :], iota[:, bass.ds(base, SLOTS)],
                                      rt["posm"][:, s, bass.ds(e, 1)], None, ALU.is_equal
                                      ).then_inc(S["sel_ready"], 1)
                dve.tensor_copy(mo["esel"], ident[0:NE, bass.ds(e, 1)].to_broadcast([NE, SLOTS])
                                ).then_inc(S["esel_ready"], 1)
                return e

            def gate_selected(n, e):
                dve.wait_ge(S["sel_ready"], n * 2 + 2)
                for s in range(2):
                    dve.tensor_scalar(mo["selz"][:, s, SLOTS:2 * SLOTS], mo["sel"][:, s, :],
                                      rt["gm"][:, s, bass.ds(e, 1)], None, ALU.mult).then_inc(S["selg_ready"], 1)

            link(dve.memset(mo["selz"], 0.0))
            dve.memset(mo["selt"], 0.0).then_inc(S["selt_kept"], 1)
            dve.memset(mo["y"], 0.0).then_inc(S["y_kept"], 1)
            dve.wait_ge(S["table_made"], 1)
            gate_selected(0, select(0))
            n_pass = table(dve, T_ALL, NE, MAX_PASS)
            STEPS = 2
            with dve.Fori(0, n_pass) as n:
                dve.wait_ge(S["gathered"], n + 1)
                dve.wait_ge(S["selg_ready"], n * 2 + 2)
                dve.wait_ge(S["biased"], n + 1)
                e_next = select(n + 1)
                dve.wait_ge(S["chunk_used"], n * RING + (N_TRUNK + GU_CHUNKS))
                dve.tensor_scalar(mo["glu"], bank[5][:, :], LIMIT, None, ALU.min).then_inc(S["glu_ready"], 1)
                dve.tensor_scalar(mo["lin"], bank[6][:, :], LIMIT, -LIMIT, ALU.min, ALU.max
                                  ).then_inc(S["dve_pass"], 1)
                dve.wait_ge(S["sig_ready"], n + 1)
                dve.tensor_tensor(mo["sig"], mo["sig"], mo["glu"], ALU.mult).then_inc(S["dve_pass"], 1)
                dve.wait_ge(S["dve_pass"], n * STEPS + STEPS)
                dve.scalar_tensor_tensor(mo["act"], mo["lin"], 1.0, mo["sig"], ALU.add, ALU.mult
                                         ).then_inc(S["act_ready"], 1)
                dve.wait_ge(S["selt_turned"], n + 1)
                gate_selected(n + 1, e_next)

            dve.wait_ge(S["acc_turned"], 1)
            add_gated(lambda k, s: bank[4 + k // 2][:, (k % 2) * TOK + s * L:(k % 2) * TOK + (s + 1) * L], 40, 2)
            dve.wait_ge(S["mixed"], 2)
            dve.wait_ge(S["ssq"], 3)
            rstd_from(bank[0][:, 0:TOK], D, RMS_EPS, "var", "root", 3)
            link(dve.tensor_tensor(x[:, :, :], x[:, :, :], rstd[:, :].unsqueeze(1).to_broadcast([P, KD, TOK]),
                                   ALU.mult))
            dve.tensor_tensor(x[:, :, :], x[:, :, :], over(pcol("final", 0, KD), TOK), ALU.mult
                              ).then_inc(S["y_ready"], 1)

        @block.tensor
        def _(pe):
            def norm_sum(n, to):
                pe.wait_ge(S["squared"], n)
                for k in range(KD):
                    ins = pe.matmul(to, ones[:, :], h[:, k, :], start=k == 0, stop=k == KD - 1)
                ins.then_inc(S["ssq"], 1)

            def trunk_chunk(c, k):
                return ring[:, c % RING, :].rearrange("p (k n) -> p k n", k=k)

            def product(c, b, src, to):
                w = trunk_chunk(c, KD)
                for k in range(KD):
                    ins = pe.matmul(to, w[:, k, b * P:(b + 1) * P], src[:, k, :], start=k == 0, stop=k == KD - 1)
                return ins

            def product4(c, src, to):
                arrived(pe, c)
                for b in range(4):
                    ins = product(c, b, src, to(b))
                ins.then_inc(S["chunk_used"], 1)

            def mod_sum(g):
                for j in range(MOD_CHUNKS):
                    c = C_MOD[g] + j
                    arrived(pe, c)
                    w = trunk_chunk(c, 2)
                    for i in range(2):
                        k = 2 * j + i
                        for q in range(4):
                            ins = pe.matmul(bank[5][32 * q:32 * q + 32, :], cond[:, k, :],
                                            w[:, i, q * 512:(q + 1) * 512], start=k == 0, stop=k == KD - 1)
                    ins.then_inc(S["chunk_used"], 1)

            def mod_turn(g):
                pe.wait_ge(S["mod_kept"], g + 1)
                for j in range(4):
                    ins = pe.transpose(bank[0][:, j * P:(j + 1) * P], mod_rows[:, j * P:(j + 1) * P], ident[:, :])
                ins.then_inc(S["mod_turned"], 1)

            pe.wait_ge(S["ones_made"], 1)
            norm_sum(1, bank[4][:, 0:TOK])

            pe.wait_ge(S["consts_made"], 1)
            pe.wait_ge(S["rpb_in"], 64)
            for q in range(2):
                ins = pe.matmul(bank[6 + q][:, :], mirror[:, :],
                                abias[:, 4 * q:4 * q + 4, :].rearrange("p a b -> p (a b)"), start=True, stop=True)
            ins.then_inc(S["bias_turned"], 1)

            pe.wait_ge(S["cond_ready"], 1)
            mod_sum(0)
            mod_turn(0)

            def project(i):
                if i >= 2:
                    pe.wait_ge(S["proj_kept"], 4 * (i - 1))
                product4(C_PROJ + i, h, lambda b: bank[2 * (i % 2) + b // 2][:, (b % 2) * TOK:(b % 2 + 1) * TOK])

            pe.wait_ge(S["h_ready"], 1)
            pe.wait_ge(S["mod_made"], 4)
            project(0)
            project(1)
            pe.wait_ge(S["gatew_in"], 16)
            pe.wait_ge(S["bias_ready"], 2)
            for q in range(4):
                for k in range(KD):
                    ins = pe.matmul(bank[6 + q // 2][0:MH, (q % 2) * TOK:(q % 2 + 1) * TOK],
                                    wgate[:, k, 4 * q:4 * q + 4], h[:, k, :], start=k == 0, stop=k == KD - 1)
            ins.then_inc(S["gates_summed"], 1)
            for i in range(2, EARLY):
                project(i)
            pe.wait_ge(S["proj_kept"], 4 * EARLY)
            pe.wait_ge(S["gates_kept"], 4)
            for s in range(2):
                for b in range(4):
                    ins = pe.transpose(bank[6 + s][:, b * P:(b + 1) * P], z[:, Z["va"] + b, s * L:(s + 1) * L],
                                       ident[:, :])
            ins.then_inc(S["va_turned"], 1)

            def late_project(t):
                c = C_PROJ + EARLY + t // 4
                if t % 4 == 0:
                    arrived(pe, c)
                pe.wait_ge(S["proj_kept"], 4 * EARLY + t - 1)
                ins = product(c, t % 4, h, late_bank(t))
                ins.then_inc(S["chunk_used"] if t % 4 == 3 else S["block_made"], 1)

            def scores(i):
                if i >= 2:
                    pe.wait_ge(S["exp_done"], 2 * (i - 1))
                o = HD * (i % 2)
                b = bank[4 + i % 2]
                q = z[o:o + HD, Z["qa"] + i // 2, :]
                k = z[o:o + HD, Z["ka"] + i // 2, :]
                pe.matmul(b[:, 0:L], q[:, 0:L], k[:, 0:L], start=True, stop=True)
                pe.matmul(b[:, L:2 * L], q[:, L:TOK], k[:, L:TOK], start=True, stop=True)
                pe.matmul(b[:, 2 * L:3 * L], q[:, L:TOK], kctx[o:o + HD, i // 2, :], start=True, stop=True
                          ).then_inc(S["scored"], 1)

            def attend(i):
                pe.wait_ge(S["probs_ready"], i + 1)
                if i >= 2:
                    pe.wait_ge(S["pt_kept"], i - 1)
                for q in range(3):
                    ins = pe.transpose(bank[6 + i % 2][:, q * L:(q + 1) * L], att["p"][:, i % 2, q * L:(q + 1) * L],
                                       ident[:, :])
                ins.then_inc(S["probs_turned"], 1)
                pe.wait_ge(S["pt_kept"], i + 1)
                if i >= 4 and i % 2 == 0:
                    pe.wait_ge(S["att_kept"], i // 2 - 1)
                o = HD * (i % 2)
                to = bank[(i // 2) % 2][o:o + HD, :]
                pt = att["pt"][:, i % 2, :]
                cols = slice(i * HD, (i + 1) * HD)
                pe.matmul(to[:, 0:L], va_tok[:, 0, cols], pt[:, 0:L], start=True, stop=True)
                pe.matmul(to[:, L:TOK], va_tok[:, 1, cols], pt[:, L:2 * L], start=True, stop=False)
                pe.matmul(to[:, L:TOK], vctx[:, cols], pt[:, 2 * L:3 * L], start=False, stop=True
                          ).then_inc(S["attended"], 1)

            pe.wait_ge(S["kctx_in"], 16)
            pe.wait_ge(S["vctx_in"], 16)
            pe.wait_ge(S["va_kept"], 2)
            for i in range(NH + 1):
                if i < NH:
                    scores(i)
                if i:
                    attend(i - 1)
                if i < NH:
                    late_project(2 * i)
                    late_project(2 * i + 1)

            pe.wait_ge(S["conv_step"], 4 * CONV_W)
            pe.wait_ge(S["exp_done"], 2 * NH)
            pe.wait_ge(S["pt_kept"], NH)
            pe.wait_ge(S["att_kept"], NH // 2)
            for b in range(4):
                ins = pe.matmul(bank[4][:, 0:TOK], ones[:, :], acc[:, b, :], start=b == 0, stop=b == 3)
            ins.then_inc(S["conv_sum"], 1)
            pe.wait_ge(S["proj_kept"], 4 * len(PROJ))
            for s in range(2):
                for b in range(4):
                    ins = pe.transpose(bank[2 + s][:, b * P:(b + 1) * P], z[:, Z["vm"] + b, s * L:(s + 1) * L],
                                       ident[:, :])
            ins.then_inc(S["v_turned"], 1)
            mod_sum(1)
            pe.wait_ge(S["km_scaled"], 1)
            for b in range(4):
                ins = pe.transpose(bank[7][:, b * P:(b + 1) * P], z[:, Z["km"] + b, 0:L], ident[:, :])
            ins.then_inc(S["v_turned"], 1)
            pe.wait_ge(S["conv_sq"], 1)
            for b in range(4):
                ins = pe.matmul(bank[4][:, TOK:2 * TOK], ones[:, :], conv_sq[:, b, :], start=b == 0, stop=b == 3)
            ins.then_inc(S["conv_sqsum"], 1)
            mod_turn(1)
            mod_sum(2)
            pe.wait_ge(S["rows_ready"], 1)
            pe.wait_ge(S["w_ready"], 2)
            turns = [rows["g"][:, d, s * L:(s + 1) * L] for d in range(2) for s in range(2)]
            turns += [rows["b"][:, d, s * L:(s + 1) * L] for d in range(2) for s in range(2)]
            turns += [rows["w"][:, d, :] for d in range(2)]
            for i, v in enumerate(turns):
                ins = pe.transpose(bank[6][:, MH * i:MH * i + MH], v, ident[0:MH, 0:MH])
            ins.then_inc(S["cols_turned"], 1)
            pe.wait_ge(S["mod_made"], 8)
            mod_turn(2)

            def ml_front(i):
                if i:
                    pe.wait_ge(S["decayed"], 4 * i)
                pe.matmul(bank[4][:, :], selrow[:, i, :], negm.rearrange("p d t -> p (d t)"),
                          start=True, stop=False)
                pe.matmul(bank[4][:, :], ident[:, :], dmask[:, :, :, :].rearrange("p d s t -> p (d s t)"),
                          start=False, stop=True).then_inc(S["spread"], 1)
                if i:
                    pe.wait_ge(S["ptm_ready"], i)
                q, k = z[:, Z["qm"] + i, :], z[:, Z["km"] + i, :]
                for s in range(2):
                    ins = pe.matmul(bank[5][:, s * L:(s + 1) * L], k[:, s * L:(s + 1) * L], q[:, s * L:(s + 1) * L],
                                    start=True, stop=True)
                ins.then_inc(S["keyed"], 1)
                if i:
                    pe.wait_ge(S["inter_kept"], 2 * i)
                for d in range(2):
                    ins = pe.matmul(bank[0][:, d * (P + 1):(d + 1) * (P + 1)], q[:, L:TOK], cinit[:, d, i, :],
                                    start=True, stop=True)
                ins.then_inc(S["inter_made"], 1)

            def ml_back(i):
                pe.wait_ge(S["ptm_ready"], i + 1)
                if i:
                    pe.wait_ge(S["ns_made"], 2 * i)
                for d in range(2):
                    for s in range(2):
                        ins = pe.matmul(bank[6 + d][:, s * (P + 1):(s + 1) * (P + 1)], ml["pt"][:, 2 * d + s, :],
                                        vmt[:, s, i, :], start=True, stop=True)
                ins.then_inc(S["summed"], 1)
                pe.wait_ge(S["kw_ready"], i + 1)
                if i:
                    pe.wait_ge(S["state_kept"], 2 * i)
                pe.matmul(bank[3][:, 0:2 * P], vmt[:, 0, i, 0:P], ml["kw"].rearrange("p d k -> p (d k)"),
                          start=True, stop=True)
                pe.matmul(bank[3][0:2, TOK:TOK + P], sm["wsrc"][:, i, :], kmt[:, i, :], start=True, stop=True
                          ).then_inc(S["state_made"], 1)

            pe.wait_ge(S["cinit_in"], 16)
            pe.wait_ge(S["pads_made"], 2)
            pe.wait_ge(S["conv_var"], 1)
            pe.wait_ge(S["cols_kept"], 1)
            pe.wait_ge(S["v_kept"], 3)
            pe.wait_ge(S["mod_made"], 12)
            pe.wait_ge(S["yc_ready"], 1)

            def merge_unit(u):
                c, b = C_MERGE + 3 * (u // 8), u % 8
                if b == 0:
                    for i in range(3):
                        arrived(pe, c + i)
                if u >= N_SIG:
                    pe.wait_ge(S["merge_read"], u - N_SIG + 1)
                to = merge_bank(u)
                ins = product(c + b // 4, b % 4, h, to[:, 0:TOK])
                if b % 4 == 3:
                    ins.then_inc(S["chunk_used"], 1)
                w = trunk_chunk(c + 2, 4)
                for k in range(4):
                    ins = pe.matmul(to[:, TOK:2 * TOK], w[:, k, b * P:(b + 1) * P],
                                    branch_out[BRANCHES[u // 8]][:, k, :], start=k == 0, stop=k == 3)
                ins.then_inc(S["chunk_used"] if b == 7 else S["merge_made"], 1)

            ml_front(0)
            for i in range(MH):
                if i < MH - 1:
                    ml_front(i + 1)
                merge_unit(2 * i)
                ml_back(i)
                merge_unit(2 * i + 1)
            for u in range(8, 12):
                merge_unit(u)
            pe.wait_ge(S["hm_ready"], 1)
            pe.wait_ge(S["decayed"], 4 * MH)
            pe.wait_ge(S["state_kept"], 2 * MH)
            for i in range(MH):
                for s in range(2):
                    at = (i % 2) * TOK + s * L
                    ins = pe.transpose(bank[4 + i // 2][:, at:at + L], hm[:, s, i, :], ident[:, :])
            ins.then_inc(S["hm_turned"], 1)
            for u in range(12, 16):
                merge_unit(u)
            pe.wait_ge(S["ym_ready"], 1)
            for u in range(16, 24):
                merge_unit(u)
            pe.wait_ge(S["merge_read"], 24)
            for c in range(2):
                product4(C_OUT + c, merged, lambda b: bank[4 + 2 * c + b // 2][:, (b % 2) * TOK:(b % 2 + 1) * TOK])

            norm_sum(2, bank[4][:, 0:TOK])
            pe.wait_ge(S["h_ready"], 2)
            pe.wait_ge(S["router_in"], 32)
            for s in range(2):
                for k in range(KD):
                    pe.matmul(bank[5][:, s * NE:(s + 1) * NE], h[:, k, s * L:(s + 1) * L], wrt[:, k, :],
                              start=k == 0, stop=False)
                ins = pe.matmul(bank[5][:, s * NE:(s + 1) * NE], ones[0:1, :], rt["brt"], start=False, stop=True)
            ins.then_inc(S["logits_made"], 1)
            pe.wait_ge(S["mixed"], 1)
            for s in range(2):
                for k in range(KD):
                    ins = pe.transpose(bank[2 * s + k // 4][:, (k % 4) * P:(k % 4 + 1) * P], h[:, k, s * L:(s + 1) * L],
                                       ident[:, :])
            ins.then_inc(S["h2_turned"], 1)
            pe.wait_ge(S["picked_made"], 2)
            pe.matmul(bank[5][:, 64:64 + NE], strict[:, :], rt["picked"][:, 0, :], start=True, stop=True)
            pe.matmul(bank[5][:, 64 + NE:64 + 2 * NE], ones[:, :], rt["picked"][:, 0, :], start=True, stop=False)
            pe.matmul(bank[5][:, 64 + NE:64 + 2 * NE], strict[:, :], rt["picked"][:, 1, :], start=False, stop=True
                      ).then_inc(S["ranked"], 1)
            for s in range(2):
                ins = pe.matmul(bank[6][0:NE, 0:1], rt["picked"][:, s, :], ones[:, 0:1], start=s == 0, stop=s == 1)
            ins.then_inc(S["counted"], 1)
            pe.wait_ge(S["np_made"], 1)
            pe.matmul(bank[6][0:NE, 1:2], strict[0:NE, 0:NE], rt["np"], start=True, stop=True
                      ).then_inc(S["before_made"], 1)
            pe.wait_ge(S["past_made"], 1)
            M1 = MAX_PASS + 1
            row = bank[6][0:1, 64:64 + N_TAB]
            pe.matmul(row[:, T_EXP:T_EXP + M1], ones[0:NE, 0:1], rt["past"], start=True, stop=True)
            pe.matmul(row[:, T_BASE:T_BASE + M1], rt["np"], rt["past"], start=True, stop=True)
            pe.matmul(row[:, T_BEFORE:T_BEFORE + NE], rt["np"], strict[0:NE, 0:NE], start=True, stop=True)
            pe.matmul(row[:, T_ALL:T_ALL + 1], rt["np"], ones[0:NE, 0:1], start=True, stop=True
                      ).then_inc(S["tab_summed"], 1)
            pe.wait_ge(S["gm_made"], 2)
            for s in range(2):
                ins = pe.transpose(bank[7][0:NE, s * L:(s + 1) * L], rt["gm"][:, s, 0:NE], ident[:, :])
            ins.then_inc(S["gt_turned"], 1)
            pe.wait_ge(S["gt_kept"], 1)
            pe.wait_ge(S["bdn_in"], 16)
            pe.wait_ge(S["h2_kept"], 4)
            for q in range(4):
                pe.matmul(bank[q][:, :], mo["gt"][:, (q // 2) * L:(q // 2 + 1) * L],
                          bdn[:, (q % 2) * 512:(q % 2 + 1) * 512], start=True, stop=False,
                          skip_group_check=True)

            def gather(n):
                pe.wait_ge(S["sel_ready"], n * 2 + 2)
                for s in range(2):
                    for f in range(2):
                        ins = pe.matmul(bank[4][f * SLOTS:(f + 1) * SLOTS, :], mo["sel"][:, s, :],
                                        mo["h_tok"][:, s, f * 512:(f + 1) * 512], start=s == 0, stop=s == 1)
                ins.then_inc(S["gathered"], 1)

            def turn4(to, src, name):
                for j in range(4):
                    ins = pe.transpose(bank[to][:, j * P:(j + 1) * P], src[:, j * P:(j + 1) * P], ident[:, :])
                ins.then_inc(S[name], 1)

            def scatter():
                for q in range(4):
                    ins = pe.matmul(bank[q][:, :], mo["selt"][:, q // 2, q % 2, :], mo["y"], start=False, stop=False,
                                    skip_group_check=True)
                ins.then_inc(S["scattered"], 1)

            gather(0)
            pe.wait_ge(S["gath_kept"], 1)
            turn4(6, mo["gath"], "xg_turned")
            pe.wait_ge(S["bgu_in"], 16)
            pe.wait_ge(S["table_made"], 1)
            n_pass = table(pe, T_ALL, NE, MAX_PASS)
            with pe.Fori(0, n_pass) as n:
                e = table(pe, n + T_EXP, 0, NE - 1)
                pe.wait_ge(S["xg_ready"], n + 1)
                pe.wait_ge(S["esel_ready"], n + 1)
                for f in range(2):
                    for u in range(2):
                        ins = pe.matmul(bank[5 + u][f * SLOTS:(f + 1) * SLOTS, :], mo["esel"],
                                        bgu[:, u * D + f * 512:u * D + (f + 1) * 512], start=True, stop=False)
                ins.then_inc(S["biased"], 1)
                for j in range(GU_CHUNKS):
                    expert_arrived(pe, j, e)
                    w = trunk_chunk(expert_slot(j), 2)
                    for i in range(2):
                        k = 2 * j + i
                        for u in range(2):
                            for f in range(2):
                                at = u * D + f * 512
                                ins = pe.matmul(bank[5 + u][f * SLOTS:(f + 1) * SLOTS, :],
                                                mo["xg"][:, k % 4, k // 4, :], w[:, i, at:at + 512],
                                                start=False, stop=k == KD - 1)
                    ins.then_inc(S["chunk_used"], 1)
                pe.wait_ge(S["y_kept"], n + 1)
                pe.wait_ge(S["selt_kept"], n + 1)
                scatter()
                pe.wait_ge(S["gath_kept"], n + 1)
                gather(n + 1)
                pe.wait_ge(S["selg_ready"], n * 2 + 2)
                for s in range(2):
                    for f in range(2):
                        at = (1 - f) * SLOTS
                        q = 2 * s + f
                        ins = pe.transpose(bank[7][:, q * P:(q + 1) * P], mo["selz"][:, s, at:at + P], ident[:, :])
                ins.then_inc(S["selt_turned"], 1)
                pe.wait_ge(S["act_ready"], n + 1)
                turn4(5, mo["act"], "act_turned")
                pe.wait_ge(S["gath_kept"], n + 2)
                turn4(6, mo["gath"], "xg_turned")
                pe.wait_ge(S["actt_kept"], n + 1)
                pe.wait_ge(S["selt_kept"], n + 2)
                for j in range(DN_CHUNKS):
                    expert_arrived(pe, GU_CHUNKS + j, e)
                    w = trunk_chunk(expert_slot(GU_CHUNKS + j), 4)
                    for i in range(4):
                        for f in range(2):
                            ins = pe.matmul(bank[7][f * SLOTS:(f + 1) * SLOTS, :], mo["actt"][:, i, j, :],
                                            w[:, i, f * 512:(f + 1) * 512], start=j + i == 0, stop=j + i == 4)
                    ins.then_inc(S["chunk_used"], 1)

            pe.wait_ge(S["y_kept"], n_pass + 1)
            pe.wait_ge(S["selt_kept"], n_pass + 1)
            scatter()

            pe.wait_ge(S["acc_kept"], 4)
            for k in range(KD):
                for s in range(2):
                    at = (k % 2) * TOK + s * L
                    ins = pe.transpose(bank[4 + k // 2][:, at:at + L], mo["h_tok"][:, s, k * P:(k + 1) * P], ident[:, :])
            ins.then_inc(S["acc_turned"], 1)
            norm_sum(3, bank[0][:, 0:TOK])


def _blocks(v):
    return v.reshape(-1, P).T


def _chunks(w, width=512):
    k, n = w.shape
    return w.reshape(k // P, P, n // width, width).transpose(2, 1, 0, 3).reshape(n // width, P, -1)


def pack(a):
    dA, dC, dM = NH * HD, 4 * P, MH * P
    sizes = [("qa", dA), ("ka", dA), ("va", dA), ("cu", dC), ("cg", dC), ("qm", dM), ("km", dM), ("vm", dM),
             ("om", dM), ("gate", 16), ("ga", D), ("gc", D), ("gm", D)]
    w_in, b_in = a["w_in"][0], a["b_in"][0]
    w, b, at = {}, {}, 0
    for name, n in sizes:
        w[name], b[name] = w_in[:, at:at + n], b_in[at:at + n]
        at += n
    mod = a["w_mod"][0].reshape(MOD_CHUNKS, 2, P, MOD_GROUPS, 2048).transpose(3, 0, 2, 1, 4)
    mod = mod.reshape(MOD_GROUPS, MOD_CHUNKS, P, CHUNK)
    trunk = [mod[0]] + [_chunks(w[name]) for name in PROJ] + [mod[1], mod[2]]
    for br in BRANCHES:
        trunk += [_chunks(w["g" + br]), _chunks(a["w_p" + br][0], D)]
    trunk.append(_chunks(a["w_out"][0]))
    params = {
        "norm1": _blocks(a["norm1_g"][0]), "norm2": _blocks(a["norm2_g"][0]), "final": _blocks(a["final_g"]),
        "b_mod": _blocks(a["b_mod"][0]),
        "b_in": np.concatenate([_blocks(b[n]) for n in PROJ + ["g" + br for br in BRANCHES]], axis=1),
        "w_dw": a["w_dw"][0].T.reshape(4, P, CONV_W).transpose(1, 0, 2).reshape(P, -1),
        "b_dw": _blocks(a["b_dw"][0]), "cln_g": _blocks(a["cln_g"][0]), "cln_b": _blocks(a["cln_b"][0]),
        "mnorm": _blocks(a["mnorm_g"][0]),
        "cond": np.stack([_blocks(a["c_ctx"]), _blocks(a["c"][0])], axis=2).reshape(P, -1),
    }
    x_all = np.concatenate([a["x_prompt"][0], a["x_sample"][0]], axis=0)
    c_init = np.concatenate([a["state_C"][0, 0].transpose(3, 0, 1, 2), a["state_n"][0, 0].transpose(2, 0, 1)[..., None]],
                            axis=3)
    packed = {
        "trunk_w": np.concatenate(trunk, axis=0),
        "w_gu": a["w_gu"][0],
        "w_down": a["w_down"][0],
        "x_t": x_all.T.reshape(KD, P, TOK).transpose(1, 0, 2),
        "params": np.concatenate([params[n] for n, _ in PAR_WIDTHS], axis=1),
        "w_gate": w["gate"].reshape(KD, P, 16).transpose(1, 0, 2),
        "b_gate": b["gate"].reshape(4, MH).T,
        "m_init": a["state_m"][0, 0].T,
        "k_ctx_t": a["cache_k"][0, 0].reshape(L, 4, P).transpose(2, 1, 0),
        "v_ctx": a["cache_v"][0, 0].reshape(L, NH * HD),
        "c_init_t": c_init,
        "rpb": a["rpb"][0],
        "w_router": a["w_router"][0].reshape(KD, P, NE).transpose(1, 0, 2),
        "b_router": a["b_router"],
        "b_gu": a["b_gu"][0],
        "b_down": a["b_down"][0],
    }
    return {n: np.ascontiguousarray(v) for n, v in packed.items()}


_OUTS = {"y_t": (P, KD, TOK), "k_new_t": (P, 4, L), "v_new_t": (P, 4, L), "c_new": (P, MH, 2, P),
         "n_new": (2, MH * P), "m_new": (MH, 2)}


def kernel(**inputs):
    import concourse.bacc as _bacc
    from concourse.bass_utils import run_bass_kernel_spmd as _run

    arrays = pack({n: np.asarray(v) for n, v in inputs.items()})
    nc = _bacc.Bacc("TRN2", target_bir_lowering=False, num_devices=1)
    feeds, args = {}, []
    for name, v in arrays.items():
        feeds[f"in_{name}"] = v
        args.append(nc.dram_tensor(f"in_{name}", v.shape, F32, kind="ExternalInput").ap())
    for name, shape in _OUTS.items():
        args.append(nc.dram_tensor(f"out_{name}", shape, F32, kind="ExternalOutput").ap())
    hybrid_layer(nc, *args)
    r = _run(nc, [feeds], core_ids=[0]).results[0]
    got = {n: r[f"out_{n}"] for n in _OUTS}
    y = got["y_t"].transpose(1, 0, 2).reshape(D, TOK).T
    kv = [got[n].transpose(2, 1, 0).reshape(1, 1, L, NH, HD) for n in ("k_new_t", "v_new_t")]
    return (y[None, 0:L], y[None, L:TOK], kv[0], kv[1],
            got["c_new"].transpose(2, 1, 0, 3)[None, None],
            got["n_new"].reshape(1, 1, 2, MH, P), got["m_new"].T[None, None])
```

```python
from contextlib import ExitStack

import numpy as np

import concourse.bass as bass
from concourse import mybir

F32 = mybir.dt.float32
I32 = mybir.dt.int32
U32 = mybir.dt.uint32
ALU = mybir.AluOpType
ACT = mybir.ActivationFunctionType
AX = mybir.AxisListType.X

P = 128
D = 1024
KD = D // P
L = 128
TOK = 2 * L
GRID_W = 64
NH, HD = 8, 64
MH = 4
WIN_ROWS, WIN_COLS = 8, 16
RPB_ROWS, RPB_COLS = 2 * WIN_ROWS - 1, 2 * WIN_COLS - 1
CONV_W = 31
PAD = CONV_W // 2
NE, TOPK = 32, 4
SLOTS = 64
MAX_PASS = NE + TOK * TOPK // SLOTS
ALPHA, LIMIT = 1.702, 7.0
RMS_EPS, LN_EPS = 1e-6, 1e-5
ATT_SCALE = HD ** -0.5
M_SCALE = P ** -0.5
FAR = -1.0e30
LOWEST = -3.0e38

CHUNK = 4096
RING = 6
EXPERT_RING = 8
PER_EXPERT = 6
AHEAD = EXPERT_RING - PER_EXPERT
TURN = 4
GU_CHUNKS, DN_CHUNKS = 4, 2
MOD_GROUPS, MOD_CHUNKS = 3, 4
PROJ = ["cu", "cg", "qa", "ka", "va", "qm", "km", "vm", "om"]
EARLY = 5
BRANCHES = ["c", "a", "m"]
MODS_AFTER = [1, 1, 2, 2, 2]
C_PROJ, C_MOD = [], [list(range(MOD_CHUNKS)), [], []]
_c = MOD_CHUNKS
for _i in range(len(PROJ)):
    C_PROJ.append(_c)
    _c += 1
    for _ in range(MODS_AFTER[_i] if _i < EARLY else 0):
        C_MOD[1 if len(C_MOD[1]) < MOD_CHUNKS else 2].append(_c)
        _c += 1
C_MERGE = _c
C_OUT = C_MERGE + 3 * len(BRANCHES)
N_TRUNK = C_OUT + 2
GATES_AHEAD, GATES_AFTER = [[4], [5], [7], []], [[], [6], [], []]
MERGES_AHEAD, MERGES_AFTER = [[], [], [], [2, 3]], [[], [], [0, 1], [4, 5, 6, 7]]
Z = {name: 4 * i for i, name in enumerate(PROJ)}
PAR_WIDTHS = [("norm1", KD), ("norm2", KD), ("final", KD), ("b_mod", 48), ("b_in", 60),
              ("w_dw", 4 * CONV_W), ("b_dw", 4), ("cln_g", 4), ("cln_b", 4), ("mnorm", MH), ("cond", 2 * KD)]
PC = {}
N_PAR = 0
for _name, _w in PAR_WIDTHS:
    PC[_name] = N_PAR
    N_PAR += _w
T_EXP, T_BASE = 0, MAX_PASS + 1
T_BEFORE = 2 * (MAX_PASS + 1)
T_ALL = T_BEFORE + NE
N_TAB = T_ALL + 1


ACT_BLOCKS = 6


def hybrid_layer(nc, trunk_w, w_gu, w_down, x_t, params, w_gate, b_gate, m_init, k_ctx_t, v_ctx,
                 c_init_t, rpb, w_router, b_router, b_gu, b_down,
                 y_t, k_new_t, v_new_t, c_new, n_new, m_new):
    with ExitStack() as ctx:
        def sb(name, shape, dt=F32):
            return ctx.enter_context(nc.sbuf_tensor(name, shape, dt))

        def sem(name):
            return ctx.enter_context(nc.semaphore(name))

        big = sb("big", [P, RING * CHUNK + 4 * len(PROJ) * TOK])
        ring = big[:, 0:RING * CHUNK].rearrange("p (r c) -> p r c", r=RING)
        expert_ring = big[:, 0:EXPERT_RING * CHUNK]
        x = sb("x", [P, KD, TOK])
        h = sb("h", [P, KD, TOK])
        par = sb("par", [P, N_PAR])
        mod = sb("mod", [P, 48, 2])
        gain = sb("gain", [P, 2, KD, 2])
        rstd = sb("rstd", [P, TOK])
        ident = sb("ident", [P, P])
        ones = sb("ones", [P, P])
        strict = sb("strict", [P, P])
        iota = sb("iota", [P, TOK + 1])
        stack = sb("stack", [P, NE])
        tab = sb("tab", [1, N_TAB], I32)
        zf = big[:, RING * CHUNK:RING * CHUNK + 4 * len(PROJ) * TOK]
        z = zf.rearrange("p (a b) -> p a b", b=TOK)
        merged = sb("merged", [P, KD, TOK])
        wgate = sb("wgate", [P, KD, 16])
        bgate = sb("bgate", [MH, 4])
        minit = sb("minit", [MH, 2])
        cinit = sb("cinit", [P, 2, MH, P + 1])
        abias = sb("abias", [P, NH, L])
        side = sb("side", [P, 4480])
        gates = sb("gates", [MH, 4, TOK])
        selrow = sb("selrow", [MH, MH, P])
        work = sb("work", [P, 2840])
        small = sb("small", [P, 192])

        bank = [ctx.enter_context(nc.psum_tensor(f"bank{i}", [P, 512], F32)) for i in range(8)]

        def carve(base, at, shape, parts=P):
            n = int(np.prod(shape))
            v = base[0:parts, at:at + n]
            if len(shape) == 2:
                v = v.rearrange("p (a b) -> p a b", a=shape[0])
            if len(shape) == 3:
                v = v.rearrange("p (a b c) -> p a b c", a=shape[0], b=shape[1])
            return v, at + n

        def carve_all(base, what):
            out, at = {}, 0
            for name, shape, *parts in what:
                out[name], at = carve(base, at, shape, *parts)
            return out

        mx = carve_all(side, [("kctx", [4, L]), ("vctx", [NH * HD]), ("amask", [L]), ("dmask", [2, 2, L]),
                              ("apad", [4, 2, L + 2 * PAD]), ("vmt", [2, MH, P + 1]), ("kmt", [MH, P])])
        kctx, vctx, amask, apad = mx["kctx"], mx["vctx"], mx["amask"], mx["apad"]
        dmask = mx["dmask"]
        vmt = mx["vmt"]
        kmt = mx["kmt"]
        mf = merged[:, :, :].rearrange("p a b -> p (a b)")
        hf = h[:, :, :].rearrange("p a b -> p (a b)")
        af = apad.rearrange("p a b c -> p (a b c)")

        def zblocks(name, n=4):
            return z[:, Z[name]:Z[name] + n, :]

        va_tok = zf[:, Z["cg"] * TOK:(Z["cg"] + 4) * TOK].rearrange("p (s c) -> p s c", s=2)
        acc = zblocks("cu")
        branch_out = {"c": zblocks("cu"), "a": zblocks("qa"), "m": zblocks("om")}
        rows = carve_all(mf, [("b", [2, TOK], MH), ("g", [2, TOK], MH), ("w", [2, L], MH)])
        negm = gates[:, 0:2, :]
        n_out = gates[0:2, 2:4, :].rearrange("p a b -> p (a b)")
        mirror = mf[:, 5 * TOK:5 * TOK + P]
        cond = mf[:, 6 * TOK:7 * TOK].rearrange("p (k c) -> p k c", k=KD)
        conv_sq = af[:, 0:4 * TOK].rearrange("p (a b) -> p a b", a=4)
        hm = af[:, 0:2 * MH * P].rearrange("p (s h d) -> p s h d", s=2, h=MH)
        att = carve_all(work, [("p", [2, 3 * L]), ("pt", [2, 3 * L])])
        mod_rows = [work[:, at:at + 512] for at in (2048, 1536, 2048)]
        mod_bank, turn_bank = [bank[5], bank[5], bank[4]], [bank[0], bank[0], bank[5]]
        ml = carve_all(work, [("decay", [4, L]), ("pt", [4, L]), ("inter", [2, 2, P + 1]),
                              ("ns", [2, 2 * (P + 1)]), ("hd", [4, P]), ("kw", [2, P])])
        c_out = abias[:, :, :].rearrange("p (h e) k -> p h e k", h=MH)
        sm = carve_all(small, [("amax", [NH, 2]), ("aneg", [NH, 2]), ("asum", [NH, 2]), ("arec", [NH, 2]),
                               ("cols", [10, MH]), ("em", [4, MH]), ("wsrc", [MH, 2]), ("den", [4]),
                               ("hsum", [8]), ("hvar", [8]), ("mlast", [2], MH)])

        def sig_gate(u):
            return z[:, Z["cg" if u % 8 < 4 else "ka"] + u % 4, :]

        mo = carve_all(side, [("h_tok", [2, D]), ("gath", [512]), ("selt", [2, 2, L]), ("sel", [2, SLOTS]),
                              ("selz", [2, 3 * SLOTS]), ("esel", [SLOTS], NE), ("y", [512])])
        mo |= carve_all(hf, [("xg", [4, 2, SLOTS]), ("glu", [512]), ("lin", [512]), ("sig", [512])])
        mo |= carve_all(zf[:, Z["om"] * TOK:], [("act", [512]), ("actt", [4, 2, SLOTS])])
        bgu = mf[0:NE, :]
        bdn = abias[0:NE, :, :].rearrange("p a b -> p (a b)")
        rt = carve_all(work, [("lg", [2, NE]), ("top", [2, 8]), ("idxf", [2, 8]), ("ex", [2, TOPK]),
                              ("neg", [2]), ("sum", [2]), ("oh", [2 * TOPK, NE]),
                              ("ohg", [2 * TOPK, NE]), ("picked", [2, NE]), ("posm", [2, NE + 1]),
                              ("gm", [2, NE + 1]), ("cmp", [3], NE), ("np", [1], NE), ("pinc", [1], NE),
                              ("past", [MAX_PASS + 1], NE), ("tabf", [N_TAB], 1), ("brt", [NE], 1), ("brs", [2, NE], 1),
                              ("lt", [TOK]), ("wrs", [2 * KD, NE])])
        wrt = cinit[:, :, :, :].rearrange("p a b c -> p (a b c)")[:, 0:KD * NE].rearrange(
            "p (k e) -> p k e", k=KD)
        idx = sb("idx", [P, 2, 8], U32)

        def pcol(name, i=0, n=1):
            return par[:, PC[name] + i:PC[name] + i + n]

        def over(v, n):
            return v.unsqueeze(2).to_broadcast([v.shape[0], v.shape[1], n])

        chunk_in = [sem(f"chunk_in{i}") for i in range(RING)]
        expert_in = [[sem(f"expert_in{o}_{j}") for j in range(PER_EXPERT)] for o in range(2)]
        S = {}

        def S_(names):
            for n in names.split():
                S[n] = sem(n)

        S_("chunk_used x_in par_in gatew_in mrow_in kctx_in vctx_in cinit_in rpb_in bgu_in router_in bdn_in")
        S_("ones_made consts_made pads_made squared ssq var root cond_sig cond_ready mod_kept mod_turned "
           "mod_made h_ready bias_turned bias_ready")
        S_("block_made proj_kept gates_summed gates_kept cg_sig glu_done f_abs f_exp f_log rows_ready w_ready "
           "km_scaled cols_turned cols_kept em_ready conv_step conv_sum conv_sq conv_sqsum conv_var conv_root "
           "conv_lin conv_sig yc_ready va_turned va_kept v_turned v_kept")
        S_("scored exp_in exp_done probs_ready probs_turned pt_kept attended att_kept")
        S_("spread decayed keyed ptm_ready summed inter_made inter_kept kw_ready state_made state_kept ns_made "
           "hm_var hm_root hm_ready hm_turned om_sig ym_ready")
        S_("gate_made merge_made gate_sig merge_read out_made mixed wrs_ready shift_summed brs_ready raw_logits "
           "lt_ready h2_scaled h2_first h2_last h2_turned h2_kept logits_made top_made top_exp picked_made gm_made "
           "ranked np_made before_made past_made tab_summed table_made ")
        S_("sel_ready esel_ready selg_ready biased gathered gath_kept xg_turned xg_ready glu_ready sig_ready act_ready "
           "act_turned actt_kept selt_turned selt_kept y_kept scattered acc_kept acc_turned y_ready")
        S_("acc_copied dve_step act_step pool_step dve_pass kv_stored state_stored y_stored")

        def linker(eng, name):
            n = [0]

            def link(ins):
                n[0] += 1
                ins.then_inc(S[name], 1)
                eng.wait_ge(S[name], n[0])
            return link

        def slot_of(c):
            return (c - N_TRUNK) % RING

        def arrived(eng, c):
            eng.wait_ge(chunk_in[slot_of(c)], 16 * (c // RING + 1))

        def expert_slot(e, j):
            return (e * PER_EXPERT + j) % EXPERT_RING

        def late_bank(t):
            return bank[2 + t % 2][:, 0:TOK]

        def turn_h_bank(half, s):
            return bank[4 + (2 * half + s) % 3]

        def unit_bank(u):
            return bank[1 + u % 2][:, 0:TOK]

        def gate_summed(eng, u):
            if u % 4 == 3:
                eng.wait_ge(S["chunk_used"], C_MERGE + 3 * (u // 8) + (u % 8) // 4 + 1)
            else:
                eng.wait_ge(S["gate_made"], 3 * (u // 4) + u % 4 + 1)

        def merge_summed(eng, u):
            if u % 8 == 7:
                eng.wait_ge(S["chunk_used"], C_MERGE + 3 * (u // 8 + 1))
            else:
                eng.wait_ge(S["merge_made"], 7 * (u // 8) + u % 8 + 1)

        def table(eng, at, lo, hi):
            return eng.value_load(tab[0:1, bass.ds(at, 1)], min_val=lo, max_val=hi)

        block = ctx.enter_context(nc.Block())

        @block.sync
        def _(sp):
            sp.dma_start(x[:, :, :], x_t).then_inc(S["x_in"], 16)
            sp.dma_start(par[:, :], params).then_inc(S["par_in"], 16)
            for c in range(RING - 1):
                sp.dma_start(ring[:, slot_of(c), :], trunk_w[c]).then_inc(chunk_in[slot_of(c)], 16)
            sp.dma_start(wgate[:, :, :], w_gate).then_inc(S["gatew_in"], 16)
            sp.dma_start(bgate[:, :], b_gate).then_inc(S["mrow_in"], 16)
            sp.dma_start(minit[:, :], m_init).then_inc(S["mrow_in"], 16)
            for r in range(2):
                for rk in range(2):
                    at = (rk - r + WIN_ROWS - 1) * RPB_COLS + WIN_COLS - 1 - (GRID_W - 1)
                    sp.dma_start(abias[r * GRID_W:(r + 1) * GRID_W, :, rk * GRID_W:(rk + 1) * GRID_W],
                                  bass.AP(rpb.tensor, at, [[1, GRID_W], [RPB_ROWS * RPB_COLS, NH], [1, GRID_W]])
                                  ).then_inc(S["rpb_in"], 16)
            sp.dma_start(kctx[:, :, :], k_ctx_t).then_inc(S["kctx_in"], 16)
            sp.dma_start(vctx[:, :], v_ctx).then_inc(S["vctx_in"], 16)
            sp.dma_start(cinit[:, :, :, :], c_init_t).then_inc(S["cinit_in"], 16)
            sp.dma_start(ring[:, slot_of(RING - 1), :], trunk_w[RING - 1]).then_inc(chunk_in[slot_of(RING - 1)], 16)
            rounds = N_TRUNK // RING
            with sp.Fori(1, rounds) as r:
                for s in range(RING):
                    sp.wait_ge(S["chunk_used"], r * RING + (s + 1 - RING))
                    sp.dma_start(ring[:, slot_of(s), :], trunk_w[bass.ds(r * RING + s, 1)].rearrange(
                        "o p n -> (o p) n")).then_inc(chunk_in[slot_of(s)], 16)
            for c in range(rounds * RING, N_TRUNK):
                sp.wait_ge(S["chunk_used"], c - RING + 1)
                sp.dma_start(ring[:, slot_of(c), :], trunk_w[c]).then_inc(chunk_in[slot_of(c)], 16)

            def load_expert(e, i, j):
                k = KD // (GU_CHUNKS if j < GU_CHUNKS else DN_CHUNKS)
                w, row = (w_gu, j * k * P) if j < GU_CHUNKS else (w_down, (j - GU_CHUNKS) * k * P)
                slot = expert_slot(i, j)
                sp.dma_start(expert_ring[:, slot * CHUNK:(slot + 1) * CHUNK].rearrange("p (k n) -> p k n", k=k),
                             w[bass.ds(e, 1), row:row + k * P, :].rearrange("o (k p) n -> p (o k) n", p=P)
                             ).then_inc(expert_in[i % 2][j], 16)

            for j in range(PER_EXPERT):
                sp.wait_ge(S["chunk_used"], N_TRUNK - RING + j + 1)
                load_expert(0, 0, j)
            sp.dma_start(bgu, b_gu).then_inc(S["bgu_in"], 16)
            sp.wait_ge(S["merge_read"], 3 * KD)
            for j in range(AHEAD):
                load_expert(1, 1, j)

            sp.wait_ge(S["table_made"], 1)

            def later_expert(e, i, begin=0):
                passes = {j < AHEAD: table(sp, e + (T_BEFORE - (j < AHEAD)), 1, MAX_PASS)
                          for j in (range(begin, PER_EXPERT, PER_EXPERT - 1) if begin < AHEAD else (begin,))}
                for j in range(begin, PER_EXPERT):
                    used = j - AHEAD + 1 - PER_EXPERT * (j >= AHEAD)
                    sp.wait_ge(S["chunk_used"], passes[j < AHEAD] * PER_EXPERT + (N_TRUNK + used))
                    load_expert(e, i, j)

            later_expert(1, 1, begin=AHEAD)
            for e in range(2, TURN):
                later_expert(e, e)
            with sp.Fori(1, NE // TURN) as turn:
                for i in range(TURN):
                    later_expert(turn * TURN + i, i)

        @block.gpsimd
        def _(pool):
            link = linker(pool, "pool_step")
            link(pool.memset(ident[:, :], 0.0))
            link(pool.affine_select(out=ident[:, :], in_=ident[:, :], compare_op=ALU.not_equal, fill=1.0,
                                    base=0, pattern=[[-1, P]], channel_multiplier=1))
            link(pool.memset(stack[:, :], 0.0))
            for q in range(P // NE):
                link(pool.affine_select(out=stack[:, :], in_=stack[:, :], compare_op=ALU.not_equal, fill=1.0,
                                        base=q * NE, pattern=[[1, NE]], channel_multiplier=-1))
            link(pool.memset(mirror[:, :], 0.0))
            for r in range(2):
                link(pool.affine_select(out=mirror[:, :], in_=mirror[:, :], compare_op=ALU.not_equal, fill=1.0,
                                        base=-(2 * r * GRID_W + GRID_W - 1), pattern=[[1, P]], channel_multiplier=1))
            link(pool.memset(strict[:, :], 1.0))
            link(pool.affine_select(out=strict[:, :], in_=strict[:, :], compare_op=ALU.is_gt, fill=0.0,
                                    base=0, pattern=[[1, P]], channel_multiplier=-1))
            link(pool.memset(selrow[:, :, :], 0.0))
            link(pool.affine_select(out=selrow[:, :, :], in_=selrow[:, :, :], compare_op=ALU.not_equal, fill=1.0,
                                    base=0, pattern=[[-1, MH], [0, P]], channel_multiplier=1))
            link(pool.memset(dmask[:, :, :, :], 0.0))
            for d, sign in ((0, 1), (1, -1)):
                link(pool.affine_select(out=dmask[:, d, :, :], in_=dmask[:, d, :, :], compare_op=ALU.is_ge,
                                        fill=FAR, base=0, pattern=[[0, 2], [sign, L]], channel_multiplier=-sign))
            link(pool.memset(amask[:, :], 0.0))
            half = WIN_COLS // 2
            for r in range(2):
                m = amask[r * GRID_W:(r + 1) * GRID_W, :].rearrange("p (r c) -> p r c", r=2)
                low, high = m[:, :, 0:GRID_W - WIN_COLS], m[:, :, WIN_COLS:GRID_W]
                link(pool.affine_select(out=low, in_=low, compare_op=ALU.is_ge, fill=FAR, base=half,
                                        pattern=[[0, 2], [1, GRID_W - WIN_COLS]], channel_multiplier=-1))
                link(pool.affine_select(out=high, in_=high, compare_op=ALU.is_ge, fill=FAR,
                                        base=half - 1 - WIN_COLS,
                                        pattern=[[0, 2], [-1, GRID_W - WIN_COLS]], channel_multiplier=1))
            pool.iota(iota[:, :], pattern=[[1, TOK + 1]], base=0, channel_multiplier=0,
                      allow_small_or_imprecise_dtypes=True).then_inc(S["consts_made"], 1)

        @block.scalar
        def _(act):
            link = linker(act, "act_step")

            def func(out, in_, f, **kw):
                return act.activation(out, in_, f, **kw)

            def norm_root(n):
                act.wait_ge(S["var"], n)
                func(rstd[:, :], rstd[:, :], ACT.Sqrt).then_inc(S["root"], 1)

            def square(t):
                func(h[:, 2 * t:2 * t + 2, :], x[:, 2 * t:2 * t + 2, :], ACT.Square).then_inc(S["squared"], 1)

            act.wait_ge(S["x_in"], 16)
            for t in range(4):
                square(t)
            act.wait_ge(S["par_in"], 16)
            act.wait_ge(S["pads_made"], 3)
            cond_in = pcol("cond", 0, 2 * KD).rearrange("p (k s) -> p k s", k=KD)
            func(cond[:, :, 0:2], cond_in, ACT.Sigmoid).then_inc(S["cond_sig"], 1)
            norm_root(1)

            def keep_mod(g):
                act.wait_ge(S["chunk_used"], C_MOD[g][-1] + 1)
                if g == 2:
                    act.wait_ge(S["mod_turned"], 1)
                func(mod_rows[g], mod_bank[g][:, :], ACT.Copy).then_inc(S["mod_kept"], 1)

            keep_mod(0)

            def keep_proj(i):
                act.wait_ge(S["chunk_used"], C_PROJ[i] + 1)
                for b in range(4):
                    func(z[:, 4 * i + b, :], bank[2 * (i % 2) + b // 2][:, (b % 2) * TOK:(b % 2 + 1) * TOK],
                         ACT.Identity, bias=pcol("b_in", 4 * i + b)).then_inc(S["proj_kept"], 1)

            keep_proj(0)
            keep_proj(1)
            act.wait_ge(S["proj_kept"], 8)
            func(zblocks("cg"), zblocks("cg"), ACT.Sigmoid).then_inc(S["cg_sig"], 1)
            act.wait_ge(S["gates_summed"], 1)
            act.wait_ge(S["mrow_in"], 32)
            for q in range(4):
                func(gates[:, q, :], bank[6][32 * q:32 * q + MH, 0:TOK], ACT.Identity,
                     bias=bgate[:, q:q + 1]).then_inc(S["gates_kept"], 1)
            act.wait_ge(S["f_abs"], 1)
            func(rows["g"], rows["g"], ACT.Exp, scale=-1.0).then_inc(S["f_exp"], 1)
            act.wait_ge(S["f_exp"], 1)
            func(rows["g"], rows["g"], ACT.Ln, bias=1.0).then_inc(S["f_log"], 1)
            act.wait_ge(S["rows_ready"], 1)
            for d in range(2):
                func(rows["w"][:, d, :], negm[:, d, L:TOK], ACT.Exp, bias=minit[:, d:d + 1]
                     ).then_inc(S["w_ready"], 1)
            keep_proj(2)
            keep_mod(1)
            keep_proj(3)
            keep_proj(4)
            keep_mod(2)
            act.wait_ge(S["proj_kept"], 4 * EARLY)
            act.dma_start(k_new_t, z[:, Z["ka"]:Z["ka"] + 4, 0:L]).then_inc(S["kv_stored"], 16)
            act.dma_start(v_new_t, z[:, Z["va"]:Z["va"] + 4, 0:L]).then_inc(S["kv_stored"], 16)
            def late_block(t):
                if t % 4 == 3:
                    act.wait_ge(S["chunk_used"], C_PROJ[EARLY + t // 4] + 1)
                else:
                    act.wait_ge(S["block_made"], 3 * (t // 4) + t % 4 + 1)
                func(z[:, 4 * EARLY + t, :], late_bank(t), ACT.Identity, bias=pcol("b_in", 4 * EARLY + t)
                     ).then_inc(S["proj_kept"], 1)

            def exponentials(i):
                act.wait_ge(S["exp_in"], i + 1)
                if i >= 2:
                    act.wait_ge(S["probs_turned"], i - 1)
                b = bank[4 + i % 2]
                func(att["p"][:, i % 2, 0:L], b[:, 0:L], ACT.Exp, scale=ATT_SCALE, bias=sm["aneg"][:, i, 0:1],
                     accum_out=sm["asum"][:, i, 0:1]).then_inc(S["exp_done"], 1)
                func(att["p"][:, i % 2, L:3 * L], b[:, L:3 * L], ACT.Exp, scale=ATT_SCALE,
                     bias=sm["aneg"][:, i, 1:2], accum_out=sm["asum"][:, i, 1:2]).then_inc(S["exp_done"], 1)

            late_block(0)
            act.wait_ge(S["va_turned"], 1)
            act.wait_ge(S["glu_done"], 1)
            for s in range(2):
                func(va_tok[:, s, :], bank[6 + s][:, :], ACT.Copy).then_inc(S["va_kept"], 1)
            exponentials(0)
            for i in range(NH):
                late_block(2 * i + 1)
                if i < NH - 1:
                    exponentials(i + 1)
                    late_block(2 * i + 2)
            act.wait_ge(S["proj_kept"], 4 * len(PROJ))
            func(zblocks("km"), zblocks("km"), ACT.Copy, scale=M_SCALE).then_inc(S["km_scaled"], 1)
            func(zblocks("om"), zblocks("om"), ACT.Sigmoid).then_inc(S["om_sig"], 1)

            def merge_gate(u):
                gate_summed(act, u)
                if u >= 8:
                    act.wait_ge(S["merge_read"], u - 7)
                func(sig_gate(u), unit_bank(u), ACT.Sigmoid, bias=pcol("b_in", 36 + u)
                     ).then_inc(S["gate_sig"], 1)

            act.wait_ge(S["v_turned"], 1)
            for s in range(2):
                func(vmt[:, s, :, 0:P], bank[2 + s][:, :].rearrange("p (a b) -> p a b", a=MH), ACT.Copy
                     ).then_inc(S["v_kept"], 1)
            act.wait_ge(S["kv_stored"], 32)
            act.wait_ge(S["attended"], NH)
            merge_gate(0)
            act.wait_ge(S["v_turned"], 2)
            func(kmt[:, :, :], bank[7][:, :].rearrange("p (a b) -> p a b", a=MH), ACT.Copy
                 ).then_inc(S["v_kept"], 1)
            act.wait_ge(S["cols_turned"], 1)
            func(sm["cols"], bank[6][:, 0:40].rearrange("p (a b) -> p a b", a=10), ACT.Copy
                 ).then_inc(S["cols_kept"], 1)
            merge_gate(1)
            act.wait_ge(S["cols_kept"], 1)
            func(sm["em"], sm["cols"][:, 4:8, :], ACT.Exp, scale=-1.0).then_inc(S["em_ready"], 1)
            act.wait_ge(S["conv_var"], 1)
            func(rstd[:, :], rstd[:, :], ACT.Sqrt).then_inc(S["conv_root"], 1)
            merge_gate(2)
            merge_gate(3)

            act.wait_ge(S["att_kept"], NH // 2)
            act.wait_ge(S["mod_turned"], 3)
            for i in range(MH):
                act.wait_ge(S["spread"], i + 1)
                if i:
                    act.wait_ge(S["kw_ready"], i)
                for q in range(4):
                    func(ml["decay"][:, q, :], bank[4][:, q * L:(q + 1) * L], ACT.Exp,
                         bias=sm["cols"][:, q, i:i + 1]).then_inc(S["decayed"], 1)
                act.wait_ge(S["inter_made"], i + 1)
                if i:
                    act.wait_ge(S["ns_made"], 2 * i)
                for d in range(2):
                    func(ml["inter"][:, d, 1, :], bank[0][:, d * (P + 1):(d + 1) * (P + 1)], ACT.Copy,
                         scale=sm["cols"][:, 8 + d, i:i + 1]).then_inc(S["inter_kept"], 1)
                for u in GATES_AHEAD[i]:
                    merge_gate(u)
                if i == 0:
                    act.wait_ge(S["conv_lin"], 1)
                    func(conv_sq, acc, ACT.Sigmoid).then_inc(S["conv_sig"], 1)
                act.wait_ge(S["state_made"], i + 1)
                func(c_out[:, i, :, :], bank[3][:, 0:2 * P].rearrange("p (a b) -> p a b", a=2), ACT.Copy
                     ).then_inc(S["state_kept"], 1)
                func(n_out[:, i * P:(i + 1) * P], bank[3][0:2, TOK:TOK + P], ACT.Copy).then_inc(S["state_kept"], 1)
                for u in GATES_AFTER[i]:
                    merge_gate(u)
            act.wait_ge(S["state_kept"], 2 * MH)
            act.dma_start(c_new, c_out).then_inc(S["state_stored"], 16)
            act.dma_start(n_new, n_out).then_inc(S["state_stored"], 16)
            act.dma_start(m_new, sm["mlast"]).then_inc(S["state_stored"], 16)
            merge_gate(8)
            merge_gate(9)
            act.wait_ge(S["hm_var"], 1)
            func(sm["hvar"], sm["hvar"], ACT.Sqrt).then_inc(S["hm_root"], 1)
            act.dma_start(wrt, w_router).then_inc(S["router_in"], 16)
            act.dma_start(rt["brt"], b_router).then_inc(S["router_in"], 16)
            for u in range(10, 24):
                merge_gate(u)
            act.wait_ge(S["state_stored"], 48)
            act.dma_start(bdn, b_down).then_inc(S["bdn_in"], 16)

            act.wait_ge(S["hm_ready"], 1)
            func(sm["hvar"], sm["hvar"], ACT.Sqrt)
            for t in range(4):
                act.wait_ge(S["mixed"], t + 1)
                square(t)
            norm_root(2)
            func(sm["em"], sm["em"], ACT.Exp, scale=-1.0)
            for k in range(ACT_BLOCKS):
                act.wait_ge(S["h2_scaled"], k // 4 + 1)
                for s in range(2):
                    hs = h[:, k, s * L:(s + 1) * L]
                    ins = func(hs, hs, ACT.Identity, scale=gain[:, 1, k, s:s + 1], bias=mod[:, 24 + k, s:s + 1])
                ins.then_inc(S["h2_first"], 1)
            for half in range(2):
                for s in range(2):
                    act.wait_ge(S["h2_turned"], 2 * half + s + 1)
                    func(mo["h_tok"][:, s, half * 512:(half + 1) * 512], turn_h_bank(half, s)[:, :], ACT.Copy
                         ).then_inc(S["h2_kept"], 1)
            act.wait_ge(S["top_made"], 1)
            for s in range(2):
                func(rt["ex"][:, s, :], rt["top"][:, s, 0:TOPK], ACT.Exp, bias=rt["neg"][:, s:s + 1],
                     accum_out=rt["sum"][:, s:s + 1]).then_inc(S["top_exp"], 1)

            def keep(out, in_, name):
                func(out, in_, ACT.Copy).then_inc(S[name], 1)

            def by_half(b):
                return bank[b][:, :].rearrange("p (j h c) -> p j h c", j=4, h=2)

            act.wait_ge(S["gathered"], 1)
            keep(mo["gath"], bank[4][:, :], "gath_kept")
            act.wait_ge(S["xg_turned"], 1)
            keep(mo["xg"], by_half(4), "xg_ready")
            act.wait_ge(S["table_made"], 1)
            n_pass = table(act, T_ALL, NE, MAX_PASS)
            with act.Fori(0, n_pass) as n:
                func(sm["hvar"], sm["hvar"], ACT.Sigmoid)
                act.wait_ge(S["gathered"], n + 2)
                keep(mo["gath"], bank[4][:, :], "gath_kept")
                act.wait_ge(S["glu_ready"], n + 1)
                func(mo["sig"], mo["glu"], ACT.Sigmoid, scale=ALPHA).then_inc(S["sig_ready"], 1)
                act.wait_ge(S["xg_turned"], n + 2)
                keep(mo["xg"], by_half(4), "xg_ready")
                act.wait_ge(S["act_turned"], n + 1)
                keep(mo["actt"], by_half(5), "actt_kept")
                act.wait_ge(S["selt_turned"], n + 1)
                keep(mo["selt"], bank[6][:, :].rearrange("p (s h t) -> p s h t", s=2, h=2), "selt_kept")
                act.wait_ge(S["chunk_used"], n * PER_EXPERT + (N_TRUNK + PER_EXPERT))
                keep(mo["y"], bank[7][:, :], "y_kept")

            func(sm["hvar"], sm["hvar"], ACT.Sqrt)
            for f in range(2):
                act.wait_ge(S["scattered"], 2 * f + 1)
                func(mo["h_tok"][:, 0, f * 512:(f + 1) * 512], bank[f][:, :], ACT.Copy).then_inc(S["acc_kept"], 1)
            for t in range(4):
                act.wait_ge(S["mixed"], 4 + t + 1)
                square(t)
            norm_root(3)
            for t in range(4):
                act.wait_ge(S["y_ready"], 2 * t + 2)
                act.dma_start(y_t[:, 2 * t:2 * t + 2, :], x[:, 2 * t:2 * t + 2, :]).then_inc(S["y_stored"], 16)
            act.wait_ge(S["y_stored"], 64)
            act.wait_ge(S["kv_stored"], 32)
            act.wait_ge(S["state_stored"], 48)

        @block.vector
        def _(dve):
            link = linker(dve, "dve_step")

            def rstd_from(src, count, eps, ready, root, n):
                dve.tensor_scalar(rstd[:, :], src, 1.0 / count, eps, ALU.mult, ALU.add).then_inc(S[ready], 1)
                dve.wait_ge(S[root], n)
                link(dve.reciprocal(rstd[:, :], rstd[:, :]))

            def mod_group(g):
                dve.wait_ge(S["mod_turned"], g + 1)
                made = turn_bank[g][:, :].rearrange("p (j q c) -> p j q c", j=4, q=4)[:, :, :, 0:2]
                to = mod[:, 16 * g:16 * g + 16, :].rearrange("p (q j) s -> p j q s", q=4)
                bias = pcol("b_mod", 16 * g, 16).rearrange("p (q j) -> p j q", q=4)
                for j in range(4):
                    ins = dve.tensor_tensor(to[:, j, :, :], made[:, j, :, :], over(bias[:, j, :], 2), ALU.add)
                    ins.then_inc(S["mod_made"], 1)
                dve.wait_ge(S["mod_made"], 4 * g + 4)
                if g != 1:
                    i = g // 2
                    link(dve.scalar_tensor_tensor(gain[:, i, :, :], mod[:, 24 * i + 8:24 * i + 16, :], 1.0,
                                                  over(pcol(("norm1", "norm2")[i], 0, KD), 2), ALU.add, ALU.mult))

            def first_norm():
                dve.wait_ge(S["ssq"], 1)
                rstd_from(bank[4][:, 0:TOK], D, RMS_EPS, "var", "root", 1)
                link(dve.tensor_tensor(h[:, :, :], x[:, :, :],
                                       rstd[:, :].unsqueeze(1).to_broadcast([P, KD, TOK]), ALU.mult))
                mod_group(0)
                for k in range(KD):
                    for s in range(2):
                        modulate(0, k, s).then_inc(S["h_ready"], 1)

            def modulate(which, k, s):
                hs = h[:, k, s * L:(s + 1) * L]
                return dve.tensor_scalar(hs, hs, gain[:, which, k, s:s + 1], mod[:, 24 * which + k, s:s + 1],
                                         ALU.mult, ALU.add)

            dve.memset(ones[:, :], 1.0).then_inc(S["ones_made"], 1)
            dve.memset(apad[:, :, :, :], 0.0).then_inc(S["pads_made"], 1)
            dve.memset(vmt[:, :, :, P:P + 1], 1.0).then_inc(S["pads_made"], 1)
            dve.memset(cond, 0.0).then_inc(S["pads_made"], 1)
            dve.wait_ge(S["cond_sig"], 1)
            dve.tensor_tensor(cond[:, :, 0:2], cond[:, :, 0:2],
                              pcol("cond", 0, 2 * KD).rearrange("p (k s) -> p k s", k=KD), ALU.mult
                              ).then_inc(S["cond_ready"], 1)
            first_norm()
            dve.wait_ge(S["bias_turned"], 1)
            for q in range(2):
                dve.scalar_tensor_tensor(abias[:, 4 * q:4 * q + 4, :],
                                         bank[6 + q][:, :].rearrange("p (a b) -> p a b", a=4), 1.0 / ATT_SCALE,
                                         amask[:, :].unsqueeze(1).to_broadcast([P, 4, L]), ALU.mult, ALU.add
                                         ).then_inc(S["bias_ready"], 1)

            dve.wait_ge(S["cg_sig"], 1)
            dve.wait_ge(S["pads_made"], 1)
            dve.tensor_tensor(apad[:, :, :, PAD:PAD + L], zblocks("cu").rearrange("p k (s t) -> p k s t", s=2),
                              zblocks("cg").rearrange("p k (s t) -> p k s t", s=2), ALU.mult
                              ).then_inc(S["glu_done"], 1)

            dve.wait_ge(S["gates_kept"], 4)
            dve.scalar_tensor_tensor(rows["g"], gates[:, 1:4:2, :], -1.0, gates[:, 1:4:2, :], ALU.mult, ALU.max
                                     ).then_inc(S["f_abs"], 1)
            dve.wait_ge(S["f_log"], 1)
            link(dve.scalar_tensor_tensor(rows["g"], gates[:, 1:4:2, :], 0.0, rows["g"], ALU.min, ALU.subtract))

            def along(v, d, s):
                v = v[:, d, s * L:(s + 1) * L]
                return v if d == 0 else v[:, ::-1]

            dve.wait_ge(S["ones_made"], 1)
            for d in range(2):
                for s in range(2):
                    link(dve.tensor_tensor_scan(along(rows["b"], d, s), ones[0:MH, :], along(rows["g"], d, s), 0.0,
                                                ALU.mult, ALU.add))
            link(dve.tensor_tensor(rows["g"], gates[:, 0:4:2, :], rows["b"], ALU.subtract))
            for d in range(2):
                for s in range(2):
                    g = along(rows["g"], d, s)
                    link(dve.tensor_tensor_scan(along(negm, d, s), g, g,
                                                minit[:, d:d + 1] if s else LOWEST, ALU.max, ALU.max))
            link(dve.tensor_tensor(rows["b"], rows["b"], negm, ALU.add))
            dve.tensor_scalar(negm, negm, -1.0, None, ALU.mult).then_inc(S["rows_ready"], 1)
            link(dve.tensor_copy(sm["mlast"][:, 0:1], rows["b"][:, 0, L - 1:L]))
            link(dve.tensor_copy(sm["mlast"][:, 1:2], rows["b"][:, 1, 0:1]))

            dve.wait_ge(S["glu_done"], 1)

            def conv_in(b, w):
                return apad[:, b, :, bass.ds(w, L)]

            accs = [acc[:, b, :].rearrange("p (s t) -> p s t", s=2) for b in range(4)]
            for b in range(4):
                dve.tensor_scalar(accs[b], conv_in(b, 0), pcol("w_dw", b * CONV_W), pcol("b_dw", b),
                                  ALU.mult, ALU.add).then_inc(S["conv_step"], 1)
            with dve.Fori(1, CONV_W) as w:
                for b in range(4):
                    dve.wait_ge(S["conv_step"], w * 4 + (b + 1 - 4))
                    tap = par[:, bass.ds(w + (PC["w_dw"] + b * CONV_W), 1)]
                    dve.scalar_tensor_tensor(accs[b], conv_in(b, w), tap, accs[b], ALU.mult, ALU.add
                                             ).then_inc(S["conv_step"], 1)
            def att_scores(i):
                dve.wait_ge(S["scored"], i + 1)
                b = bank[4 + i % 2]
                link(dve.tensor_tensor(b[:, L:2 * L], b[:, L:2 * L], abias[:, i, :], ALU.add))
                dve.tensor_reduce(sm["amax"][:, i, 0:1], b[:, 0:L], AX, ALU.max)
                link(dve.tensor_reduce(sm["amax"][:, i, 1:2], b[:, L:3 * L], AX, ALU.max))
                dve.tensor_scalar(sm["aneg"][:, i, :], sm["amax"][:, i, :], -ATT_SCALE, None, ALU.mult
                                  ).then_inc(S["exp_in"], 1)

            def att_probs(i):
                dve.wait_ge(S["exp_done"], 2 * i + 2)
                link(dve.reciprocal(sm["arec"][:, i, :], sm["asum"][:, i, :]))
                p = att["p"][:, i % 2, :]
                link(dve.tensor_scalar(p[:, 0:L], p[:, 0:L], sm["arec"][:, i, 0:1], None, ALU.mult))
                dve.tensor_scalar(p[:, L:3 * L], p[:, L:3 * L], sm["arec"][:, i, 1:2], None, ALU.mult
                                  ).then_inc(S["probs_ready"], 1)

            def att_turned(i):
                dve.wait_ge(S["probs_turned"], i + 1)
                if i >= 2:
                    dve.wait_ge(S["attended"], i - 1)
                dve.tensor_copy(att["pt"][:, i % 2, :], bank[6 + i % 2][:, 0:3 * L]).then_inc(S["pt_kept"], 1)
                if i % 2:
                    dve.wait_ge(S["attended"], i + 1)
                    dve.tensor_copy(branch_out["a"][:, i // 2, :], bank[(i // 2) % 2][:, 0:TOK]
                                    ).then_inc(S["att_kept"], 1)

            dve.wait_ge(S["bias_ready"], 2)
            att_scores(0)
            for i in range(NH):
                att_probs(i)
                if i < NH - 1:
                    att_scores(i + 1)
                att_turned(i)

            dve.wait_ge(S["conv_sum"], 1)
            link(dve.tensor_scalar(rstd[:, :], bank[4][:, 0:TOK], -1.0 / (4 * P), None, ALU.mult))
            link(dve.tensor_tensor(acc, acc, rstd[:, :].unsqueeze(1).to_broadcast([P, 4, TOK]), ALU.add))
            dve.tensor_tensor(conv_sq, acc, acc, ALU.mult).then_inc(S["conv_sq"], 1)
            dve.wait_ge(S["conv_sqsum"], 1)
            rstd_from(bank[4][:, TOK:2 * TOK], 4 * P, LN_EPS, "conv_var", "conv_root", 1)
            link(dve.tensor_tensor(acc, acc, rstd[:, :].unsqueeze(1).to_broadcast([P, 4, TOK]), ALU.mult))
            for b in range(4):
                dve.tensor_scalar(acc[:, b, :], acc[:, b, :], pcol("cln_g", b), pcol("cln_b", b),
                                  ALU.mult, ALU.add).then_inc(S["conv_lin"] if b == 3 else S["conv_step"], 1)
            mod_group(1)
            mod_group(2)

            def merge(u):
                b = u % 8
                dve.wait_ge(S["gate_sig"], u + 1)
                merge_summed(dve, u)
                sg, pr = sig_gate(u), unit_bank(u)
                if u < 8:
                    dve.tensor_tensor(merged[:, b, :], sg, pr, ALU.mult).then_inc(S["merge_read"], 1)
                else:
                    link(dve.tensor_tensor(sg, sg, pr, ALU.mult))
                    dve.tensor_tensor(merged[:, b, :], merged[:, b, :], sg, ALU.add).then_inc(S["merge_read"], 1)

            km_tok = kmt[:, :, :]
            dve.wait_ge(S["mod_turned"], 3)
            dve.memset(ml["inter"][:, :, 0, :], 0.0).then_inc(S["pads_made"], 1)
            dve.wait_ge(S["em_ready"], 1)
            dve.wait_ge(S["v_kept"], 3)
            for i in range(MH):
                dve.wait_ge(S["decayed"], 4 * i + 4)
                dve.wait_ge(S["keyed"], i + 1)
                if i:
                    dve.wait_ge(S["summed"], i)
                keys = bank[5][:, 0:TOK].unsqueeze(1).to_broadcast([P, 2, TOK])
                dve.tensor_tensor(ml["pt"].rearrange("p (d s) t -> p d (s t)", d=2), keys,
                                  ml["decay"].rearrange("p (d s) t -> p d (s t)", d=2), ALU.mult
                                  ).then_inc(S["ptm_ready"], 1)
                link(dve.tensor_copy(sm["wsrc"][:, i, 0:1], ml["decay"][:, 0, L - 1:L]))
                link(dve.tensor_copy(sm["wsrc"][:, i, 1:2], ml["decay"][:, 2, 0:1]))
                if i:
                    dve.wait_ge(S["state_made"], i)
                link(dve.tensor_scalar(ml["kw"][:, 0, :], km_tok[:, i, :], sm["wsrc"][:, i, 0:1], None, ALU.mult))
                dve.tensor_scalar(ml["kw"][:, 1, :], km_tok[:, i, :], sm["wsrc"][:, i, 1:2], None, ALU.mult
                                  ).then_inc(S["kw_ready"], 1)
                if i == 0:
                    dve.wait_ge(S["conv_sig"], 1)
                    dve.tensor_tensor(acc, acc, conv_sq, ALU.mult).then_inc(S["yc_ready"], 1)
                    dve.wait_ge(S["yc_ready"], 1)
                for u in MERGES_AHEAD[i]:
                    merge(u)
                dve.wait_ge(S["summed"], i + 1)
                dve.wait_ge(S["inter_kept"], 2 * i + 2)
                for d in range(2):
                    dve.tensor_tensor(ml["ns"][:, d, :], bank[6 + d][:, 0:2 * (P + 1)],
                                      ml["inter"][:, d, :, :].rearrange("p s c -> p (s c)"), ALU.add
                                      ).then_inc(S["ns_made"], 1)
                dve.wait_ge(S["ns_made"], 2 * i + 2)
                ns = ml["ns"].rearrange("p d (s c) -> p (d s) c", s=2)
                den = ns[:, :, P:P + 1].rearrange("p a b -> p (a b)")
                link(dve.scalar_tensor_tensor(sm["den"], den, -1.0, den, ALU.mult, ALU.max))
                link(dve.tensor_tensor(sm["den"], sm["den"], sm["em"][:, :, i:i + 1].rearrange("p a b -> p (a b)"),
                                       ALU.max))
                link(dve.reciprocal(sm["den"], sm["den"]))
                link(dve.tensor_tensor(ml["hd"], ns[:, :, 0:P], over(sm["den"], P), ALU.mult))
                link(dve.tensor_tensor(hm[:, :, i, :], ml["hd"][:, 0:2, :], ml["hd"][:, 2:4, :], ALU.add))
                for u in MERGES_AFTER[i]:
                    merge(u)
            hv = hm.rearrange("p s h d -> p (s h) d")
            sq = work[:, 0:2 * MH * P].rearrange("p (a d) -> p a d", a=2 * MH)
            link(dve.tensor_reduce(sm["hsum"], hv, AX, ALU.add))
            link(dve.tensor_scalar(sm["hsum"], sm["hsum"], -1.0 / P, None, ALU.mult))
            link(dve.tensor_tensor(hv, hv, over(sm["hsum"], P), ALU.add))
            link(dve.tensor_tensor(sq, hv, hv, ALU.mult))
            link(dve.tensor_reduce(sm["hvar"], sq, AX, ALU.add))
            dve.tensor_scalar(sm["hvar"], sm["hvar"], 1.0 / P, LN_EPS, ALU.mult, ALU.add).then_inc(S["hm_var"], 1)
            dve.wait_ge(S["hm_root"], 1)
            link(dve.reciprocal(sm["hvar"], sm["hvar"]))
            dve.tensor_tensor(hv, hv, over(sm["hvar"], P), ALU.mult).then_inc(S["hm_ready"], 1)
            dve.wait_ge(S["hm_turned"], 1)
            dve.wait_ge(S["om_sig"], 1)
            for i in range(MH):
                om = branch_out["m"][:, i, :]
                ins = dve.scalar_tensor_tensor(om, bank[4 + i // 2][:, (i % 2) * TOK:(i % 2 + 1) * TOK],
                                               pcol("mnorm", i), om, ALU.mult, ALU.mult)
            ins.then_inc(S["ym_ready"], 1)

            for u in range(8, 24):
                merge(u)

            dve.wait_ge(S["router_in"], 32)
            for s in range(2):
                dve.tensor_tensor(rt["wrs"][:, s * KD:(s + 1) * KD, :], wrt, over(gain[:, 1, :, s], NE), ALU.mult
                                  ).then_inc(S["wrs_ready"], 1)
            dve.wait_ge(S["shift_summed"], 1)
            dve.tensor_tensor(rt["brs"], bank[6][0:1, 0:2 * NE].rearrange("p (s e) -> p s e", s=2),
                              rt["brt"].unsqueeze(1).to_broadcast([1, 2, NE]), ALU.add).then_inc(S["brs_ready"], 1)
            dve.memset(rt["gm"], 0.0)
            dve.memset(rt["posm"], 0.0)
            link(dve.memset(mo["selz"], 0.0))
            dve.memset(mo["selt"], 0.0).then_inc(S["selt_kept"], 1)
            dve.memset(mo["y"], 0.0).then_inc(S["y_kept"], 1)

            def add_gated(part, t):
                for k in range(2 * t, 2 * t + 2):
                    for s in range(2):
                        at = (k % 2) * TOK + s * L
                        ins = dve.scalar_tensor_tensor(x[:, k, s * L:(s + 1) * L], bank[4 + t][:, at:at + L],
                                                       mod[:, part + k, s:s + 1], x[:, k, s * L:(s + 1) * L],
                                                       ALU.mult, ALU.add)
                ins.then_inc(S["mixed"], 1)

            for t in range(4):
                if t % 2 == 0:
                    dve.wait_ge(S["out_made"], t // 2 + 1)
                else:
                    dve.wait_ge(S["chunk_used"], C_OUT + t // 2 + 1)
                add_gated(16, t)

            dve.wait_ge(S["ssq"], 2)
            rstd_from(bank[4][:, 0:TOK], D, RMS_EPS, "var", "root", 2)
            dve.wait_ge(S["raw_logits"], 1)
            dve.tensor_tensor(rt["lt"], bank[5][:, 0:TOK], rstd[:, :], ALU.mult).then_inc(S["lt_ready"], 1)
            dve.wait_ge(S["mixed"], 4)
            for half in range(2):
                dve.tensor_tensor(h[:, 4 * half:4 * half + 4, :], x[:, 4 * half:4 * half + 4, :],
                                  rstd[:, :].unsqueeze(1).to_broadcast([P, 4, TOK]), ALU.mult
                                  ).then_inc(S["h2_scaled"], 1)

            dve.wait_ge(S["logits_made"], 1)
            link(dve.tensor_copy(rt["lg"], bank[7][:, 0:2 * NE].rearrange("p (a b) -> p a b", a=2)))
            for s in range(2):
                ins = dve.max(rt["top"][:, s, :], rt["lg"][:, s, :])
            link(ins)
            for s in range(2):
                ins = dve.max_index(idx[:, s, :], rt["top"][:, s, :], rt["lg"][:, s, :])
            link(ins)
            link(dve.tensor_copy(rt["idxf"], idx[:, :, :]))
            for s in range(2):
                ins = dve.tensor_tensor(rt["oh"][:, TOPK * s:TOPK * s + TOPK, :],
                                        iota[:, 0:NE].unsqueeze(1).to_broadcast([P, TOPK, NE]),
                                        over(rt["idxf"][:, s, 0:TOPK], NE), ALU.is_equal)
            link(ins)
            for s in range(2):
                dve.tensor_reduce(rt["picked"][:, s, :], rt["oh"][:, TOPK * s:TOPK * s + TOPK, :].rearrange(
                    "p k e -> p e k"), AX, ALU.add).then_inc(S["picked_made"], 1)
            dve.tensor_scalar(rt["neg"], rt["top"][:, :, 0:1].rearrange("p a b -> p (a b)"), -1.0, None, ALU.mult
                              ).then_inc(S["top_made"], 1)
            dve.wait_ge(S["h2_scaled"], 2)
            for k in range(ACT_BLOCKS, KD):
                for s in range(2):
                    ins = modulate(1, k, s)
                ins.then_inc(S["h2_last"], 1)
            dve.wait_ge(S["ranked"], 1)
            dve.wait_ge(S["picked_made"], 2)
            link(dve.scalar_tensor_tensor(rt["posm"][:, :, 0:NE],
                                          bank[7][:, 64:64 + 2 * NE].rearrange("p (a b) -> p a b", a=2), 1.0,
                                          rt["picked"], ALU.add, ALU.mult))

            def select(e, base):
                for s in range(2):
                    dve.tensor_scalar(mo["sel"][:, s, :], iota[:, bass.ds(base + 1, SLOTS)],
                                      rt["posm"][:, s, bass.ds(e, 1)], None, ALU.is_equal
                                      ).then_inc(S["sel_ready"], 1)
                dve.tensor_copy(mo["esel"], ident[0:NE, bass.ds(e, 1)].to_broadcast([NE, SLOTS])
                                ).then_inc(S["esel_ready"], 1)

            select(0, 0)
            link(dve.tensor_scalar(rt["cmp"], iota[0:NE, SLOTS:TOK:SLOTS], bank[7][0:NE, 128:129], None, ALU.is_lt))
            link(dve.tensor_reduce(rt["np"], rt["cmp"], AX, ALU.add))
            dve.tensor_scalar(rt["np"], rt["np"], 1.0, None, ALU.add).then_inc(S["np_made"], 1)
            dve.wait_ge(S["before_made"], 1)
            link(dve.tensor_tensor(rt["pinc"], bank[7][0:NE, 129:130], rt["np"], ALU.add))
            dve.tensor_scalar(rt["past"], iota[0:NE, 0:MAX_PASS + 1], rt["pinc"], None, ALU.is_ge
                              ).then_inc(S["past_made"], 1)
            dve.wait_ge(S["top_exp"], 2)
            link(dve.reciprocal(rt["sum"], rt["sum"]))
            for s in range(2):
                ins = dve.tensor_scalar(rt["ex"][:, s, :], rt["ex"][:, s, :], rt["sum"][:, s:s + 1], None, ALU.mult)
            link(ins)
            for s in range(2):
                ins = dve.tensor_tensor(rt["ohg"][:, TOPK * s:TOPK * s + TOPK, :],
                                        rt["oh"][:, TOPK * s:TOPK * s + TOPK, :], over(rt["ex"][:, s, :], NE), ALU.mult)
            link(ins)
            for s in range(2):
                ins = dve.tensor_reduce(rt["gm"][:, s, 0:NE], rt["ohg"][:, TOPK * s:TOPK * s + TOPK, :].rearrange(
                    "p k e -> p e k"), AX, ALU.add)
            ins.then_inc(S["gm_made"], 1)
            dve.wait_ge(S["tab_summed"], 1)
            M1 = MAX_PASS + 1
            link(dve.tensor_copy(rt["tabf"], bank[7][0:1, 192:192 + N_TAB]))
            base = rt["tabf"][:, T_BASE:T_BASE + M1]
            link(dve.tensor_tensor(base, iota[0:1, 0:M1], base, ALU.subtract))
            link(dve.tensor_scalar(base, base, float(SLOTS), float(TOK - SLOTS), ALU.mult, ALU.min))
            dve.tensor_copy(tab[:, :], rt["tabf"]).then_inc(S["table_made"], 1)

            def gate_selected(n, e):
                dve.wait_ge(S["sel_ready"], n * 2 + 2)
                for s in range(2):
                    dve.tensor_scalar(mo["selz"][:, s, SLOTS:2 * SLOTS], mo["sel"][:, s, :],
                                      rt["gm"][:, s, bass.ds(e, 1)], None, ALU.mult).then_inc(S["selg_ready"], 1)

            dve.wait_ge(S["gm_made"], 1)
            gate_selected(0, 0)
            dve.wait_ge(S["table_made"], 1)
            n_pass = table(dve, T_ALL, NE, MAX_PASS)
            STEPS = 2
            with dve.Fori(0, n_pass) as n:
                dve.wait_ge(S["gathered"], n + 1)
                dve.wait_ge(S["selg_ready"], n * 2 + 2)
                dve.wait_ge(S["biased"], n + 1)
                e_next = table(dve, n + 1 + T_EXP, 0, NE)
                select(e_next, table(dve, n + 1 + T_BASE, 0, TOK - SLOTS))
                dve.wait_ge(S["chunk_used"], n * PER_EXPERT + (N_TRUNK + GU_CHUNKS))
                dve.tensor_scalar(mo["glu"], bank[5][:, :], LIMIT, None, ALU.min).then_inc(S["glu_ready"], 1)
                dve.tensor_scalar(mo["lin"], bank[6][:, :], LIMIT, -LIMIT, ALU.min, ALU.max
                                  ).then_inc(S["dve_pass"], 1)
                dve.wait_ge(S["sig_ready"], n + 1)
                dve.tensor_tensor(mo["sig"], mo["sig"], mo["glu"], ALU.mult).then_inc(S["dve_pass"], 1)
                dve.wait_ge(S["dve_pass"], n * STEPS + STEPS)
                dve.scalar_tensor_tensor(mo["act"], mo["lin"], 1.0, mo["sig"], ALU.add, ALU.mult
                                         ).then_inc(S["act_ready"], 1)
                dve.wait_ge(S["selt_turned"], n + 1)
                gate_selected(n + 1, e_next)

            for f in range(2):
                dve.wait_ge(S["scattered"], 2 * f + 2)
                dve.tensor_copy(mo["h_tok"][:, 1, f * 512:(f + 1) * 512], bank[2 + f][:, :]
                                ).then_inc(S["acc_copied"], 1)
            for t in range(4):
                dve.wait_ge(S["acc_turned"], t + 1)
                add_gated(40, t)
            dve.wait_ge(S["mixed"], 8)
            dve.wait_ge(S["ssq"], 3)
            rstd_from(bank[0][:, 0:TOK], D, RMS_EPS, "var", "root", 3)
            for k in range(KD):
                dve.scalar_tensor_tensor(x[:, k, :], x[:, k, :], pcol("final", k), rstd[:, :], ALU.mult, ALU.mult
                                         ).then_inc(S["y_ready"], 1)

        @block.tensor
        def _(pe):
            def norm_sum(n, to):
                for k in range(KD):
                    if k % 2 == 0:
                        pe.wait_ge(S["squared"], 4 * (n - 1) + k // 2 + 1)
                    ins = pe.matmul(to, ones[:, :], h[:, k, :], start=k == 0, stop=k == KD - 1)
                ins.then_inc(S["ssq"], 1)

            def trunk_chunk(c, k):
                return ring[:, slot_of(c), :].rearrange("p (k n) -> p k n", k=k)

            def product(c, b, src, to, h_blocks=False):
                w = trunk_chunk(c, KD)
                for k in range(KD):
                    if h_blocks:
                        pe.wait_ge(S["h_ready"], 2 * k + 2)
                    ins = pe.matmul(to, w[:, k, b * P:(b + 1) * P], src[:, k, :], start=k == 0, stop=k == KD - 1)
                return ins

            def mod_sum(c):
                g = [c in chunks for chunks in C_MOD].index(True)
                j = C_MOD[g].index(c)
                if g and j == 0:
                    pe.wait_ge(S["mod_kept"], 1)
                    pe.wait_ge(S["var"], 1)
                arrived(pe, c)
                w = trunk_chunk(c, 2)
                for i in range(2):
                    k = 2 * j + i
                    for q in range(4):
                        ins = pe.matmul(mod_bank[g][32 * q:32 * q + 32, :], cond[:, k, :],
                                        w[:, i, q * 512:(q + 1) * 512], start=k == 0, stop=k == KD - 1)
                ins.then_inc(S["chunk_used"], 1)

            def mod_turn(g):
                pe.wait_ge(S["mod_kept"], g + 1)
                for j in range(4):
                    ins = pe.transpose(turn_bank[g][:, j * P:(j + 1) * P], mod_rows[g][:, j * P:(j + 1) * P],
                                       ident[:, :])
                ins.then_inc(S["mod_turned"], 1)

            pe.wait_ge(S["ones_made"], 1)
            norm_sum(1, bank[4][:, 0:TOK])

            pe.wait_ge(S["cond_ready"], 1)
            for c in C_MOD[0]:
                mod_sum(c)
            pe.wait_ge(S["consts_made"], 1)
            mod_turn(0)

            def project(i):
                if i >= 2:
                    pe.wait_ge(S["proj_kept"], 4 * (i - 1))
                arrived(pe, C_PROJ[i])
                for b in range(4):
                    ins = product(C_PROJ[i], b, h, bank[2 * (i % 2) + b // 2][:, (b % 2) * TOK:(b % 2 + 1) * TOK],
                                  h_blocks=i + b == 0)
                ins.then_inc(S["chunk_used"], 1)
                for c in range(C_PROJ[i] + 1, C_PROJ[i + 1]):
                    mod_sum(c)

            pe.wait_ge(S["mod_made"], 4)
            project(0)
            pe.wait_ge(S["rpb_in"], 64)
            for q in range(2):
                ins = pe.matmul(bank[6 + q][:, :], mirror[:, :],
                                abias[:, 4 * q:4 * q + 4, :].rearrange("p a b -> p (a b)"), start=True, stop=True)
            ins.then_inc(S["bias_turned"], 1)
            project(1)
            pe.wait_ge(S["gatew_in"], 16)
            pe.wait_ge(S["bias_ready"], 2)
            for k in range(KD):
                for q in range(4):
                    ins = pe.matmul(bank[6][32 * q:32 * q + MH, 0:TOK], wgate[:, k, 4 * q:4 * q + 4], h[:, k, :],
                                    start=k == 0, stop=k == KD - 1)
            ins.then_inc(S["gates_summed"], 1)
            for i in range(2, EARLY):
                project(i)
            def late_project(t):
                c = C_PROJ[EARLY + t // 4]
                if t % 4 == 0:
                    arrived(pe, c)
                pe.wait_ge(S["proj_kept"], 4 * EARLY + t - 1 if t >= 2 else 4 * (EARLY - 1))
                ins = product(c, t % 4, h, late_bank(t))
                ins.then_inc(S["chunk_used"] if t % 4 == 3 else S["block_made"], 1)

            def scores(i):
                if i >= 2:
                    pe.wait_ge(S["exp_done"], 2 * (i - 1))
                o = HD * (i % 2)
                b = bank[4 + i % 2]
                q = z[o:o + HD, Z["qa"] + i // 2, :]
                k = z[o:o + HD, Z["ka"] + i // 2, :]
                pe.matmul(b[:, 0:L], q[:, 0:L], k[:, 0:L], start=True, stop=True)
                pe.matmul(b[:, L:2 * L], q[:, L:TOK], k[:, L:TOK], start=True, stop=True)
                pe.matmul(b[:, 2 * L:3 * L], q[:, L:TOK], kctx[o:o + HD, i // 2, :], start=True, stop=True
                          ).then_inc(S["scored"], 1)

            def turn_probs(i):
                pe.wait_ge(S["probs_ready"], i + 1)
                if i >= 2:
                    pe.wait_ge(S["pt_kept"], i - 1)
                for q in range(3):
                    ins = pe.transpose(bank[6 + i % 2][:, q * L:(q + 1) * L], att["p"][:, i % 2, q * L:(q + 1) * L],
                                       ident[:, :])
                ins.then_inc(S["probs_turned"], 1)

            def attend(i):
                pe.wait_ge(S["pt_kept"], i + 1)
                if i >= 4 and i % 2 == 0:
                    pe.wait_ge(S["att_kept"], i // 2 - 1)
                o = HD * (i % 2)
                to = bank[(i // 2) % 2][o:o + HD, :]
                pt = att["pt"][:, i % 2, :]
                cols = slice(i * HD, (i + 1) * HD)
                pe.matmul(to[:, 0:L], va_tok[:, 0, cols], pt[:, 0:L], start=True, stop=True)
                pe.matmul(to[:, L:TOK], va_tok[:, 1, cols], pt[:, L:2 * L], start=True, stop=False)
                pe.matmul(to[:, L:TOK], vctx[:, cols], pt[:, 2 * L:3 * L], start=False, stop=True
                          ).then_inc(S["attended"], 1)

            pe.wait_ge(S["kctx_in"], 16)
            pe.wait_ge(S["vctx_in"], 16)
            late_project(0)
            pe.wait_ge(S["proj_kept"], 4 * EARLY)
            pe.wait_ge(S["gates_kept"], 4)
            for s in range(2):
                for b in range(4):
                    ins = pe.transpose(bank[6 + s][:, b * P:(b + 1) * P], z[:, Z["va"] + b, s * L:(s + 1) * L],
                                       ident[:, :])
            ins.then_inc(S["va_turned"], 1)
            pe.wait_ge(S["mod_kept"], 3)
            scores(0)
            for i in range(NH):
                late_project(2 * i + 1)
                if i < NH - 1:
                    scores(i + 1)
                turn_probs(i)
                if i < NH - 1:
                    late_project(2 * i + 2)
                else:
                    pe.wait_ge(S["conv_step"], 4 * CONV_W)
                    pe.wait_ge(S["exp_done"], 2 * NH)
                    for b in range(4):
                        ins = pe.matmul(bank[4][:, 0:TOK], ones[:, :], acc[:, b, :], start=b == 0, stop=b == 3)
                    ins.then_inc(S["conv_sum"], 1)
                if i == 0:
                    pe.wait_ge(S["va_kept"], 2)
                attend(i)

            pe.wait_ge(S["pt_kept"], NH)
            pe.wait_ge(S["att_kept"], NH // 2)
            pe.wait_ge(S["proj_kept"], 4 * len(PROJ))
            for s in range(2):
                for b in range(4):
                    ins = pe.transpose(bank[2 + s][:, b * P:(b + 1) * P], z[:, Z["vm"] + b, s * L:(s + 1) * L],
                                       ident[:, :])
            ins.then_inc(S["v_turned"], 1)

            def gate_unit(u):
                c = C_MERGE + 3 * (u // 8) + (u % 8) // 4
                if u % 4 == 0:
                    arrived(pe, c)
                if u >= 2:
                    pe.wait_ge(S["gate_sig"] if u % 8 >= 2 else S["merge_read"], u - 1)
                ins = product(c, u % 4, h, unit_bank(u))
                ins.then_inc(S["chunk_used"] if u % 4 == 3 else S["gate_made"], 1)

            def merge_unit(u):
                c, b = C_MERGE + 3 * (u // 8) + 2, u % 8
                if b == 0:
                    arrived(pe, c)
                if b >= 2:
                    pe.wait_ge(S["merge_read"], u - 1)
                else:
                    pe.wait_ge(S["gate_sig"], u + 7)
                w = trunk_chunk(c, 4)
                for k in range(4):
                    ins = pe.matmul(unit_bank(u), w[:, k, b * P:(b + 1) * P],
                                    branch_out[BRANCHES[u // 8]][:, k, :], start=k == 0, stop=k == 3)
                ins.then_inc(S["chunk_used"] if b == 7 else S["merge_made"], 1)

            gate_unit(0)
            pe.wait_ge(S["km_scaled"], 1)
            for b in range(4):
                ins = pe.transpose(bank[7][:, b * P:(b + 1) * P], z[:, Z["km"] + b, 0:L], ident[:, :])
            ins.then_inc(S["v_turned"], 1)
            pe.wait_ge(S["rows_ready"], 1)
            pe.wait_ge(S["w_ready"], 2)
            turns = [rows["g"][:, d, s * L:(s + 1) * L] for d in range(2) for s in range(2)]
            turns += [rows["b"][:, d, s * L:(s + 1) * L] for d in range(2) for s in range(2)]
            turns += [rows["w"][:, d, :] for d in range(2)]
            for i, v in enumerate(turns):
                ins = pe.transpose(bank[6][:, MH * i:MH * i + MH], v, ident[0:MH, 0:MH])
            ins.then_inc(S["cols_turned"], 1)
            pe.wait_ge(S["v_kept"], 2)
            gate_unit(1)
            pe.wait_ge(S["conv_sq"], 1)
            for b in range(4):
                ins = pe.matmul(bank[4][:, TOK:2 * TOK], ones[:, :], conv_sq[:, b, :], start=b == 0, stop=b == 3)
            ins.then_inc(S["conv_sqsum"], 1)
            mod_turn(1)
            mod_turn(2)
            gate_unit(2)
            gate_unit(3)

            def ml_front(i):
                if i:
                    pe.wait_ge(S["decayed"], 4 * i)
                pe.matmul(bank[4][:, :], selrow[:, i, :], negm.rearrange("p d t -> p (d t)"),
                          start=True, stop=False)
                pe.matmul(bank[4][:, :], ident[:, :], dmask[:, :, :, :].rearrange("p d s t -> p (d s t)"),
                          start=False, stop=True).then_inc(S["spread"], 1)
                if i:
                    pe.wait_ge(S["ptm_ready"], i)
                q, k = z[:, Z["qm"] + i, :], z[:, Z["km"] + i, :]
                for s in range(2):
                    ins = pe.matmul(bank[5][:, s * L:(s + 1) * L], k[:, s * L:(s + 1) * L], q[:, s * L:(s + 1) * L],
                                    start=True, stop=True)
                ins.then_inc(S["keyed"], 1)
                if i:
                    pe.wait_ge(S["inter_kept"], 2 * i)
                for d in range(2):
                    ins = pe.matmul(bank[0][:, d * (P + 1):(d + 1) * (P + 1)], q[:, L:TOK], cinit[:, d, i, :],
                                    start=True, stop=True)
                ins.then_inc(S["inter_made"], 1)

            def ml_back(i):
                pe.wait_ge(S["ptm_ready"], i + 1)
                if i:
                    pe.wait_ge(S["ns_made"], 2 * i)
                for d in range(2):
                    for s in range(2):
                        ins = pe.matmul(bank[6 + d][:, s * (P + 1):(s + 1) * (P + 1)], ml["pt"][:, 2 * d + s, :],
                                        vmt[:, s, i, :], start=True, stop=True)
                ins.then_inc(S["summed"], 1)
                pe.wait_ge(S["kw_ready"], i + 1)
                if i:
                    pe.wait_ge(S["state_kept"], 2 * i)
                pe.matmul(bank[3][:, 0:2 * P], vmt[:, 0, i, 0:P], ml["kw"].rearrange("p d k -> p (d k)"),
                          start=True, stop=True)
                pe.matmul(bank[3][0:2, TOK:TOK + P], sm["wsrc"][:, i, :], kmt[:, i, :], start=True, stop=True
                          ).then_inc(S["state_made"], 1)

            pe.wait_ge(S["cinit_in"], 16)
            pe.wait_ge(S["pads_made"], 2)
            pe.wait_ge(S["conv_var"], 1)
            pe.wait_ge(S["cols_kept"], 1)
            pe.wait_ge(S["v_kept"], 3)
            pe.wait_ge(S["mod_made"], 12)
            for i in range(MH):
                ml_front(i)
                for u in GATES_AHEAD[i]:
                    gate_unit(u)
                for u in MERGES_AHEAD[i]:
                    merge_unit(u)
                ml_back(i)
                for u in GATES_AFTER[i]:
                    gate_unit(u)
                if i == 2:
                    pe.wait_ge(S["yc_ready"], 1)
                for u in MERGES_AFTER[i]:
                    merge_unit(u)
            for u in range(8, 14):
                gate_unit(u)
            pe.wait_ge(S["hm_ready"], 1)
            pe.wait_ge(S["decayed"], 4 * MH)
            for i in range(MH):
                for s in range(2):
                    at = (i % 2) * TOK + s * L
                    ins = pe.transpose(bank[4 + i // 2][:, at:at + L], hm[:, s, i, :], ident[:, :])
            ins.then_inc(S["hm_turned"], 1)
            pe.wait_ge(S["router_in"], 32)
            for s in range(2):
                for k in range(KD):
                    ins = pe.matmul(bank[6][0:1, s * NE:(s + 1) * NE], mod[:, 24 + k, s:s + 1], wrt[:, k, :],
                                    start=k == 0, stop=k == KD - 1)
            ins.then_inc(S["shift_summed"], 1)
            for u in range(14, 16):
                gate_unit(u)
            for u in range(8, 16):
                merge_unit(u)
            for u in range(16, 24):
                gate_unit(u)
            pe.wait_ge(S["ym_ready"], 1)
            for u in range(16, 24):
                merge_unit(u)
            pe.wait_ge(S["merge_read"], 24)
            pe.wait_ge(S["brs_ready"], 1)
            for c in range(2):
                arrived(pe, C_OUT + c)
                for b in range(4):
                    ins = product(C_OUT + c, b, merged, bank[4 + 2 * c + b // 2][:, (b % 2) * TOK:(b % 2 + 1) * TOK])
                    if b % 2:
                        ins.then_inc(S["out_made"] if b == 1 else S["chunk_used"], 1)

            norm_sum(2, bank[4][:, 0:TOK])
            pe.wait_ge(S["wrs_ready"], 2)
            for s in range(2):
                for k in range(KD):
                    q = k % 4
                    ins = pe.matmul(bank[5][NE * q:NE * (q + 1), s * L:(s + 1) * L], rt["wrs"][:, s * KD + k, :],
                                    x[:, k, s * L:(s + 1) * L], start=k < 4, stop=k >= 4)
            ins.then_inc(S["raw_logits"], 1)

            def clear(q):
                return pe.matmul(bank[q][:, :], selrow[0:1, 1, :], x[0:1, 0:2, :].rearrange("p a b -> p (a b)"),
                                 start=True, stop=False, skip_group_check=True)

            for q in range(4):
                clear(q)
            pe.wait_ge(S["lt_ready"], 1)
            for s in range(2):
                to = bank[7][:, s * NE:(s + 1) * NE]
                pe.matmul(to, rt["lt"][:, s * L:(s + 1) * L], stack[:, :], start=True, stop=False)
                ins = pe.matmul(to, ones[0:1, :], rt["brs"][:, s, :], start=False, stop=True)
            ins.then_inc(S["logits_made"], 1)

            def turn_h(half, s):
                for k in range(4 * half, 4 * half + 4):
                    if k < ACT_BLOCKS:
                        pe.wait_ge(S["h2_first"], k + 1)
                    else:
                        pe.wait_ge(S["h2_last"], k - ACT_BLOCKS + 1)
                    ins = pe.transpose(turn_h_bank(half, s)[:, (k % 4) * P:(k % 4 + 1) * P],
                                       h[:, k, s * L:(s + 1) * L], ident[:, :])
                ins.then_inc(S["h2_turned"], 1)

            turn_h(0, 0)
            turn_h(0, 1)
            pe.wait_ge(S["picked_made"], 2)
            pe.matmul(bank[7][:, 64:64 + NE], strict[:, :], rt["picked"][:, 0, :], start=True, stop=True)
            pe.matmul(bank[7][:, 64 + NE:64 + 2 * NE], ones[:, :], rt["picked"][:, 0, :], start=True, stop=False)
            pe.matmul(bank[7][:, 64 + NE:64 + 2 * NE], strict[:, :], rt["picked"][:, 1, :], start=False, stop=True)
            for s in range(2):
                ins = pe.matmul(bank[7][0:NE, 128:129], rt["picked"][:, s, :], ones[:, 0:1], start=s == 0, stop=s == 1)
            ins.then_inc(S["ranked"], 1)
            turn_h(1, 0)
            pe.wait_ge(S["h2_kept"], 1)
            turn_h(1, 1)

            def gather(n):
                pe.wait_ge(S["sel_ready"], n * 2 + 2)
                for s in range(2):
                    for f in range(2):
                        ins = pe.matmul(bank[4][f * SLOTS:(f + 1) * SLOTS, :], mo["sel"][:, s, :],
                                        mo["h_tok"][:, s, f * 512:(f + 1) * 512], start=s == 0, stop=s == 1)
                ins.then_inc(S["gathered"], 1)

            def turn4(to, src, name):
                for j in range(4):
                    ins = pe.transpose(bank[to][:, j * P:(j + 1) * P], src[:, j * P:(j + 1) * P], ident[:, :])
                ins.then_inc(S[name], 1)

            def scatter(q):
                return pe.matmul(bank[q][:, :], mo["selt"][:, q // 2, q % 2, :], mo["y"], start=False, stop=False,
                                 skip_group_check=True)

            def weights(slot, row, width, at):
                at += slot * CHUNK + row * width
                return expert_ring[:, at:at + 512]

            def up_bias(n):
                pe.wait_ge(S["esel_ready"], n + 1)
                pe.wait_ge(S["selt_kept"], n + 1)
                for f in range(2):
                    for u in range(2):
                        pe.matmul(bank[5 + u][f * SLOTS:(f + 1) * SLOTS, :], mo["esel"],
                                  bgu[:, u * D + f * 512:u * D + (f + 1) * 512], start=True, stop=False,
                                  skip_group_check=True)

            pe.wait_ge(S["np_made"], 1)
            pe.matmul(bank[7][0:NE, 129:130], strict[0:NE, 0:NE], rt["np"], start=True, stop=True
                      ).then_inc(S["before_made"], 1)
            pe.wait_ge(S["h2_kept"], 4)
            gather(0)
            pe.wait_ge(S["past_made"], 1)
            M1 = MAX_PASS + 1
            row = bank[7][0:1, 192:192 + N_TAB]
            pe.matmul(row[:, T_EXP:T_EXP + M1], ones[0:NE, 0:1], rt["past"], start=True, stop=True)
            pe.matmul(row[:, T_BASE:T_BASE + M1], rt["np"], rt["past"], start=True, stop=True)
            pe.matmul(row[:, T_BEFORE:T_BEFORE + NE], rt["np"], strict[0:NE, 0:NE], start=True, stop=True)
            pe.matmul(row[:, T_ALL:T_ALL + 1], rt["np"], ones[0:NE, 0:1], start=True, stop=True
                      ).then_inc(S["tab_summed"], 1)
            pe.wait_ge(S["gath_kept"], 1)
            turn4(4, mo["gath"], "xg_turned")
            pe.wait_ge(S["bgu_in"], 16)
            pe.wait_ge(S["bdn_in"], 16)
            up_bias(0)
            pe.wait_ge(S["table_made"], 1)
            n_pass = table(pe, T_ALL, NE, MAX_PASS)

            def expert_pass(n, turn, e):
                pe.wait_ge(S["xg_ready"], n + 1)
                for j in range(GU_CHUNKS):
                    pe.wait_ge(expert_in[e % 2][j], turn * (8 * TURN) + 16 * (e // 2 + 1))
                    for i in range(2):
                        k = 2 * j + i
                        for u in range(2):
                            for f in range(2):
                                at = u * D + f * 512
                                ins = pe.matmul(bank[5 + u][f * SLOTS:(f + 1) * SLOTS, :],
                                                mo["xg"][:, k % 4, k // 4, :], weights(expert_slot(e, j), i, 2 * D, at),
                                                start=False, stop=k == KD - 1, skip_group_check=True)
                    ins.then_inc(S["chunk_used"], 1)
                    if j == 0:
                        pe.wait_ge(S["y_kept"], n + 1)
                        for f in range(2):
                            ins = pe.matmul(bank[7][f * SLOTS:(f + 1) * SLOTS, :], mo["esel"],
                                            bdn[:, f * 512:(f + 1) * 512], start=True, stop=False)
                        ins.then_inc(S["biased"], 1)
                        scatter(0)
                    if j == 1:
                        scatter(1)
                        scatter(2)
                    if j == 2:
                        gather(n + 1)
                scatter(3)
                pe.wait_ge(S["gath_kept"], n + 2)
                turn4(4, mo["gath"], "xg_turned")
                pe.wait_ge(S["act_ready"], n + 1)
                turn4(5, mo["act"], "act_turned")
                pe.wait_ge(S["selg_ready"], n * 2 + 2)
                for s in range(2):
                    for f in range(2):
                        at = (1 - f) * SLOTS
                        q = 2 * s + f
                        ins = pe.transpose(bank[6][:, q * P:(q + 1) * P], mo["selz"][:, s, at:at + P], ident[:, :])
                ins.then_inc(S["selt_turned"], 1)
                pe.wait_ge(S["actt_kept"], n + 1)
                for j in range(DN_CHUNKS):
                    pe.wait_ge(expert_in[e % 2][GU_CHUNKS + j], turn * (8 * TURN) + 16 * (e // 2 + 1))
                    for i in range(4):
                        for f in range(2):
                            ins = pe.matmul(bank[7][f * SLOTS:(f + 1) * SLOTS, :], mo["actt"][:, i, j, :],
                                            weights(expert_slot(e, GU_CHUNKS + j), i, D, f * 512),
                                            start=False, stop=j + i == 4)
                    ins.then_inc(S["chunk_used"], 1)
                up_bias(n + 1)

            with pe.Fori(0, NE // TURN) as turn:
                for e in range(TURN):
                    first = table(pe, turn * TURN + (T_BEFORE + e), 0, MAX_PASS)
                    last = table(pe, turn * TURN + (T_BEFORE + e + 1), 1, MAX_PASS)
                    with pe.Fori(first, last) as n:
                        expert_pass(n, turn, e)

            pe.wait_ge(S["y_kept"], n_pass + 1)
            pe.wait_ge(S["selt_kept"], n_pass + 1)
            for q in (0, 2, 1, 3):
                scatter(q).then_inc(S["scattered"], 1)

            for k in range(KD):
                if k % 4 == 0:
                    pe.wait_ge(S["acc_kept"], k // 4 + 1)
                    pe.wait_ge(S["acc_copied"], k // 4 + 1)
                for s in range(2):
                    at = (k % 2) * TOK + s * L
                    ins = pe.transpose(bank[4 + k // 2][:, at:at + L], mo["h_tok"][:, s, k * P:(k + 1) * P],
                                       ident[:, :])
                if k % 2:
                    ins.then_inc(S["acc_turned"], 1)
            norm_sum(3, bank[0][:, 0:TOK])


def _blocks(v):
    return v.reshape(-1, P).T


def _chunks(w, width=512):
    k, n = w.shape
    return w.reshape(k // P, P, n // width, width).transpose(2, 1, 0, 3).reshape(n // width, P, -1)


def pack(a):
    dA, dC, dM = NH * HD, 4 * P, MH * P
    sizes = [("qa", dA), ("ka", dA), ("va", dA), ("cu", dC), ("cg", dC), ("qm", dM), ("km", dM), ("vm", dM),
             ("om", dM), ("gate", 16), ("ga", D), ("gc", D), ("gm", D)]
    w_in, b_in = a["w_in"][0], a["b_in"][0]
    w, b, at = {}, {}, 0
    for name, n in sizes:
        w[name], b[name] = w_in[:, at:at + n], b_in[at:at + n]
        at += n
    mod = a["w_mod"][0].reshape(MOD_CHUNKS, 2, P, MOD_GROUPS, 2048).transpose(3, 0, 2, 1, 4)
    mod = mod.reshape(MOD_GROUPS, MOD_CHUNKS, P, CHUNK)
    mods = iter(mod[1:].reshape(-1, P, CHUNK))
    trunk = [mod[0]]
    for i, name in enumerate(PROJ):
        trunk.append(_chunks(w[name]))
        trunk += [next(mods)[None] for _ in range(MODS_AFTER[i] if i < EARLY else 0)]
    for br in BRANCHES:
        trunk += [_chunks(w["g" + br]), _chunks(a["w_p" + br][0], D)]
    trunk.append(_chunks(a["w_out"][0]))
    params = {
        "norm1": _blocks(a["norm1_g"][0]), "norm2": _blocks(a["norm2_g"][0]), "final": _blocks(a["final_g"]),
        "b_mod": _blocks(a["b_mod"][0]),
        "b_in": np.concatenate([_blocks(b[n]) for n in PROJ + ["g" + br for br in BRANCHES]], axis=1),
        "w_dw": a["w_dw"][0].T.reshape(4, P, CONV_W).transpose(1, 0, 2).reshape(P, -1),
        "b_dw": _blocks(a["b_dw"][0]), "cln_g": _blocks(a["cln_g"][0]), "cln_b": _blocks(a["cln_b"][0]),
        "mnorm": _blocks(a["mnorm_g"][0]),
        "cond": np.stack([_blocks(a["c_ctx"]), _blocks(a["c"][0])], axis=2).reshape(P, -1),
    }
    x_all = np.concatenate([a["x_prompt"][0], a["x_sample"][0]], axis=0)
    c_init = np.concatenate([a["state_C"][0, 0].transpose(3, 0, 1, 2),
                             a["state_n"][0, 0].transpose(2, 0, 1)[..., None]], axis=3)
    packed = {
        "trunk_w": np.concatenate(trunk, axis=0),
        "w_gu": a["w_gu"][0],
        "w_down": a["w_down"][0],
        "x_t": x_all.T.reshape(KD, P, TOK).transpose(1, 0, 2),
        "params": np.concatenate([params[n] for n, _ in PAR_WIDTHS], axis=1),
        "w_gate": w["gate"].reshape(KD, P, 16).transpose(1, 0, 2),
        "b_gate": b["gate"].reshape(4, MH).T,
        "m_init": a["state_m"][0, 0].T,
        "k_ctx_t": a["cache_k"][0, 0].reshape(L, 4, P).transpose(2, 1, 0),
        "v_ctx": a["cache_v"][0, 0].reshape(L, NH * HD),
        "c_init_t": c_init,
        "rpb": a["rpb"][0],
        "w_router": a["w_router"][0].reshape(KD, P, NE).transpose(1, 0, 2),
        "b_router": a["b_router"],
        "b_gu": a["b_gu"][0],
        "b_down": a["b_down"][0],
    }
    return {n: np.ascontiguousarray(v) for n, v in packed.items()}


_OUTS = {"y_t": (P, KD, TOK), "k_new_t": (P, 4, L), "v_new_t": (P, 4, L), "c_new": (P, MH, 2, P),
         "n_new": (2, MH * P), "m_new": (MH, 2)}


def kernel(**inputs):
    import concourse.bacc as _bacc
    from concourse.bass_utils import run_bass_kernel_spmd as _run

    arrays = pack({n: np.asarray(v) for n, v in inputs.items()})
    nc = _bacc.Bacc("TRN2", target_bir_lowering=False, num_devices=1)
    feeds, args = {}, []
    for name, v in arrays.items():
        feeds[f"in_{name}"] = v
        args.append(nc.dram_tensor(f"in_{name}", v.shape, F32, kind="ExternalInput").ap())
    for name, shape in _OUTS.items():
        args.append(nc.dram_tensor(f"out_{name}", shape, F32, kind="ExternalOutput").ap())
    hybrid_layer(nc, *args)
    r = _run(nc, [feeds], core_ids=[0]).results[0]
    got = {n: r[f"out_{n}"] for n in _OUTS}
    y = got["y_t"].transpose(1, 0, 2).reshape(D, TOK).T
    kv = [got[n].transpose(2, 1, 0).reshape(1, 1, L, NH, HD) for n in ("k_new_t", "v_new_t")]
    return (y[None, 0:L], y[None, L:TOK], kv[0], kv[1],
            got["c_new"].transpose(2, 1, 0, 3)[None, None],
            got["n_new"].reshape(1, 1, 2, MH, P), got["m_new"].T[None, None])
```
